# Optimizing a Trainium2 kernel written in Bass

```python
import math
import jax, jax.numpy as jnp
from jax import lax
import numpy as np

D_MODEL = 1024
BATCH = 1
SEQ = 256
DEPTH = 2

GRID_W = 64
CTX_LEN = 256

DA_HEADS = 4
DA_QK_DIM = 64
DA_V_DIM = 2 * DA_QK_DIM
ML_HEADS = 4
ML_DIM = 128
ML_CHUNK = 128
ML_CONV = 3
FN_GROUPS = 4
FN_GROUP_DIM = D_MODEL // FN_GROUPS
N_EXPERTS = 16
N_EXPERT_GROUPS = 4
EXPERTS_PER_GROUP = N_EXPERTS // N_EXPERT_GROUPS
TOP_K = 2
D_EXPERT = 512
ROPE_BASE = 10000.0
Q_BLOCK = 128
NORM_EPS = 1e-6
N_EVEN = (DEPTH + 1) // 2
N_ODD = DEPTH // 2

DA_QK_W = DA_HEADS * 2 * DA_QK_DIM
DA_V_W = DA_HEADS * DA_V_DIM
ML_W = ML_HEADS * ML_DIM
ML_GATE_W = 4 * ML_HEADS
IN_SPLITS = [DA_QK_W, 2 * DA_QK_W, 2 * DA_QK_W + DA_V_W, 2 * DA_QK_W + DA_V_W + 2 * ML_W,
             2 * DA_QK_W + DA_V_W + 3 * ML_W, 2 * DA_QK_W + DA_V_W + 4 * ML_W]
IN_COLS = 2 * DA_QK_W + DA_V_W + 4 * ML_W + ML_GATE_W
MIX_W = DA_V_W + ML_W

kernel_name = "hybrid_diffattn_mlstm_fnet_groupmoe_prefix"

def rmsnorm(x, g):
    xf = x.astype(jnp.float32)
    y = xf * lax.rsqrt(jnp.mean(xf * xf, axis=-1, keepdims=True) + NORM_EPS)
    return (y * g.astype(jnp.float32)).astype(x.dtype)

def modulate(h, shift, scale):
    return h * (1 + scale) + shift

def tokens_to_heads(a, n_heads):
    b, t, w = a.shape
    return a.reshape(b, t, n_heads, w // n_heads).transpose(0, 2, 1, 3)

def heads_to_tokens(a):
    b, h, t, d = a.shape
    return a.transpose(0, 2, 1, 3).reshape(b, t, h * d)

def axial_rope_tables(row, col):
    n_pairs_axis = DA_QK_DIM // 4
    inv = ROPE_BASE ** (-jnp.arange(n_pairs_axis, dtype=jnp.float32) / n_pairs_axis)
    ang = jnp.concatenate([row.astype(jnp.float32)[:, None] * inv,
                           col.astype(jnp.float32)[:, None] * inv], axis=-1)
    return jnp.cos(ang), jnp.sin(ang)

def apply_rope(x, cos, sin):
    xp = x.reshape(*x.shape[:-1], -1, 2)
    x0, x1 = xp[..., 0], xp[..., 1]
    cs, sn = cos.astype(x.dtype), sin.astype(x.dtype)
    return jnp.stack([x0 * cs - x1 * sn, x0 * sn + x1 * cs], axis=-1).reshape(x.shape)

def centred_dwconv(x, w):
    k = w.shape[0]
    p = k // 2
    t = x.shape[1]
    xp = jnp.pad(x, ((0, 0), (p, p), (0, 0)))
    out = xp[:, 0:t] * w[0]
    for j in range(1, k):
        out = out + xp[:, j:j + t] * w[j]
    return out

def split_projection(u, conv_w, gate_b):
    b, t, _ = u.shape
    da_q, da_k, da_v, ml_qk, ml_v, ml_o, gates = jnp.split(u, IN_SPLITS, axis=-1)
    dq = da_q.reshape(b, t, DA_HEADS, 2, DA_QK_DIM).transpose(3, 0, 2, 1, 4)
    dk = da_k.reshape(b, t, DA_HEADS, 2, DA_QK_DIM).transpose(3, 0, 2, 1, 4)
    dv = tokens_to_heads(da_v, DA_HEADS)
    qk = jax.nn.silu(centred_dwconv(ml_qk, conv_w))
    mq, mk = jnp.split(qk, 2, axis=-1)
    mq = tokens_to_heads(mq, ML_HEADS)
    mk = tokens_to_heads(mk, ML_HEADS) * (ML_DIM ** -0.5)
    mv = tokens_to_heads(ml_v, ML_HEADS)
    og = jax.nn.sigmoid(ml_o)
    g = (gates.astype(jnp.float32).reshape(b, t, 4, ML_HEADS)
         + gate_b.astype(jnp.float32)).transpose(2, 0, 3, 1)
    g = jnp.stack([g[0], jax.nn.log_sigmoid(g[1]), g[2], jax.nn.log_sigmoid(g[3])])
    return dq, dk, dv, mq, mk, mv, og, g

def diff_attn_block(q, k, v, lam):
    s = jnp.einsum("mbhqd,mbhkd->mbhqk", q, k).astype(jnp.float32) * (DA_QK_DIM ** -0.5)
    p = jax.nn.softmax(s, axis=-1)
    w = p[0] - lam * p[1]
    return jnp.einsum("bhqk,bhkd->bhqd", w.astype(v.dtype), v)

def diff_attention(q_c, k_c, v_c, q_l, k_l, v_l, lam, subln_g, lam_init, need_ctx):
    k_all = jnp.concatenate([k_c, k_l], axis=3)
    v_all = jnp.concatenate([v_c, v_l], axis=2)
    _, b, h, s, dq = q_l.shape
    nb = s // Q_BLOCK
    q_blocks = jnp.moveaxis(q_l.reshape(2, b, h, nb, Q_BLOCK, dq), 3, 0)
    o_blocks = lax.map(lambda qb: diff_attn_block(qb, k_all, v_all, lam), q_blocks)
    o_l = jnp.moveaxis(o_blocks, 0, 2).reshape(b, h, s, DA_V_DIM)
    o_l = rmsnorm(o_l, subln_g) * (1.0 - lam_init)
    o_c = None
    if need_ctx:
        o_c = rmsnorm(diff_attn_block(q_c, k_c, v_c, lam), subln_g) * (1.0 - lam_init)
    return o_c, o_l

def mlstm_chunkwise(q, k, v, log_i, log_f, state, with_output):
    b, h, t, d = q.shape
    nc = t // ML_CHUNK
    lc = ML_CHUNK

    def to_chunks(a):
        a = a.astype(jnp.float32)
        return jnp.moveaxis(a.reshape(b, h, nc, lc, *a.shape[3:]), 2, 0)

    xs = (to_chunks(q), to_chunks(k), to_chunks(v), to_chunks(log_i), to_chunks(log_f))
    causal = jnp.tril(jnp.ones((lc, lc), dtype=bool))

    def step(carry, inp):
        c_st, n_st, m_st = carry
        qc, kc, vc, lic, lfc = inp
        bcum = jnp.cumsum(lfc, axis=-1)
        b_last = bcum[..., -1]
        logw = b_last[..., None] - bcum + lic
        m_new = jnp.maximum(b_last + m_st, jnp.max(logw, axis=-1))
        wgt = jnp.exp(logw - m_new[..., None])
        decay = jnp.exp(b_last + m_st - m_new)
        c_new = decay[..., None, None] * c_st + jnp.einsum("bhl,bhlv,bhlk->bhvk", wgt, vc, kc)
        n_new = decay[..., None] * n_st + jnp.einsum("bhl,bhlk->bhk", wgt, kc)
        if not with_output:
            return (c_new, n_new, m_new), None
        log_d = bcum[..., :, None] - bcum[..., None, :] + lic[..., None, :]
        log_d = jnp.where(causal, log_d, -jnp.inf)
        m_inter = bcum + m_st[..., None]
        m_t = jnp.maximum(m_inter, jnp.max(log_d, axis=-1))
        dmat = jnp.exp(log_d - m_t[..., None])
        inter = jnp.exp(m_inter - m_t)
        sc = jnp.einsum("bhqd,bhkd->bhqk", qc, kc) * dmat
        num = (inter[..., None] * jnp.einsum("bhvk,bhqk->bhqv", c_st, qc)
               + jnp.einsum("bhqk,bhkv->bhqv", sc, vc))
        nq = inter * jnp.einsum("bhk,bhqk->bhq", n_st, qc) + jnp.sum(sc, axis=-1)
        den = jnp.maximum(jnp.abs(nq), jnp.exp(-m_t))
        return (c_new, n_new, m_new), num / den[..., None]

    final, hs = lax.scan(step, state, xs)
    if not with_output:
        return final, None
    out = jnp.moveaxis(hs, 0, 2).reshape(b, h, t, d).astype(q.dtype)
    return final, out

def mlstm_bidir(ctx_in, lat_in, need_ctx):
    q_c, k_c, v_c, g_c = ctx_in
    q_l, k_l, v_l, g_l = lat_in
    b, h, _, d = q_c.shape
    init = (jnp.zeros((b, h, d, d), jnp.float32), jnp.zeros((b, h, d), jnp.float32),
            jnp.zeros((b, h), jnp.float32))
    fl = lambda a: jnp.flip(a, axis=2)
    st_fc, h_fc = mlstm_chunkwise(q_c, k_c, v_c, g_c[0], g_c[1], init, need_ctx)
    _, h_fl = mlstm_chunkwise(q_l, k_l, v_l, g_l[0], g_l[1], st_fc, True)
    st_bc, h_bc = mlstm_chunkwise(fl(q_c), fl(k_c), fl(v_c), fl(g_c[2]), fl(g_c[3]), init, need_ctx)
    _, h_bl = mlstm_chunkwise(fl(q_l), fl(k_l), fl(v_l), fl(g_l[2]), fl(g_l[3]), st_bc, True)
    h_l = h_fl + fl(h_bl)
    h_c = h_fc + fl(h_bc) if need_ctx else None
    return h_c, h_l

def merge_groups(a, m, og):
    return jnp.concatenate([heads_to_tokens(a), heads_to_tokens(m) * og], axis=-1)

def even_mixer(h_c, h_l, w_in, w_out, conv_w, gate_b, lam_vec, subln_g, lam_init, cos, sin, need_ctx):
    dq_c, dk_c, dv_c, mq_c, mk_c, mv_c, og_c, g_c = split_projection(h_c @ w_in, conv_w, gate_b)
    dq_l, dk_l, dv_l, mq_l, mk_l, mv_l, og_l, g_l = split_projection(h_l @ w_in, conv_w, gate_b)
    dq_l = apply_rope(dq_l, cos, sin)
    dk_l = apply_rope(dk_l, cos, sin)
    lv = lam_vec.astype(jnp.float32)
    lam = jnp.exp(jnp.sum(lv[0] * lv[1])) - jnp.exp(jnp.sum(lv[2] * lv[3])) + lam_init
    a_c, a_l = diff_attention(dq_c, dk_c, dv_c, dq_l, dk_l, dv_l, lam, subln_g, lam_init, need_ctx)
    m_c, m_l = mlstm_bidir((mq_c, mk_c, mv_c, g_c), (mq_l, mk_l, mv_l, g_l), need_ctx)
    out_l = merge_groups(a_l, m_l, og_l) @ w_out
    out_c = merge_groups(a_c, m_c, og_c) @ w_out if need_ctx else None
    return out_c, out_l

def fourier_mix(h, w_fnet):
    b, t, d = h.shape
    hg = h.astype(jnp.float32).reshape(b, t, FN_GROUPS, FN_GROUP_DIM)
    f = jnp.fft.fft2(hg, axes=(1, 3), norm="ortho").real
    return f.reshape(b, t, d).astype(h.dtype) @ w_fnet

def grouped_moe(h, router_w, router_b, w_gate, w_up, w_down):
    aff = jax.nn.sigmoid((h @ router_w).astype(jnp.float32))
    biased = aff + router_b.astype(jnp.float32)
    grp = biased.reshape(*biased.shape[:-1], N_EXPERT_GROUPS, EXPERTS_PER_GROUP)
    grp_score = jnp.sum(lax.top_k(grp, TOP_K)[0], axis=-1)
    sel_group = jnp.argmax(grp_score, axis=-1)
    in_group = (jnp.arange(N_EXPERTS) // EXPERTS_PER_GROUP) == sel_group[..., None]
    _, idx = lax.top_k(jnp.where(in_group, biased, -jnp.inf), TOP_K)
    sel_aff = jnp.take_along_axis(aff, idx, axis=-1)
    wts = sel_aff / jnp.sum(sel_aff, axis=-1, keepdims=True)
    combine = jnp.sum(jax.nn.one_hot(idx, N_EXPERTS, dtype=jnp.float32) * wts[..., None], axis=-2)
    combine = combine.astype(h.dtype)
    y = jnp.zeros_like(h)
    for e in range(N_EXPERTS):
        he = jax.nn.silu(h @ w_gate[e]) * (h @ w_up[e])
        y = y + combine[..., e:e + 1] * (he @ w_down[e])
    return y

def setup_inputs(seed: int = 0) -> dict:
    key = jax.random.key(seed)
    ks = jax.random.split(key, 21)
    nrm = lambda k, shape, s: jax.random.normal(k, shape, jnp.float32) * s
    d = D_MODEL
    gate_base = jnp.array([0.0, 3.0, 0.0, 3.0], jnp.float32)[None, :, None]
    return {
        "x": nrm(ks[0], (BATCH, SEQ, d), 1.0),
        "c": nrm(ks[1], (BATCH, d), 1.0),
        "ctx": nrm(ks[2], (BATCH, CTX_LEN, d), 1.0),
        "c_ctx": nrm(ks[3], (d,), 1.0),
        "ada_w": nrm(ks[4], (DEPTH, d, 6 * d), 0.5 * d ** -0.5),
        "ada_b": nrm(ks[5], (DEPTH, 6 * d), 0.02),
        "norm_mix_g": 1.0 + nrm(ks[6], (DEPTH, d), 0.02),
        "norm_ffn_g": 1.0 + nrm(ks[7], (DEPTH, d), 0.02),
        "even_w_in": nrm(ks[8], (N_EVEN, d, IN_COLS), d ** -0.5),
        "even_w_out": nrm(ks[9], (N_EVEN, MIX_W, d), MIX_W ** -0.5),
        "even_conv_w": nrm(ks[10], (N_EVEN, ML_CONV, 2 * ML_W), ML_CONV ** -0.5),
        "even_gate_b": gate_base + nrm(ks[11], (N_EVEN, 4, ML_HEADS), 0.1),
        "even_lam": nrm(ks[12], (N_EVEN, 4, DA_QK_DIM), 0.1),
        "even_subln_g": 1.0 + nrm(ks[13], (N_EVEN, DA_V_DIM), 0.02),
        "odd_w_fnet": nrm(ks[14], (N_ODD, d, d), d ** -0.5),
        "router_w": nrm(ks[15], (d, N_EXPERTS), d ** -0.5),
        "router_b": nrm(ks[16], (N_EXPERTS,), 0.01),
        "exp_w_gate": nrm(ks[17], (DEPTH, N_EXPERTS, d, D_EXPERT), d ** -0.5),
        "exp_w_up": nrm(ks[18], (DEPTH, N_EXPERTS, d, D_EXPERT), d ** -0.5),
        "exp_w_down": nrm(ks[19], (DEPTH, N_EXPERTS, D_EXPERT, d), D_EXPERT ** -0.5),
        "final_g": 1.0 + nrm(ks[20], (d,), 0.02),
    }

def reference(x, c, ctx, c_ctx, ada_w, ada_b, norm_mix_g, norm_ffn_g, even_w_in, even_w_out,
              even_conv_w, even_gate_b, even_lam, even_subln_g, odd_w_fnet, router_w, router_b,
              exp_w_gate, exp_w_up, exp_w_down, final_g):
    n_lat = x.shape[1]
    rows = n_lat // GRID_W
    row = jnp.repeat(jnp.arange(rows, dtype=jnp.int32), GRID_W)
    col = jnp.tile(jnp.arange(GRID_W, dtype=jnp.int32), rows)
    cos, sin = axial_rope_tables(row, col)
    s_c = jax.nn.silu(c)
    s_cc = jax.nn.silu(c_ctx)
    x_l, x_c = x, ctx
    for i in range(DEPTH):
        last = i == DEPTH - 1
        even = i % 2 == 0
        ctx_out = not last
        ctx_in = ctx_out or even
        j = i // 2
        mod_l = jnp.split((s_c @ ada_w[i] + ada_b[i])[:, None, :], 6, axis=-1)
        h_l = modulate(rmsnorm(x_l, norm_mix_g[i]), mod_l[0], mod_l[1])
        h_c = None
        mod_c = None
        if ctx_in:
            mod_c = jnp.split(s_cc @ ada_w[i] + ada_b[i], 6, axis=-1)
            h_c = modulate(rmsnorm(x_c, norm_mix_g[i]), mod_c[0], mod_c[1])
        if even:
            lam_init = 0.8 - 0.6 * math.exp(-0.3 * i)
            o_c, o_l = even_mixer(h_c, h_l, even_w_in[j], even_w_out[j], even_conv_w[j],
                                  even_gate_b[j], even_lam[j], even_subln_g[j], lam_init,
                                  cos, sin, ctx_out)
        else:
            o_l = fourier_mix(h_l, odd_w_fnet[j])
            o_c = fourier_mix(h_c, odd_w_fnet[j]) if ctx_out else None
        x_l = x_l + mod_l[2] * o_l
        f_l = modulate(rmsnorm(x_l, norm_ffn_g[i]), mod_l[3], mod_l[4])
        if ctx_out:
            x_c = x_c + mod_c[2] * o_c
            f_c = modulate(rmsnorm(x_c, norm_ffn_g[i]), mod_c[3], mod_c[4])
            n_ctx = x_c.shape[1]
            y = grouped_moe(jnp.concatenate([f_c, f_l], axis=1), router_w, router_b,
                            exp_w_gate[i], exp_w_up[i], exp_w_down[i])
            x_c = x_c + mod_c[5] * y[:, :n_ctx]
            y_l = y[:, n_ctx:]
        else:
            y_l = grouped_moe(f_l, router_w, router_b, exp_w_gate[i], exp_w_up[i], exp_w_down[i])
        x_l = x_l + mod_l[5] * y_l
    return rmsnorm(x_l, final_g)


_drawn_inputs = setup_inputs


def setup_inputs(seed=0):
    import zlib

    import numpy as np

    out = dict(_drawn_inputs(seed))
    spreads = {}
    factors = {'even_subln_g': 13.002, 'final_g': 8.773, 'norm_ffn_g': 2.835}
    for name, (base, spread) in spreads.items():
        noise = np.random.default_rng([zlib.crc32(name.encode()), seed]).standard_normal(out[name].shape)
        drawn = base * np.exp(spread * noise) if base else spread * noise
        out[name] = __import__('jax').numpy.asarray(drawn.astype(out[name].dtype))
    for name, factor in factors.items():
        out[name] = (out[name] * factor).astype(out[name].dtype)
    return out
```

```python
from contextlib import ExitStack
import math

import concourse.bass as bass
from concourse import mybir

F32 = mybir.dt.float32
I32 = mybir.dt.int32
ALU = mybir.AluOpType
ACT = mybir.ActivationFunctionType
AX = mybir.AxisListType.X

P = 128
D = 1024
KD = D // P
SEQ = 256
TT = SEQ // P
TOK = 2 * SEQ
NT = TOK // P
HEADS = 4
QK = 64
HD = 128
W = 512
FE = 512
KF = FE // P
NE = 16
NG = 4
EG = NE // NG
GP = 2
EP = GP * EG
TURNS = NG // GP
RING = 6
EPS = 1e-6
LAM_INIT = 0.8 - 0.6 * math.exp(0.0)
BIG = 1e30

C_Q, C_K, C_V, C_MQ, C_MK, C_MV, C_O, C_G = 0, 512, 1024, 1536, 2048, 2560, 3072, 3584

CONSTS = {}
_at = 0
for _name, _n in (("ident", P), ("dft", TT * 2 * SEQ), ("cos", SEQ), ("sin", SEQ), ("le", P), ("ge", P),
                  ("lt", P), ("gt", P), ("mask", 3 * P), ("iota", P), ("ones", P), ("first4", NG),
                  ("first16", NE)):
    CONSTS[_name] = (_at, _at + _n)
    _at += _n
N_CONSTS = _at


def constants():
    import numpy as np

    t = np.zeros((P, N_CONSTS), np.float32)

    def put(name, a):
        t[:, CONSTS[name][0]:CONSTS[name][1]] = a

    r, c = np.arange(P)[:, None], np.arange(P)[None, :]
    put("ident", r == c)
    n = np.arange(SEQ)
    ang = 2 * np.pi * ((n[:, None] * n[None, :]) % SEQ) / SEQ
    cs = np.concatenate([np.cos(ang), np.sin(ang)], 1) / math.sqrt(SEQ)
    put("dft", cs.reshape(TT, P, 2 * SEQ).transpose(1, 0, 2).reshape(P, -1))
    pairs = QK // 4
    inv = 10000.0 ** (-np.arange(pairs, dtype=np.float32) / pairs)
    pair, tok = np.arange(P)[:, None] % (2 * pairs), np.arange(SEQ)[None, :]
    pos = np.where(pair < pairs, tok // 64, tok % 64).astype(np.float32)
    rot = pos * inv[pair % pairs].astype(np.float32)
    put("cos", np.cos(rot))
    put("sin", np.sin(rot))
    put("le", r <= c)
    put("ge", r >= c)
    put("lt", r < c)
    put("gt", r > c)
    put("mask", np.concatenate([np.where(c > r, -BIG, 0), np.full((P, P), -BIG), np.where(c < r, -BIG, 0)], 1))
    put("iota", np.broadcast_to(c, (P, P)))
    put("ones", 1.0)
    put("first4", np.broadcast_to(NG - np.arange(NG), (P, NG)))
    put("first16", np.broadcast_to(NE - np.arange(NE), (P, NE)))
    return t


STREAM = ([("ada", c) for c in range(4)] + [("in", C_K), ("in", C_V), ("ada", 4), ("ada", 5), ("in", C_Q),
          ("ada", 6), ("ada", 7), ("ada", 8), ("ada", 9), ("ada", 10), ("ada", 11), ("in", C_MK), ("in", C_MQ),
          ("in", C_MV), ("in", C_O), ("out", 0), ("out", 1)])


def expert_stream(with_ada):
    s = []
    for i in range(EP):
        if i and i % EG == 0:
            s.append(("down", i - 1))
        s += [("gate", i), ("up", i)]
        if i % EG:
            s.append(("down", i - 1))
        if with_ada and i < 6:
            s.append(("ada", i))
    return s + [("down", EP - 1)]


ITEMS = ([("k", a) for a in range(4)] + [("v", a) for a in range(4)] + [("q", a) for a in range(2)]
         + [("mk", a) for a in range(4)] + [("mq", a) for a in range(2)] + [("mv", a) for a in range(4)]
         + [("o", a) for a in range(2)] + [("g", 0)])
LAST_OF = [("k", 3), ("v", 3), ("q", 1), ("mk", 3), ("mq", 1), ("mv", 3), ("o", 1)]
ADA_AFTER = {4: 4, 5: 5, 6: 6, 7: 7, 8: 8, 9: 9, 10: 10, 12: 11}
EV_A, EV_D, EV_C = [], [], []
_a = _d = 0
for _kind, _i in ITEMS:
    if _kind in ("k", "v", "mv", "o", "mk", "mq"):
        _a += 1
        EV_A.append(_a)
    else:
        EV_A.append(0)
    if _kind in ("mk", "mq"):
        EV_C.append(_a)
    if _kind in ("q", "g") or (_kind == "k" and _i % 2):
        _d += 1
    EV_D.append(_d + 1 if _kind == "k" and _i % 2 == 0 else _d if _kind in ("k", "q", "g") else 0)
N_EV_A = _a


def program(nc, x, ctx, cvec, adaw, adab, gmix, gffn, w_in, w_out, convw, gateb, lamv, subln, fnet, rw, rb,
            wg, wu, wd, gfin, consts, out):
    es = ExitStack()
    with es:
        def sb(name, shape, dt=F32):
            return es.enter_context(nc.sbuf_tensor(name, shape, dt))

        def sem(name):
            return es.enter_context(nc.semaphore(name))

        ring = sb("ring", [P, RING, KD * W])
        K_ = sb("consts_sb", [P, N_CONSTS])
        xl = sb("xl", [P, TT, D])
        bias = sb("bias", [P, 2, W])
        gain = sb("gain", [P, D])
        small = sb("small", [P, 512])
        cnt_i = sb("cnt_i", [P, 2], I32)
        ROOM = 20480
        arena = sb("arena", [P, ROOM])

        def cst(name, *more):
            return K_[:, CONSTS[name][0]:CONSTS[name][1]]

        ident, ones, iota = cst("ident"), cst("ones"), cst("iota")
        dft = cst("dft").rearrange("p (t n) -> p t n", t=TT)
        cosT, sinT = cst("cos"), cst("sin")
        mask = cst("mask")

        def lay(spec, base=0):
            views, at = {}, base
            for name, dims in spec:
                n = math.prod(dims)
                v = arena[:, at:at + n]
                if len(dims) == 2:
                    v = v.rearrange("p (a b) -> p a b", a=dims[0])
                if len(dims) == 3:
                    v = v.rearrange("p (a b c) -> p a b c", a=dims[0], b=dims[1])
                views[name] = v
                at += n
            assert at <= ROOM, at
            return views, at

        MODS = 11776
        mods = arena[:, MODS:MODS + 7 * D].rearrange("p (a n) -> p a n", a=7)
        mod1, mod0 = mods[:, 0:6, :], mods[:, 3:7, :]
        mx, at = lay([("hT", (KD, TOK)), ("kT", (4, TOK)), ("qT", (4, SEQ)), ("v", (NT, W)), ("mv", (NT, W)),
                      ("mkT", (HEADS, TOK)), ("mqT", (HEADS, SEQ)), ("acc", (W,))])
        assert at <= MODS + 3 * D
        mx.update(lay([("og", (TT, W)), ("xcst", (480,))], MODS + 7 * D)[0])
        hT, kT, qT, v_, mv, mkT, mqT, og, acc0 = (mx[n] for n in (
            "hT", "kT", "qT", "v", "mv", "mkT", "mqT", "og", "acc"))
        work = gain[:]
        early, _ = lay([("h", (2, D)), ("junk", (D,)), ("mod", (4, D)), ("xc", (TT, D))], KD * TOK)
        modc = early["mod"]
        xc, hst = early["xc"], early["h"]
        late, _ = lay([("mg", (TT, D)), ("mgT", (KD, SEQ))])
        mg, mgT = late["mg"], late["mgT"]
        me, _ = lay([("f", (TT, D)), ("fT", (KD, SEQ)), ("y", (TT, D)), ("xTg", (KD, P)), ("Yg", (D,)),
                     ("Pg", (GP, TT, P)), ("PT", (GP, SEQ)), ("sg", (2, FE)), ("h", (FE,)), ("hT", (FE,)),
                     ("acc", (W,))])
        f_, fT, y_, xTg, Yg, Pg, PT, sg, he, heT, acc1 = (me[n] for n in (
            "f", "fT", "y", "xTg", "Yg", "Pg", "PT", "sg", "h", "hT", "acc"))
        fo, _ = lay([("Z", (KD, 2 * SEQ)), ("FT", (KD, SEQ))], 2048)
        Z, FT = fo["Z"], fo["FT"]

        so = [0]

        def sm(n):
            a = so[0]
            so[0] += n
            assert so[0] <= 512
            return small[:, a:a + n]

        cc = sm(2 * KD)
        convs = sm(2 * HEADS * 3)
        rw_s = sm(KD * NE)
        rb_s = sm(NE)
        gb_s = sm(NE)
        lam_s = sm(8)
        ssq = sm(8)
        rstd = sm(8)
        att = sm(16)
        oss = sm(8)
        ors = sm(8)
        wgt_s = sm(KD * NE)
        bt = sm(TT * 8)
        G16 = mx["xcst"][:, 0:64].rearrange("p (t c) -> p t c", t=NT)
        lfF = mx["xcst"][:, 64:96].rearrange("p (t c) -> p t c", t=NT)
        lfB = mx["xcst"][:, 96:128].rearrange("p (t c) -> p t c", t=NT)
        nlfF = mx["xcst"][:, 128:160].rearrange("p (t c) -> p t c", t=NT)
        nlfB = mx["xcst"][:, 160:192].rearrange("p (t c) -> p t c", t=NT)
        li8 = mx["xcst"][:, 192:224].rearrange("p (t c) -> p t c", t=NT)
        gtmp = mx["xcst"][:, 224:288].rearrange("p (t c) -> p t c", t=NT)
        gtmp2 = mx["xcst"][:, 288:352].rearrange("p (t c) -> p t c", t=NT)
        subs = mx["xcst"][:, 352:480]
        r8 = work[0:8, W:2 * W]
        E_ = arena[:, TT * D:2 * TT * D].rearrange("p (b n) -> p b n", b=4)
        Wc = work[:, 0:W]
        lamrow = mx["xcst"][:, 0:256]
        WT = acc0

        rt, _ = lay([("aff", (TT, NE)), ("bi", (TT, NE)), ("t16", (TT, NE)), ("u16", (TT, NE)), ("o1", (TT, NE)),
                     ("o2", (TT, NE)), ("pair", (TT, 6 * NG)), ("gs", (TT, NG)), ("ing", (TT, NG)),
                     ("g1", (TT, NG)), ("s1", (TT, 8))], 2048 * 3)
        key = sm(TT * 8).rearrange("p (t c) -> p t c", t=TT)
        comb4 = sm(TT * EG).rearrange("p (t c) -> p t c", t=TT)
        combS = sm(GP * EG)

        ps = [es.enter_context(nc.psum_tensor(f"bank{b}", [P, W], F32)) for b in range(8)]

        consts_in, x_in, c_in, xc_in, smalls_in, gain_in = (sem(n) for n in (
            "consts_in", "x_in", "c_in", "xc_in", "smalls_in", "gain_in"))
        bias_in = [sem(f"bias_in{b}") for b in range(2)]
        full0 = [sem(f"ring_full_a{s}") for s in range(RING)]
        full1 = [sem(f"ring_full_b{s}") for s in range(RING)]
        w_used = [sem("w_used_a"), sem("w_used_b")]
        dve_c, act_c, dve_l, bias_zero, silu_c, one_minus = (sem(n) for n in (
            "dve_chain", "act_chain", "dve_loop_chain", "bias_zero", "silu_c", "one_minus"))
        acc_ready, ada_sum, mod_ready = (sem(n) for n in ("acc_ready", "ada_sum", "mod_ready"))
        sq_ready, ms_ready, root_ready, h_ready, ht_ps, ht_ready, gain_used = (sem(n) for n in (
            "sq_ready", "ms_ready", "root_ready", "h_ready", "hT_in_psum", "hT_ready", "gain_used"))
        proj, evac_a, evac_d, conv_done = (sem(n) for n in ("proj_done", "evac_by_act", "evac_by_dve", "conv_done"))
        exp_g, ln_g, gate_x, lf_ready, r_ps, r_ready, b_ready = (sem(n) for n in (
            "gate_exp", "gate_ln", "gate_x", "lf_ready", "r_in_psum", "r_ready", "b_ready"))
        lam_e, lam_x = sem("lam_exp"), sem("lam_sum")
        s_ps, nmax, prob, wc_ready, wt_ps, wt_ready, o_ps, o_used, expm = (sem(n) for n in (
            "scores_in_psum", "neg_max", "probs", "weights_ready", "wT_in_psum", "wT_ready", "o_in_psum", "o_used",
            "exp_m"))
        mg_ready, mgt_ps, mgt_ready, mix_ps, mix_used = (sem(n) for n in (
            "merged_ready", "mT_in_psum", "mT_ready", "mix_in_psum", "mix_used"))
        ft_ps, ft_ready, lg_ps, sig_ready, route_m, rank_ps, count_ready, z_ps, z_ready, fT2_ps, fT2_ready = (
            sem(n) for n in ("fT_in_psum", "fT_ready", "logits_in_psum", "affinity_ready", "member_ready", "rank_in_psum",
                             "count_ready", "z_in_psum", "z_ready", "FT_in_psum", "FT_ready"))
        L = []
        for l in range(2):
            L.append({n: sem(f"{n}{l}") for n in ("p_ready", "gathered", "x_ready", "silu_done",
                                                  "he_ready", "t_done", "heT_ready", "y_copied",
                                                  "scattered", "added", "m_free")})
        stored = sem("stored")

        block = es.enter_context(nc.Block())

        n_pe, n_ada, used_at = 0, 0, []
        for kind, c in STREAM:
            if kind == "ada":
                n_ada += 1
                if c < 4:
                    n_pe += 1
                used_at.append((n_pe if c < 4 else 0, n_ada))
            else:
                n_pe += 1
                used_at.append((n_pe, 0))
        PE0, ADA0 = n_pe, n_ada
        WBASE = [PE0, RING]
        BASE0 = len(STREAM) % RING
        slot_of = {c: n % RING for n, c in enumerate(STREAM)}
        fill_of = {c: n // RING + 1 for n, c in enumerate(STREAM)}
        ES = [expert_stream(True), expert_stream(False)]
        assert all(len(s) % RING == 0 for s in ES)
        BASE1 = (BASE0 + 2) % RING
        EBASE = [BASE0, BASE1]
        FILLS = [[(len(STREAM) + RING - 1 - s) // RING for s in range(RING)],
                 [1 if (s - BASE0) % RING < 2 else 0 for s in range(RING)]]
        full = [full0, full1]

        def turn_slot(l, n):
            return (EBASE[l] + n) % RING

        def turn_fill(l, j, n):
            per = len(ES[l]) // RING
            return 16 * (FILLS[l][turn_slot(l, n)] + n // RING + 1) + j * (16 * per)

        def nth(l, kind, i):
            pe_chunks = [c for c in ES[l] if c[0] != "ada"]
            return WBASE[l] + pe_chunks.index((kind, i)) + 1

        ada_v = adaw.rearrange("l (p k) n -> l p k n", k=KD)
        w_in_v = w_in.rearrange("(p k) n -> p k n", k=KD)
        w_out_v = w_out.rearrange("(p k) n -> p k n", k=KD)
        fnet_v = fnet.rearrange("(k p) n -> p k n", p=P)

        def slot(s):
            return ring[:, s, :].rearrange("p (k n) -> p k n", k=KD)

        H_FIN = 6 * TT
        src_of = [xc, xl]
        MIX = {2: 4, 3: 8, 4: 12, 5: 16}
        MIXED = [6, 14]

        @block.sync
        def _(sp):
            sp.dma_start(cc, cvec).then_inc(c_in, 16)
            sp.dma_start(K_[:], consts).then_inc(consts_in, 16)
            n_bias = 0
            sp.wait_ge(bias_zero, 1)
            for n, (kind, c) in enumerate(STREAM):
                s = n % RING
                if n >= RING:
                    pe_n, ada_n = used_at[n - RING]
                    if pe_n:
                        sp.wait_ge(w_used[0], pe_n)
                    if ada_n:
                        sp.wait_ge(acc_ready, ada_n)
                if kind == "ada":
                    src = ada_v[0, :, :, c * W:(c + 1) * W]
                elif kind == "in":
                    src = w_in_v[:, :, c:c + W]
                else:
                    src = w_out_v[:, :, c * W:(c + 1) * W]
                sp.dma_start(slot(s), src).then_inc(full0[s], 16)
                if kind == "ada":
                    if c >= 2:
                        sp.wait_ge(acc_ready, c - 1)
                        sp.wait_ge(w_used[0], min(c - 1, 4))
                    sp.dma_start(bias[0:1, c % 2, :], adab[0:1, c * W:(c + 1) * W]).then_inc(bias_in[c % 2], 16)
                if n == 0:
                    sp.dma_start(xl[:], x.rearrange("(t p) d -> p t d", p=P)).then_inc(x_in, 16)
                    sp.dma_start(xc, ctx.rearrange("(t p) d -> p t d", p=P)).then_inc(xc_in, 16)
                    sp.dma_start(gain[:], gmix[0:1, :].to_broadcast([P, D])).then_inc(gain_in, 16)
                    sp.dma_start(wgt_s.rearrange("p (k n) -> p k n", k=KD),
                                 w_in_v[:, :, C_G:C_G + NE]).then_inc(smalls_in, 16)
                    for dst, src in ((convs, convw), (rw_s, rw.rearrange("(p k) n -> p (k n)", k=KD)),
                                     (rb_s, rb.to_broadcast([P, NE])), (gb_s, gateb.to_broadcast([P, NE])),
                                     (subs, subln.to_broadcast([P, HD]))):
                        sp.dma_start(dst, src).then_inc(smalls_in, 16)
                    sp.dma_start(lamrow, lamv.to_broadcast([P, 4 * QK])).then_inc(smalls_in, 16)

            def load_turn(l, j, turn):
                for n, (kind, i) in enumerate(ES[l]):
                    s = turn_slot(l, n)
                    prev_pe = [m for m, (k, _) in enumerate(ES[l]) if k != "ada" and m <= n - RING]
                    if n < RING:
                        sp.wait_ge(w_used[l], turn * (3 * EP) + (WBASE[l] - (RING - 1 - n)))
                    elif ES[l][n - RING][0] == "ada":
                        sp.wait_ge(acc_ready, turn * 6 + (ADA0 + ES[l][n - RING][1] + 1))
                    else:
                        sp.wait_ge(w_used[l], turn * (3 * EP) + (WBASE[l] + len(prev_pe)))
                    if kind == "ada":
                        sp.dma_start(slot(s), ada_v[1, :, :, bass.ds(j * (6 * W) + i * W, W)]).then_inc(full[l][s], 16)
                        sp.wait_ge(acc_ready, turn * 6 + (ADA0 + i - 1))
                        sp.dma_start(bias[0:1, i % 2, :],
                                     adab[1:2, bass.ds(j * (6 * W) + i * W, W)]).then_inc(bias_in[i % 2], 16)
                    else:
                        wt, rows = (wd, KF) if kind == "down" else (wg if kind == "gate" else wu, KD)
                        src = wt[l, bass.ds(j * EP + i, 1), :, :].rearrange("e (p k) n -> p (e k n)", k=rows)
                        sp.dma_start(ring[:, s, :], src).then_inc(full[l][s], 16)

            def load_experts(l):
                with sp.Fori(0, TURNS) as j:
                    load_turn(l, j, j)
                sp.wait_ge(count_ready, l + 1)
                n_rounds = sp.value_load(cnt_i[0:1, l:l + 1], min_val=1, max_val=2)
                with sp.If(n_rounds > 1):
                    with sp.Fori(0, TURNS) as j:
                        load_turn(l, j, j + TURNS)

            load_experts(0)
            sp.wait_ge(w_used[1], RING - 2)
            for hf in range(2):
                s = (BASE0 + hf) % RING
                sp.dma_start(slot(s), fnet_v[:, :, hf * W:(hf + 1) * W]).then_inc(full1[s], 16)
            sp.wait_ge(gain_used, 2)
            sp.dma_start(gain[:], gmix[1:2, :].to_broadcast([P, D])).then_inc(gain_in, 16)
            sp.wait_ge(gain_used, 3)
            sp.dma_start(gain[:], gffn[1:2, :].to_broadcast([P, D])).then_inc(gain_in, 16)
            load_experts(1)
            sp.wait_ge(gain_used, 4)
            sp.dma_start(gain[:], gfin.to_broadcast([P, D])).then_inc(gain_in, 16)
            sp.wait_ge(h_ready, H_FIN)
            sp.dma_start(out.rearrange("(t p) d -> p t d", p=P), f_).then_inc(stored, 16)
            sp.wait_ge(stored, 16)

        @block.scalar
        def _(act):
            chain = [0]

            def link(ins):
                chain[0] += 1
                ins.then_inc(act_c, 1)
                act.wait_ge(act_c, chain[0])

            def norm_act(n, x_wait):
                x_wait()
                for t in range(TT):
                    if t:
                        act.wait_ge(sq_ready, TT * n + t)
                    nc.scalar.activation(early["junk"], src_of[n][:, t, :], ACT.Square,
                                         accum_out=ssq[:, t:t + 1]).then_inc(sq_ready, 1)
                act.wait_ge(ms_ready, n + 1)
                nc.scalar.activation(rstd[:, 0:TT], rstd[:, 2:2 + TT], ACT.Sqrt).then_inc(root_ready, 1)


            act.wait_ge(c_in, 16)
            nc.scalar.activation(att[:, 0:2 * KD], cc, ACT.Sigmoid).then_inc(silu_c, 1)

            def mod_copy(c, dst):
                act.wait_ge(ada_sum, c + 1)
                nc.scalar.copy(dst, ps[6][:]).then_inc(mod_ready, 1)

            for c in range(4):
                mod_copy(c, modc[:, c // 2, (c % 2) * W:(c % 2 + 1) * W])
                act.wait_ge(w_used[0], c + 1)
                nc.scalar.copy(modc[:, 2 + c // 2, (c % 2) * W:(c % 2 + 1) * W], ps[7][:]).then_inc(mod_ready, 1)
            act.wait_ge(smalls_in, 16 * 7)
            norm_act(0, lambda: act.wait_ge(xc_in, 16))
            norm_act(1, lambda: act.wait_ge(x_in, 16))
            for t in range(NT):
                for b in range(2):
                    act.wait_ge(ht_ps, 2 * t + b + 1)
                    nc.scalar.copy(hT[:, 4 * b:4 * b + 4, t * P:(t + 1) * P],
                                   ps[(2 * t + b) % 6][:].rearrange("p (k n) -> p k n", k=4)).then_inc(ht_ready, 1)

            def mod0_copy(c):
                act.wait_ge(ada_sum, c + 1)
                nc.scalar.copy(mod0[:, (c - 4) // 2, (c % 2) * W:(c % 2 + 1) * W], ps[6][:]).then_inc(mod_ready, 1)

            def ada_after(n):
                if n - 1 in ADA_AFTER:
                    mod0_copy(ADA_AFTER[n - 1])

            def a_evac(n, dst, src, fn=ACT.Copy, first=True):
                if first:
                    act.wait_ge(proj, n + 1)
                return nc.scalar.activation(dst, src, fn)

            for n, item in enumerate(ITEMS):
                kind, a = item
                bank = ps[n % 6]
                if kind == "k":
                    b, par = a // 2, a % 2
                    for g in range(4):
                        hm = 4 * b + g
                        ins = a_evac(n, kT[(hm % 2) * 64 + par * 32:(hm % 2) * 64 + par * 32 + 32, hm // 2, 0:SEQ],
                                     bank[32 * g:32 * g + 32, 0:SEQ], first=g == 0)
                    ins.then_inc(evac_a, 1)
                elif kind == "v":
                    a_evac(n, v_[:, a, :], bank[:]).then_inc(evac_a, 1)
                elif kind == "mv":
                    a_evac(n, mv[:, a, :], bank[:]).then_inc(evac_a, 1)
                elif kind == "o":
                    a_evac(n, og[:, a, :], bank[:], ACT.Sigmoid).then_inc(evac_a, 1)
                elif kind == "mk":
                    act.wait_ge(conv_done, a + 1)
                    nc.scalar.activation(mkT[:, a, :], work[:, (a % 2) * TOK:(a % 2 + 1) * TOK],
                                         ACT.Silu).then_inc(evac_a, 1)
                elif kind == "mq":
                    act.wait_ge(conv_done, HEADS + a + 1)
                    nc.scalar.activation(mqT[:, 2 * a:2 * a + 2, :],
                                         work[:, (a % 2) * TOK:(a % 2 + 1) * TOK].rearrange("p (a n) -> p a n", a=2),
                                         ACT.Silu).then_inc(evac_a, 1)
                ada_after(n)
            act.wait_ge(lam_x, 1)
            nc.scalar.activation(lam_s[:, 2:4], lam_s[:, 0:2], ACT.Exp).then_inc(lam_e, 1)
            act.wait_ge(gate_x, 1)
            nc.scalar.activation(gtmp, gtmp2, ACT.Exp, scale=-1.0).then_inc(exp_g, 1)
            act.wait_ge(gate_x, 2)
            nc.scalar.activation(gtmp2, gtmp, ACT.Ln).then_inc(ln_g, 1)

            def probs(it):
                base = 3 * (it % 2)
                if it < 8:
                    act.wait_ge(nmax, it + 1)
                    for m in range(2):
                        nc.scalar.activation(E_[:, 2 * (it % 2) + m, :], ps[base + m][:], ACT.Exp,
                                             bias=att[:, 2 * (it % 2) + m:2 * (it % 2) + m + 1], scale=QK ** -0.5,
                                             accum_out=att[:, 4 + 2 * (it % 2) + m:5 + 2 * (it % 2) + m]
                                             ).then_inc(prob, 1)
                else:
                    act.wait_ge(nmax, it + 1)
                    for m in range(2):
                        nc.scalar.activation(E_[:, 2 * (it % 2) + m, :], ps[base + 1 + m][:], ACT.Exp,
                                             bias=att[:, 2 * (it % 2) + m:2 * (it % 2) + m + 1]).then_inc(prob, 1)
                    act.wait_ge(b_ready, it - 8 + 2)
                    nc.scalar.activation(att[:, 12 + 2 * (it % 2):14 + 2 * (it % 2)],
                                         att[:, 8 + 2 * (it % 2):10 + 2 * (it % 2)], ACT.Exp).then_inc(expm, 1)

            def wt_copy(it):
                act.wait_ge(wt_ps, it + 1)
                nc.scalar.copy(WT, ps[6][:]).then_inc(wt_ready, 1)

            def o_copy(it):
                act.wait_ge(o_ps, it + 1)
                if it < 8:
                    h, t = it // 2, it % 2
                    nc.scalar.copy(mg[:, t, h * HD:(h + 1) * HD], ps[7][:, 0:HD])
                    nc.scalar.activation(mx["xcst"][:, 224:352], ps[7][:, 0:HD], ACT.Square,
                                         accum_out=oss[:, it:it + 1]).then_inc(o_used, 1)

            probs(0)
            for it in range(16):
                if it + 1 < 16:
                    probs(it + 1)
                wt_copy(it)
                o_copy(it)
            act.wait_ge(ms_ready, 3)
            nc.scalar.activation(ors, oss, ACT.Sqrt).then_inc(root_ready, 1)
            act.wait_ge(mg_ready, 1)
            act.dma_start(gain[:], gffn[0:1, :].to_broadcast([P, D])).then_inc(gain_in, 16)
            for n in range(4):
                act.wait_ge(mgt_ps, n + 1)
                t, b = n // 2, n % 2
                nc.scalar.copy(mgT[:, 4 * b:4 * b + 4, t * P:(t + 1) * P],
                               ps[n][:].rearrange("p (k n) -> p k n", k=4)).then_inc(mgt_ready, 1)

            def norm2(k):
                act.wait_ge(mix_used, MIX[k])
                for t in range(TT):
                    nc.scalar.activation(arena[:, 4096 + t * D:4096 + (t + 1) * D], xl[:, t, :], ACT.Square,
                                         accum_out=ssq[:, t:t + 1]).then_inc(sq_ready, 1)
                act.wait_ge(ms_ready, k + 2)
                nc.scalar.activation(rstd[:, 0:TT], rstd[:, 2:2 + TT], ACT.Sqrt).then_inc(root_ready, 1)

            def experts(l):
                for t in range(TT):
                    for b in range(2):
                        act.wait_ge(ft_ps, 4 * l + 2 * t + b + 1)
                        nc.scalar.copy(fT[:, 4 * b:4 * b + 4, t * P:(t + 1) * P],
                                       ps[2 * t + b][:].rearrange("p (k n) -> p k n", k=4)).then_inc(ft_ready, 1)
                act.wait_ge(lg_ps, l + 1)
                nc.scalar.activation(rt["aff"], ps[7][:, 0:TT * NE].rearrange("p (t n) -> p t n", t=TT),
                                     ACT.Sigmoid).then_inc(sig_ready, 1)
                S = L[l]
                act.wait_ge(count_ready, l + 1)
                n_rounds = act.value_load(cnt_i[0:1, l:l + 1], min_val=1, max_val=2)
                with act.Fori(0, n_rounds * TURNS) as j:
                    g0 = j * GP
                    e0 = j * EP

                    def x_copy(a):
                        act.wait_ge(S["gathered"], g0 + a + 1)
                        nc.scalar.copy(xTg[:, 4:8, :], ps[6][:].rearrange("p (k n) -> p k n", k=4)
                                       ).then_inc(S["x_ready"], 1)

                    def silu(i):
                        act.wait_ge(w_used[l], j * (3 * EP) + nth(l, "gate", i))
                        nc.scalar.activation(sg[:, i % 2, :], ps[0][:], ACT.Silu).then_inc(S["silu_done"], 1)

                    def t_copy(i):
                        act.wait_ge(S["t_done"], e0 + i + 1)
                        nc.scalar.copy(heT, ps[2][:]).then_inc(S["heT_ready"], 1)

                    def y_copy(a):
                        act.wait_ge(w_used[l], j * (3 * EP) + nth(l, "down", a * EG + EG - 1))
                        for hf in range(2):
                            nc.scalar.copy(Yg[:, hf * W:(hf + 1) * W], ps[3 + hf][:]).then_inc(S["y_copied"], 1)

                    def mod_copy1(i):
                        act.wait_ge(ada_sum, j * 6 + (ADA0 + i + 1))
                        nc.scalar.copy(mod1.rearrange("p a b -> p (a b)")[:, bass.ds(ada_off(j, i), W)],
                                       ps[7][:]).then_inc(mod_ready, 1)

                    def ada_off(j, i):
                        return (j % TURNS) * (6 * W) + i * W

                    for i in range(EP):
                        if i % EG == 0:
                            x_copy(i // EG)
                            if i:
                                t_copy(i - 1)
                                y_copy(i // EG - 1)
                        silu(i)
                        if i % EG:
                            t_copy(i - 1)
                        if l == 0 and i < 6:
                            mod_copy1(i)
                    t_copy(EP - 1)
                    y_copy(GP - 1)

            norm2(2)
            experts(0)
            norm2(3)
            for m in range(KD):
                act.wait_ge(z_ps, m + 1)
                nc.scalar.copy(Z[:, m, 0:SEQ], ps[m % 4][:, 0:SEQ])
                nc.scalar.activation(Z[:, m, SEQ:2 * SEQ], ps[m % 4][:, SEQ:2 * SEQ], ACT.Copy,
                                     scale=-1.0).then_inc(z_ready, 1)
            for m in range(KD):
                act.wait_ge(fT2_ps, m + 1)
                nc.scalar.copy(FT[:, m, :], ps[4 + m % 2][:, 0:SEQ]).then_inc(fT2_ready, 1)
            norm2(4)
            experts(1)
            norm2(5)

        @block.vector
        def _(dve):
            chain = [0]

            def link(ins):
                chain[0] += 1
                ins.then_inc(dve_c, 1)
                dve.wait_ge(dve_c, chain[0])
                return ins

            nc.vector.memset(bias[:], 0.0).then_inc(bias_zero, 1)
            dve.wait_ge(silu_c, 1)
            nc.vector.tensor_tensor(cc, cc, att[:, 0:2 * KD], ALU.mult).then_inc(one_minus, 1)
            dve.wait_ge(one_minus, 1)

            def ada_part(c, w, acc, wait_full, lk):
                wait_full()
                for k in range(KD):
                    ins = nc.vector.scalar_tensor_tensor(acc, w[:, k, :], cc[:, k:k + 1],
                                                         bias[:, c % 2, :] if k == 0 else acc, ALU.mult, ALU.add)
                    if k < KD - 1:
                        lk(ins)
                return ins

            def ada0(c):
                s, f = slot_of[("ada", c)], fill_of[("ada", c)]
                if c:
                    dve.wait_ge(ada_sum, c)

                def wait_full():
                    dve.wait_ge(full0[s], 16 * f)
                    dve.wait_ge(bias_in[c % 2], 16 * (c // 2 + 1))

                ada_part(c, slot(s), acc0, wait_full, link).then_inc(acc_ready, 1)

            for c in range(4):
                ada0(c)
            dve.wait_ge(mod_ready, 8)
            dve.wait_ge(gain_in, 16)
            for m in (1, 3):
                ins = nc.vector.scalar_tensor_tensor(modc[:, m, :], modc[:, m, :], 1.0, gain[:], ALU.add, ALU.mult)
            ins.then_inc(gain_used, 1)
            dve.wait_ge(gain_used, 1)

            def mean_root(n, i, cnt=D):
                dve.wait_ge(sq_ready, 2 * n + 2)
                nc.vector.tensor_scalar(rstd[:, 2:4], ssq[:, 0:2], 1.0 / D, EPS, ALU.mult, ALU.add
                                        ).then_inc(ms_ready, 1)
                dve.wait_ge(root_ready, i)
                link(nc.vector.reciprocal(rstd[:, 4:6], rstd[:, 0:2]))

            for n in range(2):
                mean_root(n, n + 1)
                for t in range(TT):
                    q = 2 * n + t
                    if q >= 2:
                        dve.wait_ge(ht_ps, 2 * (q - 1))
                    link(nc.vector.scalar_tensor_tensor(hst[:, q % 2, :], (xc, xl)[n][:, t, :], rstd[:, 4 + t:5 + t],
                                                        modc[:, 3 if n == 0 else 1, :], ALU.mult, ALU.mult))
                    nc.vector.tensor_tensor(hst[:, q % 2, :], hst[:, q % 2, :], modc[:, 2 if n == 0 else 0, :],
                                            ALU.add).then_inc(h_ready, 1)

            dve.wait_ge(smalls_in, 16 * 7)
            for m in range(2):
                link(nc.vector.tensor_tensor(lamrow[:, m * 128:m * 128 + QK], lamrow[:, m * 128:m * 128 + QK],
                                             lamrow[:, m * 128 + QK:m * 128 + 2 * QK], ALU.mult))
                ins = nc.vector.reduce_sum(lam_s[:, m:m + 1], lamrow[:, m * 128:m * 128 + QK], axis=AX)
            ins.then_inc(lam_x, 1)
            link(nc.vector.tensor_scalar(subs, subs, 1.0 - LAM_INIT, None, ALU.mult))

            def ada_after(n):
                if n in ADA_AFTER:
                    ada0(ADA_AFTER[n])

            rot = work[:, 0:1024].rearrange("p (a n) -> p a n", a=4)

            ropes = [0]

            def rope(even, odd, dst, b):
                if ropes[0]:
                    dve.wait_ge(evac_d, ropes[0])
                ropes[0] += 1
                nc.vector.tensor_tensor(rot[:, 0, :], even, cosT, ALU.mult)
                nc.vector.tensor_tensor(rot[:, 1, :], odd, sinT, ALU.mult)
                nc.vector.tensor_tensor(rot[:, 2, :], even, sinT, ALU.mult)
                link(nc.vector.tensor_tensor(rot[:, 3, :], odd, cosT, ALU.mult))
                for par, op in ((0, ALU.subtract), (1, ALU.add)):
                    for g in range(4):
                        hm = 4 * b + g
                        o = (hm % 2) * 64 + par * 32
                        ins = nc.vector.tensor_tensor(dst(o, hm // 2), rot[32 * g:32 * g + 32, 2 * par, :],
                                                      rot[32 * g:32 * g + 32, 2 * par + 1, :], op)
                return ins

            def conv(src, dst, taps):
                for s_ in range(2):
                    sl, dl, tp = src[:, s_ * SEQ:(s_ + 1) * SEQ], dst[:, s_ * SEQ:(s_ + 1) * SEQ], taps(s_)
                    link(nc.vector.tensor_scalar(dl, sl, tp[:, 1:2], None, ALU.mult))
                    link(nc.vector.scalar_tensor_tensor(dl[:, 1:SEQ], sl[:, 0:SEQ - 1], tp[:, 0:1], dl[:, 1:SEQ],
                                                        ALU.mult, ALU.add))
                    ins = nc.vector.scalar_tensor_tensor(dl[:, 0:SEQ - 1], sl[:, 1:SEQ], tp[:, 2:3],
                                                         dl[:, 0:SEQ - 1], ALU.mult, ALU.add)
                    if s_ == 0:
                        link(ins)
                ins.then_inc(conv_done, 1)

            tap = convs.rearrange("p (h j) -> p h j", j=3)
            for n, (kind, a) in enumerate(ITEMS):
                bank = ps[n % 6]
                if kind == "k" and a % 2 == 1:
                    dve.wait_ge(proj, n + 1)
                    dve.wait_ge(evac_a, EV_A[n])
                    b = a // 2
                    ins = rope(ps[(n - 1) % 6][:, SEQ:TOK], bank[:, SEQ:TOK],
                               lambda o, t: kT[o:o + 32, t, SEQ:TOK], b)
                    ins.then_inc(evac_d, 1)
                if kind == "q":
                    dve.wait_ge(proj, n + 1)
                    ins = rope(bank[:, 0:SEQ], bank[:, SEQ:TOK], lambda o, t: qT[o:o + 32, t, :], a)
                    ins.then_inc(evac_d, 1)
                if kind == "mk" or kind == "mq":
                    ci = a if kind == "mk" else HEADS + a
                    dve.wait_ge(proj, n + 1)
                    if ci == 0:
                        dve.wait_ge(evac_d, ropes[0])
                    if ci >= 2:
                        dve.wait_ge(evac_a, EV_C[ci - 2])
                    conv(bank, work[:, (a % 2) * TOK:(a % 2 + 1) * TOK],
                         (lambda s_: tap[:, HEADS + a, :]) if kind == "mk" else (lambda s_: tap[:, 2 * a + s_, :]))
                if kind == "g":
                    dve.wait_ge(proj, n + 1)
                    nc.vector.tensor_tensor(G16, bank[:, 0:NT * NE].rearrange("p (t c) -> p t c", t=NT),
                                            gb_s.rearrange("p (a c) -> p a c", a=1).to_broadcast([P, NT, NE]),
                                            ALU.add).then_inc(evac_d, 1)
                ada_after(n)
            dve.wait_ge(evac_d, EV_D[len(ITEMS) - 1])
            for z in (lfF, lfB, nlfF, nlfB):
                nc.vector.memset(z, 0.0)
            nc.vector.scalar_tensor_tensor(gtmp2, G16, -1.0, G16, ALU.mult, ALU.max).then_inc(gate_x, 1)
            dve.wait_ge(exp_g, 1)
            nc.vector.tensor_scalar(gtmp, gtmp, 1.0, None, ALU.add).then_inc(gate_x, 1)
            dve.wait_ge(ln_g, 1)
            link(nc.vector.scalar_tensor_tensor(gtmp, G16, 0.0, gtmp2, ALU.min, ALU.subtract))
            link(nc.vector.tensor_copy(lfF[:, :, 0:4], gtmp[:, :, 4:8]))
            link(nc.vector.tensor_copy(lfB[:, :, 4:8], gtmp[:, :, 12:16]))
            nc.vector.tensor_scalar(nlfF[:, :, 0:4], gtmp[:, :, 4:8], -1.0, None, ALU.mult)
            nc.vector.tensor_scalar(nlfB[:, :, 4:8], gtmp[:, :, 12:16], -1.0, None, ALU.mult)
            nc.vector.tensor_copy(li8[:, :, 0:4], G16[:, :, 0:4])
            nc.vector.tensor_copy(li8[:, :, 4:8], G16[:, :, 8:12]).then_inc(lf_ready, 1)
            dve.wait_ge(lam_e, 1)
            link(nc.vector.tensor_tensor(lam_s[:, 4:5], lam_s[:, 3:4], lam_s[:, 2:3], ALU.subtract))
            link(nc.vector.tensor_scalar(lam_s[:, 5:6], lam_s[:, 4:5], LAM_INIT, None, ALU.subtract))
            dve.wait_ge(r_ps, 1)
            nc.vector.tensor_copy(r8, ps[6][0:8, :]).then_inc(r_ready, 1)
            nc.vector.tensor_copy(bt, ps[7][:, 0:TT * 8]).then_inc(b_ready, 1)
            dve.wait_ge(b_ready, 1)

            def maxes(it):
                dve.wait_ge(s_ps, it + 1)
                base, o = 3 * (it % 2), 2 * (it % 2)
                if it < 8:
                    for m in range(2):
                        ins = nc.vector.tensor_reduce(att[:, o + m:o + m + 1], ps[base + m][:], AX, ALU.max, negate=True)
                    link(ins)
                    nc.vector.tensor_scalar(att[:, o:o + 2], att[:, o:o + 2], QK ** -0.5, None, ALU.mult
                                            ).then_inc(nmax, 1)
                else:
                    h, t = (it - 8) // 2, it % 2
                    for m in range(2):
                        ins = nc.vector.tensor_reduce(att[:, o + m:o + m + 1], ps[base + 1 + m][:], AX, ALU.max,
                                                      negate=True)
                    ins.then_inc(nmax, 1)
                    dve.wait_ge(nmax, it + 1)
                    nc.vector.tensor_tensor(att[:, 8 + o:10 + o], att[:, o:o + 2],
                                            bt.rearrange("p (t m h) -> p t m h", t=TT, m=2)[:, t, :, h],
                                            ALU.subtract).then_inc(b_ready, 1)

            def combine(it):
                o = 2 * (it % 2)
                dve.wait_ge(prob, 2 * it + 2)
                if it < 8:
                    link(nc.vector.reciprocal(att[:, 4 + o:6 + o], att[:, 4 + o:6 + o]))
                    link(nc.vector.tensor_tensor(att[:, 5 + o:6 + o], att[:, 5 + o:6 + o], lam_s[:, 5:6], ALU.mult))
                else:
                    base = 3 * (it % 2)
                    for m in range(2):
                        ins = nc.vector.tensor_tensor_reduce(
                            out=E_[:, o + m, :], in0=E_[:, o + m, :], in1=ps[base][:], scale=HD ** -0.5, scalar=0.0,
                            op0=ALU.mult, op1=ALU.add, accum_out=att[:, 4 + o + m:5 + o + m])
                    link(ins)
                    dve.wait_ge(expm, it - 8 + 1)
                    link(nc.vector.scalar_tensor_tensor(att[:, 4 + o:6 + o], att[:, 4 + o:6 + o], -1.0,
                                                        att[:, 4 + o:6 + o], ALU.mult, ALU.max))
                    link(nc.vector.tensor_tensor(att[:, 4 + o:6 + o], att[:, 4 + o:6 + o],
                                                 att[:, 12 + o:14 + o], ALU.max))
                    link(nc.vector.reciprocal(att[:, 4 + o:6 + o], att[:, 4 + o:6 + o]))
                if it >= 1:
                    dve.wait_ge(wt_ps, it)
                link(nc.vector.tensor_scalar(Wc, E_[:, o, :], att[:, 4 + o:5 + o], None, ALU.mult))
                nc.vector.scalar_tensor_tensor(Wc, E_[:, o + 1, :], att[:, 5 + o:6 + o], Wc, ALU.mult, ALU.add
                                               ).then_inc(wc_ready, 1)

            def o_gate(it):
                if it >= 8:
                    h, t = (it - 8) // 2, it % 2
                    dve.wait_ge(o_ps, it + 1)
                    nc.vector.tensor_tensor(mg[:, t, W + h * HD:W + (h + 1) * HD], ps[7][:, 0:HD],
                                            og[:, t, h * HD:(h + 1) * HD], ALU.mult).then_inc(o_used, 1)

            maxes(0)
            for it in range(16):
                if it + 1 < 16:
                    maxes(it + 1)
                combine(it)
                if it >= 1:
                    o_gate(it - 1)
            o_gate(15)
            dve.wait_ge(o_used, 16)
            nc.vector.tensor_scalar(oss, oss, 1.0 / HD, EPS, ALU.mult, ALU.add).then_inc(ms_ready, 1)
            dve.wait_ge(root_ready, 3)
            link(nc.vector.reciprocal(oss, ors))
            for it in range(8):
                h, t = it // 2, it % 2
                m = mg[:, t, h * HD:(h + 1) * HD]
                ins = nc.vector.scalar_tensor_tensor(m, m, oss[:, it:it + 1], subs, ALU.mult, ALU.mult)
            ins.then_inc(mg_ready, 1)

            mixed = [0]

            def residual(n, banks, gate):
                for q, b in enumerate(banks):
                    hf, t = q // 2, q % 2
                    dve.wait_ge(mix_ps, n + q + 1)
                    sl = slice(hf * W, (hf + 1) * W)
                    tmp = sgt[:, q % 2, :]
                    link(nc.vector.tensor_tensor(tmp, ps[b][:], gate[:, sl], ALU.mult))
                    nc.vector.tensor_tensor(xl[:, t, sl], xl[:, t, sl], tmp, ALU.add).then_inc(mix_used, 1)
                dve.wait_ge(mix_used, n + len(banks) + mixed[0])

            sgt = arena[:, 8192:8192 + 1024].rearrange("p (a n) -> p a n", a=2)

            def norm_mod(n, i, scale, shift, wait_gain):
                mean_root(n, i)
                dve.wait_ge(gain_in, 16 * wait_gain)
                if scale is not None:
                    nc.vector.scalar_tensor_tensor(scale, scale, 1.0, gain[:], ALU.add, ALU.mult
                                                   ).then_inc(gain_used, 1)
                    dve.wait_ge(gain_used, n)
                g = gain[:] if scale is None else scale
                for t in range(TT):
                    ins = nc.vector.scalar_tensor_tensor(f_[:, t, :], xl[:, t, :], rstd[:, 4 + t:5 + t], g,
                                                         ALU.mult, ALU.mult)
                    if shift is not None:
                        link(ins)
                        ins = nc.vector.tensor_tensor(f_[:, t, :], f_[:, t, :], shift, ALU.add)
                    ins.then_inc(h_ready, 1)

            def route(l):
                dve.wait_ge(sig_ready, l + 1)
                aff, bi, t16, u16, o1, o2 = (rt[n] for n in ("aff", "bi", "t16", "u16", "o1", "o2"))
                pair, gs, ing, g1, s1 = (rt[n] for n in ("pair", "gs", "ing", "g1", "s1"))

                def bc(a, n, m):
                    return a.rearrange("p (a c) -> p a c", a=1).to_broadcast([P, n, m])

                link(nc.vector.tensor_tensor(bi, aff, bc(rb_s, TT, NE), ALU.add))
                for t in range(TT):
                    b4 = bi[:, t, :].rearrange("p (g e) -> p g e", g=NG)
                    pr = pair[:, t, :].rearrange("p (g q) -> p g q", g=NG)
                    q = 0
                    for a in range(EG):
                        for b in range(a + 1, EG):
                            ins = nc.vector.tensor_tensor(pr[:, :, q], b4[:, :, a], b4[:, :, b], ALU.add)
                            q += 1
                    link(ins)
                    link(nc.vector.tensor_reduce(gs[:, t, :], pr, AX, ALU.max))
                    link(nc.vector.reduce_max(s1[:, t, 0:1], gs[:, t, :], AX))
                    link(nc.vector.scalar_tensor_tensor(g1[:, t, :], gs[:, t, :], s1[:, t, 0:1], cst("first4"),
                                                        ALU.is_equal, ALU.mult))
                    link(nc.vector.reduce_max(s1[:, t, 1:2], g1[:, t, :], AX))
                    nc.vector.tensor_scalar(ing[:, t, :], cst("first4"), s1[:, t, 1:2], None, ALU.is_equal
                                            ).then_inc(route_m, 1)
                dve.wait_ge(route_m, TT * (l + 1))
                for t in range(TT):
                    inb = ing[:, t, :].rearrange("p (g a) -> p g a", a=1).to_broadcast([P, NG, EG])
                    b4 = bi[:, t, :].rearrange("p (g e) -> p g e", g=NG)
                    t4 = t16[:, t, :].rearrange("p (g e) -> p g e", g=NG)
                    u4 = u16[:, t, :].rearrange("p (g e) -> p g e", g=NG)
                    link(nc.vector.tensor_tensor(t4, b4, inb, ALU.mult))
                    link(nc.vector.tensor_scalar(u4, inb, 1.0, BIG, ALU.subtract, ALU.mult))
                    link(nc.vector.tensor_tensor(t16[:, t, :], t16[:, t, :], u16[:, t, :], ALU.add))
                    for o, c in ((o1, 2), (o2, 4)):
                        link(nc.vector.reduce_max(s1[:, t, c:c + 1], t16[:, t, :], AX))
                        link(nc.vector.scalar_tensor_tensor(u16[:, t, :], t16[:, t, :], s1[:, t, c:c + 1],
                                                            cst("first16"), ALU.is_equal, ALU.mult))
                        link(nc.vector.reduce_max(s1[:, t, c + 1:c + 2], u16[:, t, :], AX))
                        link(nc.vector.tensor_scalar(o[:, t, :], cst("first16"), s1[:, t, c + 1:c + 2], None,
                                                     ALU.is_equal))
                        if c == 2:
                            link(nc.vector.scalar_tensor_tensor(t16[:, t, :], o1[:, t, :], -BIG, t16[:, t, :],
                                                                ALU.mult, ALU.add))
                    link(nc.vector.tensor_tensor(o1[:, t, :], o1[:, t, :], o2[:, t, :], ALU.add))
                    link(nc.vector.tensor_tensor(o1[:, t, :], o1[:, t, :], aff[:, t, :], ALU.mult))
                    link(nc.vector.reduce_sum(s1[:, t, 6:7], o1[:, t, :], axis=AX))
                    link(nc.vector.reciprocal(s1[:, t, 7:8], s1[:, t, 6:7]))
                    link(nc.vector.tensor_scalar(o1[:, t, :], o1[:, t, :], s1[:, t, 7:8], None, ALU.mult))
                    link(nc.vector.reduce_sum(comb4[:, t, :], o1[:, t, :].rearrange("p (g e) -> p e g", g=NG),
                                              axis=AX))
                dve.wait_ge(rank_ps, l + 1)
                link(nc.vector.scalar_tensor_tensor(g1, ps[7][:, 64:64 + TT * NG].rearrange("p (t g) -> p t g", t=TT),
                                                    1.0, ing, ALU.add, ALU.mult))
                link(nc.vector.tensor_scalar(key[:, :, 0:NG], g1, 1.0, None, ALU.subtract))
                link(nc.vector.tensor_scalar(key[:, :, NG:2 * NG], g1, 1.0 + P, None, ALU.subtract))
                link(nc.vector.reduce_max(s1[:, 0, 0:1], ps[7][:, 64 + TT * NG:64 + TT * NG + NG], AX))
                link(nc.vector.tensor_scalar(s1[:, 0, 1:2], s1[:, 0, 0:1], float(P), 1.0, ALU.is_gt, ALU.add))
                nc.vector.memset(y_, 0.0)
                nc.vector.tensor_copy(cnt_i[:, l:l + 1], s1[:, 0, 1:2]).then_inc(count_ready, 1)

            def experts(l):
                S = L[l]
                dve.wait_ge(count_ready, l + 1)
                n_rounds = dve.value_load(cnt_i[0:1, l:l + 1], min_val=1, max_val=2)
                LINKS = 6 * (KD - 1) if l == 0 else 0
                nc.vector.memset(lam_s[:, 6:7], 0.0).then_inc(S["m_free"], 1)
                nc.vector.memset(lam_s[:, 7:8], 0.0).then_inc(S["added"], 1)
                with dve.Fori(0, n_rounds * TURNS) as j:
                    g0 = j * GP
                    e0 = j * EP
                    nlink = [0]

                    def lk(ins):
                        nlink[0] += 1
                        ins.then_inc(dve_l, 1)
                        dve.wait_ge(dve_l, j * LINKS + nlink[0])

                    for a in range(GP):
                        for t in range(TT):
                            ins = nc.vector.tensor_scalar(Pg[:, a, t, :], iota, key[:, t, bass.ds(g0 + a, 1)], None,
                                                          ALU.is_equal)
                        ins.then_inc(S["p_ready"], 1)

                    def x_copy(a):
                        dve.wait_ge(S["gathered"], g0 + a + 1)
                        nc.vector.tensor_copy(xTg[:, 0:4, :], ps[5][:].rearrange("p (k n) -> p k n", k=4)
                                              ).then_inc(S["x_ready"], 1)
                        nc.vector.tensor_copy(combS[:, a * EG:(a + 1) * EG], ps[7][:, 256:256 + EG])
                        nc.vector.tensor_copy(PT[:, a, :], ps[7][:, 0:SEQ]).then_inc(S["m_free"], 1)

                    def hidden(i):
                        if i % EG == 0:
                            dve.wait_ge(S["m_free"], g0 + i // EG + 2)
                        dve.wait_ge(S["silu_done"], e0 + i + 1)
                        dve.wait_ge(w_used[l], j * (3 * EP) + nth(l, "up", i))
                        nc.vector.scalar_tensor_tensor(he, sg[:, i % 2, :], combS[:, i:i + 1], ps[1][:],
                                                       ALU.mult, ALU.mult).then_inc(S["he_ready"], 1)

                    def add(a, t):
                        dve.wait_ge(S["scattered"], (g0 + a) * TT + t + 1)
                        for hf in range(2):
                            sl = slice(hf * W, (hf + 1) * W)
                            ins = nc.vector.tensor_tensor(y_[:, t, sl], y_[:, t, sl], ps[5 + hf][:], ALU.add)
                        ins.then_inc(S["added"], 1)

                    def ada1(i):
                        pos = ES[0].index(("ada", i))
                        dve.wait_ge(ada_sum, j * 6 + (ADA0 + i))

                        def wait_full():
                            dve.wait_ge(full0[turn_slot(0, pos)], turn_fill(0, j, pos))
                            dve.wait_ge(bias_in[i % 2], 16 * (6 + i // 2 + 1) + j * 48)

                        ada_part(i, slot(turn_slot(0, pos)), acc1, wait_full, lk).then_inc(acc_ready, 1)

                    for i in range(EP):
                        if i % EG == 0:
                            x_copy(i // EG)
                            if i:
                                add(i // EG - 1, 0)
                        hidden(i)
                        if i and i % EG == 0:
                            add(i // EG - 1, 1)
                        if l == 0 and i < 6:
                            ada1(i)
                    assert nlink[0] == LINKS
                    add(GP - 1, 0)
                    add(GP - 1, 1)
                return n_rounds

            def close(l, gate, n_rounds):
                S = L[l]
                dve.wait_ge(S["added"], n_rounds * (NG * TT) + 1)
                for t in range(TT):
                    nc.vector.tensor_tensor(y_[:, t, :], y_[:, t, :], gate, ALU.mult).then_inc(mix_used, 1)
                dve.wait_ge(mix_used, MIXED[l])
                for t in range(TT):
                    nc.vector.tensor_tensor(xl[:, t, :], xl[:, t, :], y_[:, t, :], ALU.add).then_inc(mix_used, 1)
                dve.wait_ge(mix_used, MIXED[l] + TT)

            residual(0, [0, 1, 2, 3], mod0[:, 0, :])
            dve.wait_ge(mod_ready, 16)
            norm_mod(2, 4, mod0[:, 2, :], mod0[:, 1, :], 2)
            route(0)
            nr = experts(0)
            dve.wait_ge(mod_ready, nr * 12 + 16)
            close(0, mod0[:, 3, :], nr)
            norm_mod(3, 5, mod1[:, 1, :], mod1[:, 0, :], 3)
            mixed[0] = 4
            residual(4, [0, 1, 2, 3], mod1[:, 2, :])
            norm_mod(4, 6, mod1[:, 4, :], mod1[:, 3, :], 4)
            route(1)
            nr = experts(1)
            close(1, mod1[:, 5, :], nr)
            norm_mod(5, 7, None, None, 5)

        @block.tensor
        def _(pe):
            mm = nc.tensor.matmul
            pe.wait_ge(consts_in, 16)
            pe.wait_ge(one_minus, 1)
            for c in range(4):
                s, fl = slot_of[("ada", c)], fill_of[("ada", c)]
                pe.wait_ge(full0[s], 16 * fl)
                pe.wait_ge(bias_in[c % 2], 16 * (c // 2 + 1))
                if c:
                    pe.wait_ge(mod_ready, 2 * c)
                for k in range(KD):
                    mm(ps[7][:], cc[:, KD + k:KD + k + 1].to_broadcast([P, P]), slot(s)[:, k, :],
                       start=(k == 0), stop=False)
                mm(ps[7][:], ones, bias[:, c % 2, :], start=False, stop=True).then_inc(w_used[0], 1)
                pe.wait_ge(acc_ready, c + 1)
                mm(ps[6][:], ones, acc0, start=True, stop=True).then_inc(ada_sum, 1)

            def turn_h(src, wait, banks, done, q0):
                for b in range(2):
                    for k in range(4):
                        ins = nc.tensor.transpose(ps[banks[b]][:, k * P:(k + 1) * P], src[:, 4 * b + k:D:KD], ident)
                    ins.then_inc(done, 1)

            for t in range(NT):
                pe.wait_ge(h_ready, t + 1)
                if t >= 3:
                    pe.wait_ge(ht_ready, 2 * (t - 3) + 2)
                turn_h(hst[:, t % 2, :], None, [(2 * t) % 6, (2 * t + 1) % 6], ht_ps, 0)
            pe.wait_ge(ht_ready, 2 * NT)
            pe.wait_ge(smalls_in, 16 * 7)

            def read(l, bank):
                mm(ps[bank][0:1, 0:1], ones[:, 0:1], ones[:, 0:1], start=True, stop=True).then_inc(w_used[l], 1)

            def ada_after(n):
                if n - 1 in ADA_AFTER:
                    c = ADA_AFTER[n - 1]
                    pe.wait_ge(acc_ready, c + 1)
                    pe.wait_ge(mod_ready, 8 + c - 4)
                    mm(ps[6][:], ones, acc0, start=True, stop=True).then_inc(ada_sum, 1)

            wgk = wgt_s.rearrange("p (k n) -> p k n", k=KD)
            for n, (kind, a) in enumerate(ITEMS):
                bank = ps[n % 6]
                if n >= 6:
                    if EV_A[n - 6]:
                        pe.wait_ge(evac_a, EV_A[n - 6])
                    if EV_D[n - 6]:
                        pe.wait_ge(evac_d, EV_D[n - 6])
                if kind != "g":
                    col = {"k": C_K, "v": C_V, "q": C_Q, "mk": C_MK, "mq": C_MQ, "mv": C_MV, "o": C_O}[kind]
                    s, fl = slot_of[("in", col)], fill_of[("in", col)]
                    w = slot(s)
                    pe.wait_ge(full0[s], 16 * fl)
                if kind == "k":
                    b, par = a // 2, a % 2
                    for k in range(KD):
                        ins = mm(bank[:], w[:, k, 256 * b + par:256 * (b + 1):2], hT[:, k, :],
                                 start=(k == 0), stop=(k == KD - 1))
                elif kind == "q":
                    for par in range(2):
                        for k in range(KD):
                            ins = mm(bank[:, par * SEQ:(par + 1) * SEQ], w[:, k, 256 * a + par:256 * (a + 1):2],
                                     hT[:, k, SEQ:TOK], start=(k == 0), stop=(k == KD - 1))
                elif kind in ("v", "mv", "o"):
                    t = a if kind != "o" else TT + a
                    for k in range(KD):
                        ins = mm(bank[:], hT[:, k, t * P:(t + 1) * P], w[:, k, :], start=(k == 0),
                                 stop=(k == KD - 1))
                elif kind == "mk":
                    for k in range(KD):
                        ins = mm(bank[:], w[:, k, a * HD:(a + 1) * HD], hT[:, k, :], start=(k == 0),
                                 stop=(k == KD - 1))
                elif kind == "mq":
                    for q in range(2):
                        for k in range(KD):
                            ins = mm(bank[:, q * SEQ:(q + 1) * SEQ], w[:, k, (2 * a + q) * HD:(2 * a + q + 1) * HD],
                                     hT[:, k, SEQ:TOK], start=(k == 0), stop=(k == KD - 1))
                else:
                    for t in range(NT):
                        for k in range(KD):
                            ins = mm(bank[:, t * NE:(t + 1) * NE], hT[:, k, t * P:(t + 1) * P], wgk[:, k, :],
                                     start=(k == 0), stop=(k == KD - 1))
                ins.then_inc(proj, 1)
                if (kind, a) in LAST_OF:
                    read(0, 7)
                ada_after(n)

            pe.wait_ge(lf_ready, 1)
            pe.wait_ge(mod_ready, 16)
            pe.wait_ge(evac_a, N_EV_A)
            le, ge, lt, gt_ = cst("le"), cst("ge"), cst("lt"), cst("gt")

            def rr(t, lhs, rhs, start=False, stop=False):
                return mm(ps[6][0:8, t * P:(t + 1) * P], lhs, rhs, start=start, stop=stop, skip_group_check=True)

            for t in range(NT):
                rr(t, li8[:, t, :], ident, start=(t == 0))
            rr(2, nlfF[:, 2, :], le)
            rr(3, nlfF[:, 2, :], ones)
            rr(3, nlfF[:, 3, :], le)
            rr(1, lfF[:, 1, :], gt_)
            rr(0, lfF[:, 1, :], ones)
            rr(0, lfF[:, 0, :], gt_)
            rr(3, nlfB[:, 3, :], ge)
            rr(2, nlfB[:, 3, :], ones)
            rr(2, nlfB[:, 2, :], ge)
            rr(0, lfB[:, 0, :], lt)
            rr(1, lfB[:, 0, :], ones)
            rr(1, lfB[:, 1, :], lt, stop=True)

            def bb(t, lhs, rhs, start=False, stop=False):
                return mm(ps[7][:, t * 8:(t + 1) * 8], lhs, rhs, start=start, stop=stop, skip_group_check=True)

            bb(0, le, lfF[:, 2, :], start=True)
            bb(1, ones, lfF[:, 2, :])
            bb(1, le, lfF[:, 3, :])
            bb(1, ge, lfB[:, 3, :])
            bb(0, ones, lfB[:, 3, :])
            bb(0, ge, lfB[:, 2, :], stop=True).then_inc(r_ps, 1)

            def scores(it):
                base = 3 * (it % 2)
                if it >= 2:
                    pe.wait_ge(prob, 2 * (it - 1))
                    pe.wait_ge(wc_ready, it - 1)
                if it < 8:
                    h, t = it // 2, it % 2
                    for m in range(2):
                        hm = 2 * h + m
                        r = slice((hm % 2) * 64, (hm % 2) * 64 + 64)
                        ins = mm(ps[base + m][:], qT[r, hm // 2, t * P:(t + 1) * P], kT[r, hm // 2, :],
                                 start=True, stop=True)
                else:
                    h, t = (it - 8) // 2, it % 2
                    if it == 8:
                        pe.wait_ge(r_ready, 1)
                    mm(ps[base][:], mqT[:, h, t * P:(t + 1) * P], mkT[:, h, :], start=True, stop=True)
                    for m in range(2):
                        row = 4 * m + h
                        bank = ps[base + 1 + m]
                        mm(bank[:], ident[0:8, row:row + 1].to_broadcast([8, P]), r8, start=True, stop=False,
                           skip_group_check=True)
                        if m == 0:
                            cols, msk = (slice(2 * P, 4 * P), mask[:, 0:2 * P]) if t == 0 else (
                                slice(3 * P, 4 * P), mask[:, 0:P])
                        else:
                            cols, msk = (slice(2 * P, 3 * P), mask[:, 2 * P:3 * P]) if t == 0 else (
                                slice(2 * P, 4 * P), mask[:, P:3 * P])
                        ins = mm(bank[:, cols], ident, msk, start=False, stop=True, skip_group_check=True)
                ins.then_inc(s_ps, 1)

            def weights_t(it):
                pe.wait_ge(wc_ready, it + 1)
                for q in range(4):
                    ins = nc.tensor.transpose(ps[6][:, q * P:(q + 1) * P], Wc[:, q * P:(q + 1) * P], ident)
                ins.then_inc(wt_ps, 1)

            def values(it):
                pe.wait_ge(wt_ready, it + 1)
                if it >= 1:
                    pe.wait_ge(o_used, it)
                h = it % 8 // 2
                vv = v_ if it < 8 else mv
                for q in range(4):
                    ins = mm(ps[7][:, 0:HD], WT[:, q * P:(q + 1) * P], vv[:, q, h * HD:(h + 1) * HD],
                             start=(q == 0), stop=(q == 3))
                ins.then_inc(o_ps, 1)

            pe.wait_ge(b_ready, 1)
            pe.wait_ge(evac_d, EV_D[-1])
            scores(0)
            for it in range(16):
                if it + 1 < 16:
                    scores(it + 1)
                weights_t(it)
                values(it)
            pe.wait_ge(mg_ready, 1)
            for t in range(TT):
                turn_h(mg[:, t, :], None, [2 * t, 2 * t + 1], mgt_ps, 0)
            pe.wait_ge(mgt_ready, 4)
            for q in range(4):
                hf, t = q // 2, q % 2
                s, fl = slot_of[("out", hf)], fill_of[("out", hf)]
                pe.wait_ge(full0[s], 16 * fl)
                for k in range(KD):
                    ins = mm(ps[q][:], mgT[:, k, t * P:(t + 1) * P], slot(s)[:, k, :], start=(k == 0),
                             stop=(k == KD - 1))
                ins.then_inc(mix_ps, 1)
                if t == TT - 1:
                    read(0, 7)

            def experts(l):
                S = L[l]
                for t in range(TT):
                    pe.wait_ge(h_ready, 2 * (2 + 2 * l) + t + 1)
                    turn_h(f_[:, t, :], None, [2 * t, 2 * t + 1], ft_ps, 0)
                pe.wait_ge(ft_ready, 4 * l + 4)
                rwk = rw_s.rearrange("p (k n) -> p k n", k=KD)
                for t in range(TT):
                    for k in range(KD):
                        ins = mm(ps[7][:, t * NE:(t + 1) * NE], fT[:, k, t * P:(t + 1) * P], rwk[:, k, :],
                                 start=(k == 0), stop=(k == KD - 1))
                ins.then_inc(lg_ps, 1)
                pe.wait_ge(route_m, TT * (l + 1))
                ing = rt["ing"]

                def rk(c, lhs, rhs, **kw):
                    return mm(ps[7][:, 64 + c * NG:64 + (c + 1) * NG], lhs, rhs, skip_group_check=True, **kw)

                rk(0, cst("lt"), ing[:, 0, :], start=True, stop=False)
                rk(1, ones, ing[:, 0, :], start=False, stop=False)
                rk(1, cst("lt"), ing[:, 1, :], start=False, stop=False)
                rk(2, ones, ing[:, 0, :], start=False, stop=False)
                rk(2, ones, ing[:, 1, :], start=False, stop=True).then_inc(rank_ps, 1)
                pe.wait_ge(count_ready, l + 1)
                n_rounds = pe.value_load(cnt_i[0:1, l:l + 1], min_val=1, max_val=2)
                where = {c: n for n, c in enumerate(ES[l])}
                with pe.Fori(0, n_rounds * TURNS) as j:
                    g0 = j * GP
                    e0 = j * EP

                    def landed(kind, i):
                        n = where[(kind, i)]
                        pe.wait_ge(full[l][turn_slot(l, n)], turn_fill(l, j, n))
                        return ring[:, turn_slot(l, n), :]

                    def gather(a):
                        pe.wait_ge(S["p_ready"], g0 + a + 1)
                        pe.wait_ge(S["added"], g0 * TT + 1)
                        pe.wait_ge(S["m_free"], g0 + a + 1)
                        if l == 0:
                            pe.wait_ge(mod_ready, j * 6 + (16 + (0 if a == 0 else EG)))
                        for k in range(KD):
                            for t in range(TT):
                                mm(ps[5 + k // 4][:, (k % 4) * P:(k % 4 + 1) * P], f_[:, t, k:D:KD],
                                   Pg[:, a, t, :], start=(t == 0), stop=(t == TT - 1))
                        for t in range(TT):
                            mm(ps[7][:, 256:256 + EG], Pg[:, a, t, :], comb4[:, t, :], start=(t == 0),
                               stop=(t == TT - 1))
                        for t in range(TT):
                            ins = nc.tensor.transpose(ps[7][:, t * P:(t + 1) * P], Pg[:, a, t, :], ident)
                        ins.then_inc(S["gathered"], 1)

                    def gate_up(i, kind):
                        w = landed(kind, i).rearrange("p (k n) -> p k n", k=KD)
                        if kind == "gate":
                            if i % EG == 0:
                                pe.wait_ge(S["x_ready"], (g0 + i // EG) * 2 + 2)
                            else:
                                pe.wait_ge(S["silu_done"], e0 + i)
                        bank = ps[0 if kind == "gate" else 1]
                        for k in range(KD):
                            ins = mm(bank[:], xTg[:, k, :], w[:, k, :], start=(k == 0), stop=(k == KD - 1))
                        ins.then_inc(w_used[l], 1)

                    def turn(i):
                        pe.wait_ge(S["he_ready"], e0 + i + 1)
                        for q in range(KF):
                            ins = nc.tensor.transpose(ps[2][:, q * P:(q + 1) * P], he[:, q:FE:KF], ident)
                        ins.then_inc(S["t_done"], 1)

                    def down(i):
                        w = landed("down", i).rearrange("p (k n) -> p k n", k=KF)
                        pe.wait_ge(S["heT_ready"], e0 + i + 1)
                        if i % EG == 0 and i:
                            pe.wait_ge(S["y_copied"], (g0 + i // EG) * 2)
                        for q in range(KF):
                            for hf in range(2):
                                ins = mm(ps[3 + hf][:], heT[:, q * P:(q + 1) * P], w[:, q, hf * W:(hf + 1) * W],
                                         start=(i % EG == 0 and q == 0), stop=(i % EG == EG - 1 and q == KF - 1),
                                         skip_group_check=True)
                        ins.then_inc(w_used[l], 1)

                    def scatter(a, t):
                        if t == 0:
                            pe.wait_ge(S["y_copied"], (g0 + a) * 2 + 2)
                            pe.wait_ge(S["m_free"], g0 + a + 2)
                        pe.wait_ge(S["added"], (g0 + a) * TT + t + 1)
                        for hf in range(2):
                            ins = mm(ps[5 + hf][:], PT[:, a, t * P:(t + 1) * P], Yg[:, hf * W:(hf + 1) * W],
                                     start=True, stop=True)
                        ins.then_inc(S["scattered"], 1)

                    def ada_sum1(i):
                        pe.wait_ge(acc_ready, j * 6 + (ADA0 + i + 1))
                        pe.wait_ge(mod_ready, j * 6 + (16 + i))
                        pe.wait_ge(S["m_free"], g0 + i // EG + 2)
                        mm(ps[7][:], ones, acc1, start=True, stop=True).then_inc(ada_sum, 1)

                    for i in range(EP):
                        if i % EG == 0:
                            gather(i // EG)
                            if i:
                                turn(i - 1)
                                down(i - 1)
                        gate_up(i, "gate")
                        if i % EG:
                            turn(i - 1)
                        elif i:
                            scatter(i // EG - 1, 0)
                        gate_up(i, "up")
                        if i % EG:
                            down(i - 1)
                        elif i:
                            scatter(i // EG - 1, 1)
                        if l == 0 and i < 6:
                            ada_sum1(i)
                    turn(EP - 1)
                    down(EP - 1)
                    scatter(GP - 1, 0)
                    scatter(GP - 1, 1)

            experts(0)
            for _ in range(RING - 2):
                read(1, 2)
            for m in range(KD):
                pe.wait_ge(h_ready, 8)
                if m >= 4:
                    pe.wait_ge(z_ready, m - 3)
                for t in range(TT):
                    ins = mm(ps[m % 4][:], f_[:, t, m * P:(m + 1) * P], dft[:, t, 0:2 * SEQ], start=(t == 0), stop=(t == 1))
                ins.then_inc(z_ps, 1)
            for m in range(KD):
                g, half = m // 2, m % 2
                pe.wait_ge(z_ready, KD)
                if m >= 2:
                    pe.wait_ge(fT2_ready, m - 1)
                for u in range(2):
                    mm(ps[4 + m % 2][:, 0:SEQ], dft[:, u, half * P:(half + 1) * P], Z[:, 2 * g + u, 0:SEQ],
                       start=(u == 0), stop=False)
                for u in range(2):
                    ins = mm(ps[4 + m % 2][:, 0:SEQ], dft[:, u, SEQ + half * P:SEQ + (half + 1) * P], Z[:, 2 * g + u, SEQ:2 * SEQ],
                             start=False, stop=(u == 1))
                ins.then_inc(fT2_ps, 1)
            pe.wait_ge(fT2_ready, KD)
            for q in range(4):
                hf, t = q // 2, q % 2
                s = (BASE0 + hf) % RING
                pe.wait_ge(full1[s], 16)
                for k in range(KD):
                    ins = mm(ps[q][:], FT[:, k, t * P:(t + 1) * P], slot(s)[:, k, :], start=(k == 0),
                             stop=(k == KD - 1))
                ins.then_inc(mix_ps, 1)
                if t == TT - 1:
                    read(1, 7)
            experts(1)


def kernel(**inputs):
    import numpy as np
    import concourse.bacc as bacc
    from concourse.bass_utils import run_bass_kernel_spmd as run

    a = {n: np.ascontiguousarray(v) for n, v in inputs.items()}
    arrays = {
        "x": a["x"].reshape(SEQ, D),
        "ctx": a["ctx"].reshape(SEQ, D),
        "cvec": np.concatenate([a["c"].reshape(P, KD), a["c_ctx"].reshape(P, KD)], 1),
        "ada_w": a["ada_w"],
        "ada_b": a["ada_b"],
        "norm_mix_g": a["norm_mix_g"],
        "norm_ffn_g": a["norm_ffn_g"],
        "w_in": a["even_w_in"][0],
        "w_out": a["even_w_out"][0],
        "conv_w": a["even_conv_w"][0].reshape(3, 2 * HEADS, HD).transpose(2, 1, 0).reshape(P, -1),
        "gate_b": a["even_gate_b"].reshape(1, -1),
        "lam": a["even_lam"].reshape(1, -1),
        "subln_g": a["even_subln_g"].reshape(1, -1),
        "w_fnet": a["odd_w_fnet"][0],
        "router_w": a["router_w"],
        "router_b": a["router_b"].reshape(1, -1),
        "w_gate": a["exp_w_gate"],
        "w_up": a["exp_w_up"],
        "w_down": a["exp_w_down"],
        "final_g": a["final_g"].reshape(1, -1),
        "constants": constants(),
    }
    arrays = {n: np.ascontiguousarray(v) for n, v in arrays.items()}
    nc = bacc.Bacc("TRN2", target_bir_lowering=False, num_devices=1)
    args = [nc.dram_tensor(f"in_{n}", v.shape, mybir.dt.from_np(v.dtype), kind="ExternalInput").ap()
            for n, v in arrays.items()]
    args.append(nc.dram_tensor("out", (SEQ, D), F32, kind="ExternalOutput").ap())
    program(nc, *args)
    r = run(nc, [{f"in_{n}": v for n, v in arrays.items()}], core_ids=[0])
    return r.results[0]["out"].reshape(1, SEQ, D)
```

```python
from contextlib import ExitStack
import math

import concourse.bass as bass
from concourse import mybir

F32 = mybir.dt.float32
I32 = mybir.dt.int32
ALU = mybir.AluOpType
ACT = mybir.ActivationFunctionType
AX = mybir.AxisListType.X

P = 128
D = 1024
KD = D // P
SEQ = 256
TT = SEQ // P
TOK = 2 * SEQ
NT = TOK // P
HEADS = 4
QK = 64
HD = 128
W = 512
FE = 512
KF = FE // P
NE = 16
NG = 4
EG = NE // NG
RING = 6
EPS = 1e-6
LAM_INIT = 0.8 - 0.6 * math.exp(0.0)
BIG = 1e30

C_Q, C_K, C_V, C_MQ, C_MK, C_MV, C_O, C_G = 0, 512, 1024, 1536, 2048, 2560, 3072, 3584

CONSTS = {}
_at = 0
for _name, _n in (("ident", P), ("dft", TT * 2 * SEQ), ("cos", SEQ), ("sin", SEQ), ("le", P), ("ge", P),
                  ("lt", P), ("gt", P), ("mask", 3 * P), ("iota", P), ("ones", P), ("first4", NG),
                  ("first16", NE)):
    CONSTS[_name] = (_at, _at + _n)
    _at += _n
N_CONSTS = _at


def constants():
    import numpy as np

    t = np.zeros((P, N_CONSTS), np.float32)

    def put(name, a):
        t[:, CONSTS[name][0]:CONSTS[name][1]] = a

    r, c = np.arange(P)[:, None], np.arange(P)[None, :]
    put("ident", r == c)
    n = np.arange(SEQ)
    ang = 2 * np.pi * ((n[:, None] * n[None, :]) % SEQ) / SEQ
    cs = np.concatenate([np.cos(ang), np.sin(ang)], 1) / math.sqrt(SEQ)
    put("dft", cs.reshape(TT, P, 2 * SEQ).transpose(1, 0, 2).reshape(P, -1))
    pairs = QK // 4
    inv = 10000.0 ** (-np.arange(pairs, dtype=np.float32) / pairs)
    pair, tok = np.arange(P)[:, None] % (2 * pairs), np.arange(SEQ)[None, :]
    pos = np.where(pair < pairs, tok // 64, tok % 64).astype(np.float32)
    rot = pos * inv[pair % pairs].astype(np.float32)
    put("cos", np.cos(rot))
    put("sin", np.sin(rot))
    put("le", r <= c)
    put("ge", r >= c)
    put("lt", r < c)
    put("gt", r > c)
    put("mask", np.concatenate([np.where(c > r, -BIG, 0), np.full((P, P), -BIG), np.where(c < r, -BIG, 0)], 1))
    put("iota", np.broadcast_to(c, (P, P)))
    put("ones", 1.0)
    put("first4", np.broadcast_to(NG - np.arange(NG), (P, NG)))
    put("first16", np.broadcast_to(NE - np.arange(NE), (P, NE)))
    return t


N_ADA = 6 * D // W
STREAM = ([("ada", c) for c in range(4)] + [("in", C_K), ("in", C_V), ("ada", 4), ("ada", 5), ("in", C_Q),
          ("ada", 6), ("ada", 7), ("in", C_MK), ("ada", 8), ("ada", 9), ("ada", 10), ("in", C_MQ), ("ada", 11),
          ("ada", 12), ("in", C_MV), ("ada", 13), ("ada", 14), ("ada", 15), ("in", C_O)]
          + [("ada", c) for c in range(16, 2 * N_ADA)] + [("out", 0), ("out", 1)])
ADA_AFTER = {4: 4, 5: 5, 6: 6, 8: 7, 10: 8, 11: 9, 12: 10, 14: 11, 16: 12, 17: 13, 18: 14, 20: 15}
ADA_STEP = {2 * n: 16 + n for n in range(8)}

TURN = [("gate", 0), ("up", 0)]
for _i in range(1, EG):
    TURN += [("gate", _i), ("up", _i), ("down", _i - 1)]
TURN += [("down", EG - 1)]
assert len(TURN) % RING == 0


ITEMS = ([("k", a) for a in range(4)] + [("v", a) for a in range(4)] + [("q", a) for a in range(2)]
         + [("mk", a) for a in range(4)] + [("mq", a) for a in range(2)] + [("mv", a) for a in range(4)]
         + [("o", a) for a in range(2)] + [("g", 0)])
LAST_OF = [("k", 3), ("v", 3), ("q", 1), ("mk", 3), ("mq", 1), ("mv", 3), ("o", 1)]
EV_A, EV_D, EV_C = [], [], []
_a = _d = 0
for _kind, _i in ITEMS:
    if _kind in ("k", "v", "mv", "o", "mk", "mq"):
        _a += 1
        EV_A.append(_a)
    else:
        EV_A.append(0)
    if _kind in ("mk", "mq"):
        EV_C.append(_a)
    if _kind in ("q", "g") or (_kind == "k" and _i % 2):
        _d += 1
    EV_D.append(_d + 1 if _kind == "k" and _i % 2 == 0 else _d if _kind in ("k", "q", "g") else 0)
N_EV_A = _a


def program(nc, x, ctx, cvec, adaw, adab, gmix, gffn, w_in, w_out, convw, gateb, lamv, subln, fnet, rw, rb,
            wg, wu, wd, gfin, consts, scratch, out):
    es = ExitStack()
    with es:
        def sb(name, shape, dt=F32):
            return es.enter_context(nc.sbuf_tensor(name, shape, dt))

        def sem(name):
            return es.enter_context(nc.semaphore(name))

        ring = sb("ring", [P, RING, KD * W])
        K_ = sb("consts_sb", [P, N_CONSTS])
        xl = sb("xl", [P, TT, D])
        bias = sb("bias", [P, 2, W])
        gain = sb("gain", [P, D])
        small = sb("small", [P, 512])
        cnt_i = sb("cnt_i", [P, 2 * NG], I32)
        ROOM = 20480
        arena = sb("arena", [P, ROOM])

        def cst(name, *more):
            return K_[:, CONSTS[name][0]:CONSTS[name][1]]

        ident, ones, iota = cst("ident"), cst("ones"), cst("iota")
        dft = cst("dft").rearrange("p (t n) -> p t n", t=TT)
        cosT, sinT = cst("cos"), cst("sin")
        mask = cst("mask")

        def lay(spec, base=0):
            views, at = {}, base
            for name, dims in spec:
                n = math.prod(dims)
                v = arena[:, at:at + n]
                if len(dims) == 2:
                    v = v.rearrange("p (a b) -> p a b", a=dims[0])
                if len(dims) == 3:
                    v = v.rearrange("p (a b c) -> p a b c", a=dims[0], b=dims[1])
                views[name] = v
                at += n
            assert at <= ROOM, at
            return views, at

        MODS = 11776
        mods = arena[:, MODS:MODS + 7 * D].rearrange("p (a n) -> p a n", a=7)
        mod1, mod0 = mods[:, 0:6, :], mods[:, 3:7, :]
        SC = [0, 1, 5, 6]
        mx, at = lay([("hT", (KD, TOK)), ("kT", (4, TOK)), ("qT", (4, SEQ)), ("v", (NT, W)), ("mv", (NT, W)),
                      ("mkT", (HEADS, TOK)), ("mqT", (HEADS, SEQ)), ("acc", (W,))])
        assert at <= MODS + 3 * D
        mx.update(lay([("og", (TT, W)), ("xcst", (480,))], MODS + 7 * D)[0])
        hT, kT, qT, v_, mv, mkT, mqT, og, acc0 = (mx[n] for n in (
            "hT", "kT", "qT", "v", "mv", "mkT", "mqT", "og", "acc"))
        work = gain[:]
        early, _ = lay([("h", (2, D)), ("junk", (D,)), ("mod", (4, D)), ("xc", (TT, D))], KD * TOK)
        modc = early["mod"]
        xc, hst = early["xc"], early["h"]
        late, _ = lay([("mg", (TT, D)), ("mgT", (KD, SEQ))])
        mg, mgT = late["mg"], late["mgT"]
        me, at = lay([("f", (TT, D)), ("fT", (KD, SEQ)), ("y", (TT, D)), ("xTg", (2, KD, P)),
                      ("Pg", (2, TT, P)), ("PT", (2, SEQ)), ("sg", (2, FE)), ("h", (FE,)), ("hT", (FE,))])
        assert at <= MODS
        f_, fT, y_, xTg, Pg, PT, sg, he, heT = (me[n] for n in (
            "f", "fT", "y", "xTg", "Pg", "PT", "sg", "h", "hT"))
        Yg = arena[:, TT * D:2 * TT * D].rearrange("p (a n) -> p a n", a=2)
        bias1 = arena[0:1, TT * D:TT * D + 6 * D].rearrange("p (a n) -> p a n", a=N_ADA)
        fo, _ = lay([("Z", (KD, 2 * SEQ)), ("FT", (KD, SEQ))], 2048)
        Z, FT = fo["Z"], fo["FT"]

        so = [0]

        def sm(n):
            a = so[0]
            so[0] += n
            assert so[0] <= 512
            return small[:, a:a + n]

        cc = sm(2 * KD)
        convs = sm(2 * HEADS * 3)
        rw_s = sm(KD * NE)
        rb_s = sm(NE)
        gb_s = sm(NE)
        lam_s = sm(8)
        ssq = sm(8)
        rstd = sm(8)
        att = sm(16)
        oss = sm(8)
        ors = sm(8)
        wgt_s = sm(KD * NE)
        bt = sm(TT * 8)
        G16 = mx["xcst"][:, 0:64].rearrange("p (t c) -> p t c", t=NT)
        lfF = mx["xcst"][:, 64:96].rearrange("p (t c) -> p t c", t=NT)
        lfB = mx["xcst"][:, 96:128].rearrange("p (t c) -> p t c", t=NT)
        nlfF = mx["xcst"][:, 128:160].rearrange("p (t c) -> p t c", t=NT)
        nlfB = mx["xcst"][:, 160:192].rearrange("p (t c) -> p t c", t=NT)
        li8 = mx["xcst"][:, 192:224].rearrange("p (t c) -> p t c", t=NT)
        gtmp = mx["xcst"][:, 224:288].rearrange("p (t c) -> p t c", t=NT)
        gtmp2 = mx["xcst"][:, 288:352].rearrange("p (t c) -> p t c", t=NT)
        subs = mx["xcst"][:, 352:480]
        r8 = work[0:8, W:2 * W]
        E_ = arena[:, TT * D:2 * TT * D].rearrange("p (b n) -> p b n", b=4)
        Wc = work[:, 0:W]
        lamrow = mx["xcst"][:, 0:256]
        WT = acc0

        rt, _ = lay([("aff", (TT, NE)), ("bi", (TT, NE)), ("t16", (TT, NE)), ("u16", (TT, NE)), ("o1", (TT, NE)),
                     ("o2", (TT, NE)), ("pair", (TT, 6 * NG)), ("gs", (TT, NG)), ("ing", (TT, NG)),
                     ("g1", (TT, NG)), ("s1", (TT, 8))], 2048 * 3)
        NKEY = 2 * NG + 1
        key = sm(TT * NKEY).rearrange("p (t c) -> p t c", t=TT)
        comb4 = sm(TT * EG).rearrange("p (t c) -> p t c", t=TT)
        combS = sm(2 * EG)

        ps = [es.enter_context(nc.psum_tensor(f"bank{b}", [P, W], F32)) for b in range(8)]

        consts_in, x_in, c_in, xc_in, smalls_in, gain_in = (sem(n) for n in (
            "consts_in", "x_in", "c_in", "xc_in", "smalls_in", "gain_in"))
        bias_in = [sem(f"bias_in{b}") for b in range(2)]
        full0 = [sem(f"ring_full_a{s}") for s in range(RING)]
        full1 = [sem(f"ring_full_b{s}") for s in range(RING)]
        w_used = sem("w_used")
        dve_c, bias_zero, silu_c, one_minus = (sem(n) for n in (
            "dve_chain", "bias_zero", "silu_c", "one_minus"))
        acc_ready, ada_sum, mod_ready = (sem(n) for n in ("acc_ready", "ada_sum", "mod_ready"))
        gain_late = sem("gain_late")
        acc_back, bias1_in = sem("acc_back"), sem("bias1_in")
        acc_saved = [sem(f"acc_saved{b}") for b in range(2)]
        sq_ready, ms_ready, root_ready, h_ready, ht_ps, ht_ready, gain_used = (sem(n) for n in (
            "sq_ready", "ms_ready", "root_ready", "h_ready", "hT_in_psum", "hT_ready", "gain_used"))
        proj, evac_a, evac_d, conv_done = (sem(n) for n in ("proj_done", "evac_by_act", "evac_by_dve", "conv_done"))
        exp_g, ln_g, gate_x, lf_ready, r_ps, r_ready, b_ready = (sem(n) for n in (
            "gate_exp", "gate_ln", "gate_x", "lf_ready", "r_in_psum", "r_ready", "b_ready"))
        lam_e, lam_x = sem("lam_exp"), sem("lam_sum")
        s_ps, nmax, prob, s_free, wc_ready, wt_ps, wt_ready, o_ps, o_used, expm = (sem(n) for n in (
            "scores_in_psum", "neg_max", "probs", "scores_used", "weights_ready", "wT_in_psum", "wT_ready", "o_in_psum", "o_used",
            "exp_m"))
        mg_ready, mgt_ps, mgt_ready, mix_ps, mix_used = (sem(n) for n in (
            "merged_ready", "mT_in_psum", "mT_ready", "mix_in_psum", "mix_used"))
        ft_ps, ft_ready, lg_ps, sig_ready, route_m, rank_ps, count_ready, z_ps, z_ready, fT2_ps, fT2_ready = (
            sem(n) for n in ("fT_in_psum", "fT_ready", "logits_in_psum", "affinity_ready", "member_ready", "rank_in_psum",
                             "count_ready", "z_in_psum", "z_ready", "FT_in_psum", "FT_ready"))
        L = []
        for l in range(2):
            L.append({n: sem(f"{n}{l}") for n in ("p_ready", "gathered", "x_ready", "g_done", "u_done", "d_done", "silu_done",
                                                  "he_ready", "t_done", "heT_ready", "y_copied",
                                                  "scattered", "added")})
        stored = sem("stored")

        block = es.enter_context(nc.Block())

        n_pe, n_ada, used_at = 0, 0, []
        for kind, c in STREAM:
            if kind == "ada":
                n_ada += 1
                if c < 4:
                    n_pe += 1
                used_at.append((n_pe if c < 4 else 0, n_ada))
            else:
                n_pe += 1
                used_at.append((n_pe, 0))
        BASE0 = len(STREAM) % RING
        BASE1 = (BASE0 + 2) % RING
        slot_of = {c: n % RING for n, c in enumerate(STREAM)}
        fill_of = {c: n // RING + 1 for n, c in enumerate(STREAM)}
        EBASE = [BASE0, BASE1]
        FILLS = [[(len(STREAM) + RING - 1 - s) // RING for s in range(RING)],
                 [1 if (s - BASE0) % RING < 2 else 0 for s in range(RING)]]
        full = [full0, full1]

        def turn_slot(l, n):
            return (EBASE[l] + n) % RING

        def turn_fill(l, g, n):
            return g * (16 * (len(TURN) // RING)) + 16 * (FILLS[l][turn_slot(l, n)] + n // RING + 1)

        ada_v = adaw.rearrange("l (p k) n -> l p k n", k=KD)
        w_in_v = w_in.rearrange("(p k) n -> p k n", k=KD)
        w_out_v = w_out.rearrange("(p k) n -> p k n", k=KD)
        fnet_v = fnet.rearrange("(k p) n -> p k n", p=P)

        def slot(s):
            return ring[:, s, :].rearrange("p (k n) -> p k n", k=KD)

        H_FIN = 6 * TT
        src_of = [xc, xl]
        MIX = {2: 4, 3: 8, 4: 12, 5: 16}
        MIXED = [6, 14]
        MOD1_ORDER = [2, 3, 0, 1] + list(range(4, N_ADA))

        @block.sync
        def _(sp):
            sp.dma_start(cc, cvec).then_inc(c_in, 16)
            sp.dma_start(K_[:], consts).then_inc(consts_in, 16)
            sp.wait_ge(bias_zero, 1)
            for n, (kind, c) in enumerate(STREAM):
                s = n % RING
                if n >= RING:
                    pe_n, ada_n = used_at[n - RING]
                    if pe_n:
                        sp.wait_ge(w_used, pe_n)
                    if ada_n:
                        sp.wait_ge(acc_ready, ada_n)
                if kind == "ada":
                    src = ada_v[c // N_ADA, :, :, (c % N_ADA) * W:(c % N_ADA + 1) * W]
                elif kind == "in":
                    src = w_in_v[:, :, c:c + W]
                else:
                    src = w_out_v[:, :, c * W:(c + 1) * W]
                sp.dma_start(slot(s), src).then_inc(full0[s], 16)
                if kind == "ada" and c < N_ADA:
                    if c >= 2:
                        sp.wait_ge(acc_ready, c - 1)
                        sp.wait_ge(w_used, min(c - 1, 4))
                    sp.dma_start(bias[0:1, c % 2, :], adab[0:1, c * W:(c + 1) * W]).then_inc(bias_in[c % 2], 16)
                if n == 0:
                    sp.dma_start(xl[:], x.rearrange("(t p) d -> p t d", p=P)).then_inc(x_in, 16)
                    sp.dma_start(xc, ctx.rearrange("(t p) d -> p t d", p=P)).then_inc(xc_in, 16)
                    sp.dma_start(gain[:], gmix[0:1, :].to_broadcast([P, D])).then_inc(gain_in, 16)
                    sp.dma_start(wgt_s.rearrange("p (k n) -> p k n", k=KD),
                                 w_in_v[:, :, C_G:C_G + NE]).then_inc(smalls_in, 16)
                    for dst, src in ((convs, convw), (rw_s, rw.rearrange("(p k) n -> p (k n)", k=KD)),
                                     (rb_s, rb.to_broadcast([P, NE])), (gb_s, gateb.to_broadcast([P, NE])),
                                     (subs, subln.to_broadcast([P, HD]))):
                        sp.dma_start(dst, src).then_inc(smalls_in, 16)
                    sp.dma_start(lamrow, lamv.to_broadcast([P, 4 * QK])).then_inc(smalls_in, 16)

            def used(l, g, kind, i):
                sem_ = L[l]["g_done" if kind == "gate" else "u_done" if kind == "up" else "d_done"]
                sp.wait_ge(sem_, g * (2 * EG) + 2 * (i + 1))

            def load(l, g, n):
                kind, i = TURN[n]
                s = turn_slot(l, n)
                wt, rows = (wd, KF) if kind == "down" else (wg if kind == "gate" else wu, KD)
                src = wt[l, bass.ds(g * EG + i, 1), :, :].rearrange("e (p k) n -> p (e k n)", k=rows)
                sp.dma_start(ring[:, s, :], src).then_inc(full[l][s], 16)

            def load_experts(l, before):
                for n in range(len(TURN)):
                    if n < RING:
                        before[n]()
                    else:
                        used(l, 0, *TURN[n - RING])
                    load(l, 0, n)
                with sp.Fori(1, NG) as g:
                    for n in range(len(TURN)):
                        kind, i = TURN[n - RING]
                        used(l, g, kind, i if n >= RING else i - EG)
                        load(l, g, n)

            def stream_used(n):
                pe_n, ada_n = used_at[len(STREAM) - RING + n]
                if pe_n:
                    sp.wait_ge(w_used, pe_n)
                if ada_n:
                    sp.wait_ge(acc_ready, ada_n)

            load_experts(0, [lambda n=n: stream_used(n) for n in range(RING)])
            for hf in range(2):
                s = (BASE0 + hf) % RING
                used(0, NG - 1, *TURN[len(TURN) - RING + hf])
                sp.dma_start(slot(s), fnet_v[:, :, hf * W:(hf + 1) * W]).then_inc(full1[s], 16)
            before1 = [lambda n=n: used(0, NG - 1, *TURN[len(TURN) - RING + 2 + n]) for n in range(RING - 2)]
            before1 += [lambda n=n: sp.wait_ge(mix_ps, 4 + 2 * (n + 1)) for n in range(2)]
            load_experts(1, before1)
            sp.wait_ge(h_ready, H_FIN)
            sp.dma_start(out.rearrange("(t p) d -> p t d", p=P), f_).then_inc(stored, 16)
            sp.wait_ge(stored, 16)

        @block.gpsimd
        def _(pool):
            for c in range(N_ADA, 2 * N_ADA):
                pool.wait_ge(acc_ready, c + 1)
                pool.dma_start(scratch[c - N_ADA], bias[:, c % 2, :]).then_inc(acc_saved[c % 2], 16)
            for b in range(2):
                pool.wait_ge(acc_saved[b], 16 * (N_ADA // 2))
            pool.wait_ge(h_ready, 3 * TT)
            pool.dma_start(mod1.rearrange("p a (b n) -> p (a b) n", b=2),
                           scratch.rearrange("c p n -> p c n")).then_inc(acc_back, 16)
            for gains, row, n in ((gmix, 1, 2), (gffn, 1, 3), (gfin, 0, 4)):
                pool.wait_ge(gain_used, n)
                pool.dma_start(gain[:], gains[row:row + 1, :].to_broadcast([P, D])).then_inc(gain_late, 16)
                if n == 2:
                    pool.wait_ge(mix_used, MIX[3])
                    pool.dma_start(bias1, adab[1:2, :].rearrange("a (c n) -> a c n", n=W)).then_inc(bias1_in, 16)

        @block.scalar
        def _(act):
            def norm_act(n, x_wait):
                x_wait()
                for t in range(TT):
                    if t:
                        act.wait_ge(sq_ready, TT * n + t)
                    nc.scalar.activation(early["junk"], src_of[n][:, t, :], ACT.Square,
                                         accum_out=ssq[:, t:t + 1]).then_inc(sq_ready, 1)
                act.wait_ge(ms_ready, n + 1)
                nc.scalar.activation(rstd[:, 0:TT], rstd[:, 2:2 + TT], ACT.Sqrt).then_inc(root_ready, 1)


            act.wait_ge(c_in, 16)
            nc.scalar.activation(att[:, 0:2 * KD], cc, ACT.Sigmoid).then_inc(silu_c, 1)

            def mod_copy(c, dst):
                act.wait_ge(ada_sum, c + 1)
                nc.scalar.copy(dst, ps[6][:]).then_inc(mod_ready, 1)

            for c in range(4):
                mod_copy(c, modc[:, c // 2, (c % 2) * W:(c % 2 + 1) * W])
                act.wait_ge(w_used, c + 1)
                nc.scalar.copy(modc[:, 2 + c // 2, (c % 2) * W:(c % 2 + 1) * W], ps[7][:]).then_inc(mod_ready, 1)
            act.wait_ge(smalls_in, 16 * 7)
            norm_act(0, lambda: act.wait_ge(xc_in, 16))
            norm_act(1, lambda: act.wait_ge(x_in, 16))
            for t in range(NT):
                for b in range(2):
                    act.wait_ge(ht_ps, 2 * t + b + 1)
                    nc.scalar.copy(hT[:, 4 * b:4 * b + 4, t * P:(t + 1) * P],
                                   ps[(2 * t + b) % 6][:].rearrange("p (k n) -> p k n", k=4)).then_inc(ht_ready, 1)

            def mod0_copy(c):
                act.wait_ge(ada_sum, c + 1)
                nc.scalar.copy(mod0[:, (c - 4) // 2, (c % 2) * W:(c % 2 + 1) * W], ps[6][:]).then_inc(mod_ready, 1)

            def ada_after(n):
                if ADA_AFTER.get(n - 1, N_ADA) < N_ADA:
                    mod0_copy(ADA_AFTER[n - 1])

            def a_evac(n, dst, src, fn=ACT.Copy, first=True):
                if first:
                    act.wait_ge(proj, n + 1)
                return nc.scalar.activation(dst, src, fn)

            for n, item in enumerate(ITEMS):
                kind, a = item
                bank = ps[n % 6]
                if kind == "k":
                    b, par = a // 2, a % 2
                    for g in range(4):
                        hm = 4 * b + g
                        ins = a_evac(n, kT[(hm % 2) * 64 + par * 32:(hm % 2) * 64 + par * 32 + 32, hm // 2, 0:SEQ],
                                     bank[32 * g:32 * g + 32, 0:SEQ], first=g == 0)
                    ins.then_inc(evac_a, 1)
                elif kind == "v":
                    a_evac(n, v_[:, a, :], bank[:]).then_inc(evac_a, 1)
                elif kind == "mv":
                    a_evac(n, mv[:, a, :], bank[:]).then_inc(evac_a, 1)
                elif kind == "o":
                    a_evac(n, og[:, a, :], bank[:], ACT.Sigmoid).then_inc(evac_a, 1)
                elif kind == "mk":
                    act.wait_ge(conv_done, a + 1)
                    nc.scalar.activation(mkT[:, a, :], work[:, (a % 2) * TOK:(a % 2 + 1) * TOK],
                                         ACT.Silu).then_inc(evac_a, 1)
                elif kind == "mq":
                    act.wait_ge(conv_done, HEADS + a + 1)
                    nc.scalar.activation(mqT[:, 2 * a:2 * a + 2, :],
                                         work[:, (a % 2) * TOK:(a % 2 + 1) * TOK].rearrange("p (a n) -> p a n", a=2),
                                         ACT.Silu).then_inc(evac_a, 1)
                ada_after(n)
            act.wait_ge(lam_x, 1)
            nc.scalar.activation(lam_s[:, 2:4], lam_s[:, 0:2], ACT.Exp).then_inc(lam_e, 1)
            act.wait_ge(gate_x, 1)
            nc.scalar.activation(gtmp, gtmp2, ACT.Exp, scale=-1.0).then_inc(exp_g, 1)
            act.wait_ge(gate_x, 2)
            nc.scalar.activation(gtmp2, gtmp, ACT.Ln).then_inc(ln_g, 1)

            def probs(it):
                base = 3 * (it % 2)
                if it < 8:
                    act.wait_ge(nmax, it + 1)
                    for m in range(2):
                        nc.scalar.activation(E_[:, 2 * (it % 2) + m, :], ps[base + m][:], ACT.Exp,
                                             bias=att[:, 2 * (it % 2) + m:2 * (it % 2) + m + 1], scale=QK ** -0.5,
                                             accum_out=att[:, 4 + 2 * (it % 2) + m:5 + 2 * (it % 2) + m]
                                             ).then_inc(prob, 1)
                else:
                    act.wait_ge(nmax, it + 1)
                    for m in range(2):
                        nc.scalar.activation(E_[:, 2 * (it % 2) + m, :], ps[base + 1 + m][:], ACT.Exp,
                                             bias=att[:, 2 * (it % 2) + m:2 * (it % 2) + m + 1]).then_inc(prob, 1)
                    act.wait_ge(b_ready, it - 8 + 2)
                    nc.scalar.activation(att[:, 12 + 2 * (it % 2):14 + 2 * (it % 2)],
                                         att[:, 8 + 2 * (it % 2):10 + 2 * (it % 2)], ACT.Exp).then_inc(expm, 1)

            def wt_copy(it):
                act.wait_ge(wt_ps, it + 1)
                nc.scalar.copy(WT, ps[6][:]).then_inc(wt_ready, 1)

            def o_copy(it):
                act.wait_ge(o_ps, it + 1)
                if it < 8:
                    h, t = it // 2, it % 2
                    nc.scalar.copy(mg[:, t, h * HD:(h + 1) * HD], ps[7][:, 0:HD])
                    nc.scalar.activation(mx["xcst"][:, 224:352], ps[7][:, 0:HD], ACT.Square,
                                         accum_out=oss[:, it:it + 1]).then_inc(o_used, 1)

            probs(0)
            for it in range(16):
                if it + 1 < 16:
                    probs(it + 1)
                wt_copy(it)
                o_copy(it)
            act.wait_ge(ms_ready, 3)
            nc.scalar.activation(ors, oss, ACT.Sqrt).then_inc(root_ready, 1)
            act.wait_ge(mg_ready, 1)
            act.dma_start(gain[:], gffn[0:1, :].to_broadcast([P, D])).then_inc(gain_in, 16)
            for n in range(4):
                act.wait_ge(mgt_ps, n + 1)
                t, b = n // 2, n % 2
                nc.scalar.copy(mgT[:, 4 * b:4 * b + 4, t * P:(t + 1) * P],
                               ps[n][:].rearrange("p (k n) -> p k n", k=4)).then_inc(mgt_ready, 1)

            def norm2(k):
                act.wait_ge(mix_used, MIX[k])
                for t in range(TT):
                    nc.scalar.activation(arena[:, 4096 + t * D:4096 + (t + 1) * D], xl[:, t, :], ACT.Square,
                                         accum_out=ssq[:, t:t + 1]).then_inc(sq_ready, 1)
                act.wait_ge(ms_ready, k + 2)
                nc.scalar.activation(rstd[:, 0:TT], rstd[:, 2:2 + TT], ACT.Sqrt).then_inc(root_ready, 1)

            def experts(l):
                for t in range(TT):
                    for b in range(2):
                        act.wait_ge(ft_ps, 4 * l + 2 * t + b + 1)
                        nc.scalar.copy(fT[:, 4 * b:4 * b + 4, t * P:(t + 1) * P],
                                       ps[2 * t + b][:].rearrange("p (k n) -> p k n", k=4)).then_inc(ft_ready, 1)
                act.wait_ge(lg_ps, l + 1)
                nc.scalar.activation(rt["aff"], ps[7][:, 0:TT * NE].rearrange("p (t n) -> p t n", t=TT),
                                     ACT.Sigmoid).then_inc(sig_ready, 1)
                S = L[l]
                act.wait_ge(count_ready, l + 1)

                def turn(g, tiles):
                    inc = 2 // tiles
                    steps = [(i, t) for i in range(EG) for t in range(tiles)]

                    def silu(s):
                        act.wait_ge(S["g_done"], g * (2 * EG) + (s + 1) * inc)
                        nc.scalar.activation(sg[:, s % 2, :], ps[0][:], ACT.Silu).then_inc(S["silu_done"], inc)

                    def t_copy(s):
                        act.wait_ge(S["t_done"], g * (2 * EG) + (s + 1) * inc)
                        nc.scalar.copy(heT, ps[2][:]).then_inc(S["heT_ready"], inc)

                    act.wait_ge(S["gathered"], g + 1)
                    for t in range(tiles):
                        ins = nc.scalar.copy(xTg[:, t, 4:8, :], ps[4 + 2 * t][:].rearrange("p (k n) -> p k n", k=4))
                    ins.then_inc(S["x_ready"], 1)
                    for s in range(len(steps)):
                        silu(s)
                        if s:
                            t_copy(s - 1)
                    t_copy(len(steps) - 1)
                    act.wait_ge(S["d_done"], g * (2 * EG) + 2 * EG)
                    for t in range(tiles):
                        ins = nc.scalar.copy(Yg[:, t, 0:W], ps[3 + 2 * t][:])
                    ins.then_inc(S["y_copied"], 1)

                with act.Fori(0, NG) as g:
                    n_tok = act.value_load(cnt_i[0:1, bass.ds(g + l * NG, 1)], min_val=0, max_val=SEQ)
                    with act.If(n_tok > P):
                        turn(g, 2)
                    with act.Else():
                        turn(g, 1)

            norm2(2)
            experts(0)
            for n, c in enumerate(MOD1_ORDER):
                act.wait_ge(ada_sum, N_ADA + n + 1)
                nc.scalar.copy(mod1[:, c // 2, (c % 2) * W:(c % 2 + 1) * W], ps[6 + n % 2][:]).then_inc(mod_ready, 1)
            norm2(3)
            for m in range(KD):
                act.wait_ge(z_ps, m + 1)
                nc.scalar.copy(Z[:, m, 0:SEQ], ps[m % 4][:, 0:SEQ])
                nc.scalar.activation(Z[:, m, SEQ:2 * SEQ], ps[m % 4][:, SEQ:2 * SEQ], ACT.Copy,
                                     scale=-1.0).then_inc(z_ready, 1)
            for m in range(KD):
                act.wait_ge(fT2_ps, m + 1)
                nc.scalar.copy(FT[:, m, :], ps[4 + m % 2][:, 0:SEQ]).then_inc(fT2_ready, 1)
            norm2(4)
            experts(1)
            norm2(5)

        @block.vector
        def _(dve):
            chain = [0]

            def link(ins):
                chain[0] += 1
                ins.then_inc(dve_c, 1)
                dve.wait_ge(dve_c, chain[0])
                return ins

            nc.vector.memset(bias[:], 0.0).then_inc(bias_zero, 1)
            dve.wait_ge(silu_c, 1)
            nc.vector.tensor_tensor(cc, cc, att[:, 0:2 * KD], ALU.mult).then_inc(one_minus, 1)
            dve.wait_ge(one_minus, 1)

            def ada_part(c, w, acc, wait_full):
                wait_full()
                for k in range(KD):
                    if k == 0 and c >= N_ADA:
                        ins = nc.vector.tensor_scalar(acc, w[:, k, :], cc[:, k:k + 1], None, ALU.mult)
                    else:
                        ins = nc.vector.scalar_tensor_tensor(acc, w[:, k, :], cc[:, k:k + 1],
                                                             bias[:, c % 2, :] if k == 0 else acc, ALU.mult, ALU.add)
                    if k < KD - 1:
                        link(ins)
                return ins

            def ada0(c):
                s, f = slot_of[("ada", c)], fill_of[("ada", c)]
                if 0 < c < N_ADA:
                    dve.wait_ge(ada_sum, c)
                if c >= N_ADA:
                    dve.wait_ge(acc_ready, N_ADA)
                    if c >= N_ADA + 2:
                        dve.wait_ge(acc_saved[c % 2], 16 * ((c - N_ADA) // 2))

                def wait_full():
                    dve.wait_ge(full0[s], 16 * f)
                    if c < N_ADA:
                        dve.wait_ge(bias_in[c % 2], 16 * (c // 2 + 1))

                if c < N_ADA:
                    ada_part(c, slot(s), acc0, wait_full).then_inc(acc_ready, 1)
                else:
                    ada_part(c, slot(s), bias[:, c % 2, :], wait_full).then_inc(acc_ready, 1)

            for c in range(4):
                ada0(c)
            dve.wait_ge(mod_ready, 8)
            dve.wait_ge(gain_in, 16)
            for m in (1, 3):
                ins = nc.vector.scalar_tensor_tensor(modc[:, m, :], modc[:, m, :], 1.0, gain[:], ALU.add, ALU.mult)
            ins.then_inc(gain_used, 1)
            dve.wait_ge(gain_used, 1)

            def mean_root(n, i, cnt=D):
                dve.wait_ge(sq_ready, 2 * n + 2)
                nc.vector.tensor_scalar(rstd[:, 2:4], ssq[:, 0:2], 1.0 / D, EPS, ALU.mult, ALU.add
                                        ).then_inc(ms_ready, 1)
                dve.wait_ge(root_ready, i)
                link(nc.vector.reciprocal(rstd[:, 4:6], rstd[:, 0:2]))

            for n in range(2):
                mean_root(n, n + 1)
                for t in range(TT):
                    q = 2 * n + t
                    if q >= 2:
                        dve.wait_ge(ht_ps, 2 * (q - 1))
                    link(nc.vector.scalar_tensor_tensor(hst[:, q % 2, :], (xc, xl)[n][:, t, :], rstd[:, 4 + t:5 + t],
                                                        modc[:, 3 if n == 0 else 1, :], ALU.mult, ALU.mult))
                    nc.vector.tensor_tensor(hst[:, q % 2, :], hst[:, q % 2, :], modc[:, 2 if n == 0 else 0, :],
                                            ALU.add).then_inc(h_ready, 1)

            dve.wait_ge(smalls_in, 16 * 7)
            for m in range(2):
                link(nc.vector.tensor_tensor(lamrow[:, m * 128:m * 128 + QK], lamrow[:, m * 128:m * 128 + QK],
                                             lamrow[:, m * 128 + QK:m * 128 + 2 * QK], ALU.mult))
                ins = nc.vector.reduce_sum(lam_s[:, m:m + 1], lamrow[:, m * 128:m * 128 + QK], axis=AX)
            ins.then_inc(lam_x, 1)
            link(nc.vector.tensor_scalar(subs, subs, 1.0 - LAM_INIT, None, ALU.mult))

            def ada_after(n):
                if n in ADA_AFTER:
                    ada0(ADA_AFTER[n])

            rot = work[:, 0:1024].rearrange("p (a n) -> p a n", a=4)

            ropes = [0]

            def rope(even, odd, dst, b):
                if ropes[0]:
                    dve.wait_ge(evac_d, ropes[0])
                ropes[0] += 1
                nc.vector.tensor_tensor(rot[:, 0, :], even, cosT, ALU.mult)
                nc.vector.tensor_tensor(rot[:, 1, :], odd, sinT, ALU.mult)
                nc.vector.tensor_tensor(rot[:, 2, :], even, sinT, ALU.mult)
                link(nc.vector.tensor_tensor(rot[:, 3, :], odd, cosT, ALU.mult))
                for par, op in ((0, ALU.subtract), (1, ALU.add)):
                    for g in range(4):
                        hm = 4 * b + g
                        o = (hm % 2) * 64 + par * 32
                        ins = nc.vector.tensor_tensor(dst(o, hm // 2), rot[32 * g:32 * g + 32, 2 * par, :],
                                                      rot[32 * g:32 * g + 32, 2 * par + 1, :], op)
                return ins

            def conv(src, dst, taps):
                for s_ in range(2):
                    sl, dl, tp = src[:, s_ * SEQ:(s_ + 1) * SEQ], dst[:, s_ * SEQ:(s_ + 1) * SEQ], taps(s_)
                    link(nc.vector.tensor_scalar(dl, sl, tp[:, 1:2], None, ALU.mult))
                    link(nc.vector.scalar_tensor_tensor(dl[:, 1:SEQ], sl[:, 0:SEQ - 1], tp[:, 0:1], dl[:, 1:SEQ],
                                                        ALU.mult, ALU.add))
                    ins = nc.vector.scalar_tensor_tensor(dl[:, 0:SEQ - 1], sl[:, 1:SEQ], tp[:, 2:3],
                                                         dl[:, 0:SEQ - 1], ALU.mult, ALU.add)
                    if s_ == 0:
                        link(ins)
                ins.then_inc(conv_done, 1)

            tap = convs.rearrange("p (h j) -> p h j", j=3)
            for n, (kind, a) in enumerate(ITEMS):
                bank = ps[n % 6]
                if kind == "k" and a % 2 == 1:
                    dve.wait_ge(proj, n + 1)
                    dve.wait_ge(evac_a, EV_A[n])
                    b = a // 2
                    ins = rope(ps[(n - 1) % 6][:, SEQ:TOK], bank[:, SEQ:TOK],
                               lambda o, t: kT[o:o + 32, t, SEQ:TOK], b)
                    ins.then_inc(evac_d, 1)
                if kind == "q":
                    dve.wait_ge(proj, n + 1)
                    ins = rope(bank[:, 0:SEQ], bank[:, SEQ:TOK], lambda o, t: qT[o:o + 32, t, :], a)
                    ins.then_inc(evac_d, 1)
                if kind == "mk" or kind == "mq":
                    ci = a if kind == "mk" else HEADS + a
                    dve.wait_ge(proj, n + 1)
                    if ci == 0:
                        dve.wait_ge(evac_d, ropes[0])
                    if ci >= 2:
                        dve.wait_ge(evac_a, EV_C[ci - 2])
                    conv(bank, work[:, (a % 2) * TOK:(a % 2 + 1) * TOK],
                         (lambda s_: tap[:, HEADS + a, :]) if kind == "mk" else (lambda s_: tap[:, 2 * a + s_, :]))
                if kind == "g":
                    dve.wait_ge(proj, n + 1)
                    nc.vector.tensor_tensor(G16, bank[:, 0:NT * NE].rearrange("p (t c) -> p t c", t=NT),
                                            gb_s.rearrange("p (a c) -> p a c", a=1).to_broadcast([P, NT, NE]),
                                            ALU.add).then_inc(evac_d, 1)
                ada_after(n)
            dve.wait_ge(evac_d, EV_D[len(ITEMS) - 1])
            for z in (lfF, lfB, nlfF, nlfB):
                nc.vector.memset(z, 0.0)
            nc.vector.scalar_tensor_tensor(gtmp2, G16, -1.0, G16, ALU.mult, ALU.max).then_inc(gate_x, 1)
            dve.wait_ge(exp_g, 1)
            nc.vector.tensor_scalar(gtmp, gtmp, 1.0, None, ALU.add).then_inc(gate_x, 1)
            dve.wait_ge(ln_g, 1)
            link(nc.vector.scalar_tensor_tensor(gtmp, G16, 0.0, gtmp2, ALU.min, ALU.subtract))
            link(nc.vector.tensor_copy(lfF[:, :, 0:4], gtmp[:, :, 4:8]))
            link(nc.vector.tensor_copy(lfB[:, :, 4:8], gtmp[:, :, 12:16]))
            nc.vector.tensor_scalar(nlfF[:, :, 0:4], gtmp[:, :, 4:8], -1.0, None, ALU.mult)
            nc.vector.tensor_scalar(nlfB[:, :, 4:8], gtmp[:, :, 12:16], -1.0, None, ALU.mult)
            nc.vector.tensor_copy(li8[:, :, 0:4], G16[:, :, 0:4])
            nc.vector.tensor_copy(li8[:, :, 4:8], G16[:, :, 8:12]).then_inc(lf_ready, 1)
            dve.wait_ge(lam_e, 1)
            link(nc.vector.tensor_tensor(lam_s[:, 4:5], lam_s[:, 3:4], lam_s[:, 2:3], ALU.subtract))
            link(nc.vector.tensor_scalar(lam_s[:, 5:6], lam_s[:, 4:5], LAM_INIT, None, ALU.subtract))
            dve.wait_ge(r_ps, 1)
            nc.vector.tensor_copy(r8, ps[6][0:8, :]).then_inc(r_ready, 1)
            nc.vector.tensor_copy(bt, ps[7][:, 0:TT * 8]).then_inc(b_ready, 1)
            dve.wait_ge(b_ready, 1)

            def maxes(it):
                dve.wait_ge(s_ps, it + 1)
                base, o = 3 * (it % 2), 2 * (it % 2)
                if it < 8:
                    for m in range(2):
                        ins = nc.vector.tensor_reduce(att[:, o + m:o + m + 1], ps[base + m][:], AX, ALU.max, negate=True)
                    link(ins)
                    nc.vector.tensor_scalar(att[:, o:o + 2], att[:, o:o + 2], QK ** -0.5, None, ALU.mult
                                            ).then_inc(nmax, 1)
                else:
                    h, t = (it - 8) // 2, it % 2
                    for m in range(2):
                        ins = nc.vector.tensor_reduce(att[:, o + m:o + m + 1], ps[base + 1 + m][:], AX, ALU.max,
                                                      negate=True)
                    ins.then_inc(nmax, 1)
                    dve.wait_ge(nmax, it + 1)
                    nc.vector.tensor_tensor(att[:, 8 + o:10 + o], att[:, o:o + 2],
                                            bt.rearrange("p (t m h) -> p t m h", t=TT, m=2)[:, t, :, h],
                                            ALU.subtract).then_inc(b_ready, 1)

            def products(it):
                o = 2 * (it % 2)
                if it >= 8:
                    dve.wait_ge(prob, 2 * it + 2)
                    for m in range(2):
                        ins = nc.vector.tensor_tensor_reduce(
                            out=E_[:, o + m, :], in0=E_[:, o + m, :], in1=ps[3 * (it % 2)][:], scale=HD ** -0.5,
                            scalar=0.0, op0=ALU.mult, op1=ALU.add, accum_out=att[:, 4 + o + m:5 + o + m])
                    ins.then_inc(s_free, 1)

            def combine(it):
                o = 2 * (it % 2)
                dve.wait_ge(prob, 2 * it + 2)
                if it < 8:
                    link(nc.vector.reciprocal(att[:, 4 + o:6 + o], att[:, 4 + o:6 + o]))
                    link(nc.vector.tensor_tensor(att[:, 5 + o:6 + o], att[:, 5 + o:6 + o], lam_s[:, 5:6], ALU.mult))
                else:
                    dve.wait_ge(s_free, it - 8 + 1)
                    dve.wait_ge(expm, it - 8 + 1)
                    link(nc.vector.scalar_tensor_tensor(att[:, 4 + o:6 + o], att[:, 4 + o:6 + o], -1.0,
                                                        att[:, 4 + o:6 + o], ALU.mult, ALU.max))
                    link(nc.vector.tensor_tensor(att[:, 4 + o:6 + o], att[:, 4 + o:6 + o],
                                                 att[:, 12 + o:14 + o], ALU.max))
                    link(nc.vector.reciprocal(att[:, 4 + o:6 + o], att[:, 4 + o:6 + o]))
                if it >= 1:
                    dve.wait_ge(wt_ps, it)
                link(nc.vector.tensor_scalar(Wc, E_[:, o, :], att[:, 4 + o:5 + o], None, ALU.mult))
                nc.vector.scalar_tensor_tensor(Wc, E_[:, o + 1, :], att[:, 5 + o:6 + o], Wc, ALU.mult, ALU.add
                                               ).then_inc(wc_ready, 1)

            def o_gate(it):
                if it >= 8:
                    h, t = (it - 8) // 2, it % 2
                    dve.wait_ge(o_ps, it + 1)
                    nc.vector.tensor_tensor(mg[:, t, W + h * HD:W + (h + 1) * HD], ps[7][:, 0:HD],
                                            og[:, t, h * HD:(h + 1) * HD], ALU.mult).then_inc(o_used, 1)

            maxes(0)
            for it in range(16):
                products(it)
                if it + 1 < 16:
                    maxes(it + 1)
                combine(it)
                if it >= 1:
                    o_gate(it - 1)
                if it in ADA_STEP:
                    ada0(ADA_STEP[it])
            o_gate(15)
            dve.wait_ge(o_used, 16)
            nc.vector.tensor_scalar(oss, oss, 1.0 / HD, EPS, ALU.mult, ALU.add).then_inc(ms_ready, 1)
            dve.wait_ge(root_ready, 3)
            link(nc.vector.reciprocal(oss, ors))
            for it in range(8):
                h, t = it // 2, it % 2
                m = mg[:, t, h * HD:(h + 1) * HD]
                ins = nc.vector.scalar_tensor_tensor(m, m, oss[:, it:it + 1], subs, ALU.mult, ALU.mult)
            ins.then_inc(mg_ready, 1)

            mixed = [0]

            def residual(n, banks, gate):
                for q, b in enumerate(banks):
                    hf, t = q // 2, q % 2
                    dve.wait_ge(mix_ps, n + q + 1)
                    sl = slice(hf * W, (hf + 1) * W)
                    tmp = sgt[:, q % 2, :]
                    link(nc.vector.tensor_tensor(tmp, ps[b][:], gate[:, sl], ALU.mult))
                    nc.vector.tensor_tensor(xl[:, t, sl], xl[:, t, sl], tmp, ALU.add).then_inc(mix_used, 1)
                dve.wait_ge(mix_used, n + len(banks) + mixed[0])

            sgt = arena[:, 8192:8192 + 1024].rearrange("p (a n) -> p a n", a=2)

            def norm_mod(n, i, scale, shift, wait_gain):
                mean_root(n, i)
                dve.wait_ge(*wait_gain)
                if scale is not None:
                    nc.vector.scalar_tensor_tensor(scale, scale, 1.0, gain[:], ALU.add, ALU.mult
                                                   ).then_inc(gain_used, 1)
                    dve.wait_ge(gain_used, n)
                g = gain[:] if scale is None else scale
                for t in range(TT):
                    ins = nc.vector.scalar_tensor_tensor(f_[:, t, :], xl[:, t, :], rstd[:, 4 + t:5 + t], g,
                                                         ALU.mult, ALU.mult)
                    if shift is not None:
                        link(ins)
                        ins = nc.vector.tensor_tensor(f_[:, t, :], f_[:, t, :], shift, ALU.add)
                    ins.then_inc(h_ready, 1)

            def route(l):
                dve.wait_ge(sig_ready, l + 1)
                aff, bi, t16, u16, o1, o2 = (rt[n] for n in ("aff", "bi", "t16", "u16", "o1", "o2"))
                pair, gs, ing, g1, s1 = (rt[n] for n in ("pair", "gs", "ing", "g1", "s1"))

                def bc(a, n, m):
                    return a.rearrange("p (a c) -> p a c", a=1).to_broadcast([P, n, m])

                link(nc.vector.tensor_tensor(bi, aff, bc(rb_s, TT, NE), ALU.add))
                for t in range(TT):
                    b4 = bi[:, t, :].rearrange("p (g e) -> p g e", g=NG)
                    pr = pair[:, t, :].rearrange("p (g q) -> p g q", g=NG)
                    q = 0
                    for a in range(EG):
                        for b in range(a + 1, EG):
                            ins = nc.vector.tensor_tensor(pr[:, :, q], b4[:, :, a], b4[:, :, b], ALU.add)
                            q += 1
                    link(ins)
                    link(nc.vector.tensor_reduce(gs[:, t, :], pr, AX, ALU.max))
                    link(nc.vector.reduce_max(s1[:, t, 0:1], gs[:, t, :], AX))
                    link(nc.vector.scalar_tensor_tensor(g1[:, t, :], gs[:, t, :], s1[:, t, 0:1], cst("first4"),
                                                        ALU.is_equal, ALU.mult))
                    link(nc.vector.reduce_max(s1[:, t, 1:2], g1[:, t, :], AX))
                    nc.vector.tensor_scalar(ing[:, t, :], cst("first4"), s1[:, t, 1:2], None, ALU.is_equal
                                            ).then_inc(route_m, 1)
                dve.wait_ge(route_m, TT * (l + 1))
                for t in range(TT):
                    inb = ing[:, t, :].rearrange("p (g a) -> p g a", a=1).to_broadcast([P, NG, EG])
                    b4 = bi[:, t, :].rearrange("p (g e) -> p g e", g=NG)
                    t4 = t16[:, t, :].rearrange("p (g e) -> p g e", g=NG)
                    u4 = u16[:, t, :].rearrange("p (g e) -> p g e", g=NG)
                    link(nc.vector.tensor_tensor(t4, b4, inb, ALU.mult))
                    link(nc.vector.tensor_scalar(u4, inb, 1.0, BIG, ALU.subtract, ALU.mult))
                    link(nc.vector.tensor_tensor(t16[:, t, :], t16[:, t, :], u16[:, t, :], ALU.add))
                    for o, c in ((o1, 2), (o2, 4)):
                        link(nc.vector.reduce_max(s1[:, t, c:c + 1], t16[:, t, :], AX))
                        link(nc.vector.scalar_tensor_tensor(u16[:, t, :], t16[:, t, :], s1[:, t, c:c + 1],
                                                            cst("first16"), ALU.is_equal, ALU.mult))
                        link(nc.vector.reduce_max(s1[:, t, c + 1:c + 2], u16[:, t, :], AX))
                        link(nc.vector.tensor_scalar(o[:, t, :], cst("first16"), s1[:, t, c + 1:c + 2], None,
                                                     ALU.is_equal))
                        if c == 2:
                            link(nc.vector.scalar_tensor_tensor(t16[:, t, :], o1[:, t, :], -BIG, t16[:, t, :],
                                                                ALU.mult, ALU.add))
                    link(nc.vector.tensor_tensor(o1[:, t, :], o1[:, t, :], o2[:, t, :], ALU.add))
                    link(nc.vector.tensor_tensor(o1[:, t, :], o1[:, t, :], aff[:, t, :], ALU.mult))
                    link(nc.vector.reduce_sum(s1[:, t, 6:7], o1[:, t, :], axis=AX))
                    link(nc.vector.reciprocal(s1[:, t, 7:8], s1[:, t, 6:7]))
                    link(nc.vector.tensor_scalar(o1[:, t, :], o1[:, t, :], s1[:, t, 7:8], None, ALU.mult))
                    link(nc.vector.reduce_sum(comb4[:, t, :], o1[:, t, :].rearrange("p (g e) -> p e g", g=NG),
                                              axis=AX))
                dve.wait_ge(rank_ps, l + 1)
                link(nc.vector.scalar_tensor_tensor(g1, ps[7][:, 64:64 + TT * NG].rearrange("p (t g) -> p t g", t=TT),
                                                    1.0, ing, ALU.add, ALU.mult))
                nc.vector.memset(key[:, :, 2 * NG:NKEY], -1.0)
                nc.vector.tensor_scalar(key[:, :, 0:NG], g1, 1.0, None, ALU.subtract)
                link(nc.vector.tensor_scalar(key[:, :, NG:2 * NG], g1, 1.0 + P, None, ALU.subtract))
                nc.vector.memset(y_, 0.0)
                nc.vector.tensor_copy(cnt_i[:, l * NG:(l + 1) * NG], ps[7][:, 64 + TT * NG:64 + (TT + 1) * NG]
                                      ).then_inc(count_ready, 1)

            def experts(l):
                S = L[l]
                dve.wait_ge(count_ready, l + 1)

                def select(g):
                    for tile in range(2):
                        for t in range(TT):
                            ins = nc.vector.tensor_scalar(Pg[:, tile, t, :], iota,
                                                          key[:, t, bass.ds(g + tile * NG, 1)], None, ALU.is_equal)
                    ins.then_inc(S["p_ready"], 1)

                def turn(g, tiles):
                    inc = 2 // tiles
                    steps = [(i, t) for i in range(EG) for t in range(tiles)]

                    def hidden(s):
                        i, t = steps[s]
                        dve.wait_ge(S["silu_done"], g * (2 * EG) + (s + 1) * inc)
                        dve.wait_ge(S["u_done"], g * (2 * EG) + (s + 1) * inc)
                        nc.vector.scalar_tensor_tensor(he, sg[:, s % 2, :], combS[:, t * EG + i:t * EG + i + 1],
                                                       ps[1][:], ALU.mult, ALU.mult).then_inc(S["he_ready"], inc)

                    dve.wait_ge(S["gathered"], g + 1)
                    nc.vector.tensor_copy(combS[:, 0:tiles * EG], ps[2][:, 0:tiles * EG])
                    nc.vector.tensor_copy(PT[:, 0:tiles, :],
                                          ps[7][:, 0:tiles * SEQ].rearrange("p (t n) -> p t n", t=tiles))
                    for t in range(tiles):
                        ins = nc.vector.tensor_copy(xTg[:, t, 0:4, :],
                                                    ps[3 + 2 * t][:].rearrange("p (k n) -> p k n", k=4))
                    ins.then_inc(S["x_ready"], 1)
                    dve.wait_ge(S["x_ready"], g * 2 + 2)
                    for s in range(len(steps)):
                        hidden(s)
                        if s == 0:
                            select(g + 1)
                    dve.wait_ge(S["d_done"], g * (2 * EG) + 2 * EG)
                    for t in range(tiles):
                        ins = nc.vector.tensor_copy(Yg[:, t, W:D], ps[4 + 2 * t][:])
                    ins.then_inc(S["y_copied"], 1)
                    for t in range(TT):
                        for hf in range(2):
                            sl = slice(hf * W, (hf + 1) * W)
                            dve.wait_ge(S["scattered"], g * 4 + (2 * t + hf + 1))
                            ins = nc.vector.tensor_tensor(y_[:, t, sl], y_[:, t, sl], ps[SC[2 * t + hf]][:],
                                                          ALU.add).then_inc(S["added"], 1)

                nc.vector.memset(lam_s[:, 7:8], 0.0).then_inc(S["added"], 4)
                select(0)
                with dve.Fori(0, NG) as g:
                    n_tok = dve.value_load(cnt_i[0:1, bass.ds(g + l * NG, 1)], min_val=0, max_val=SEQ)
                    with dve.If(n_tok > P):
                        turn(g, 2)
                    with dve.Else():
                        turn(g, 1)

            def close(l, gate):
                dve.wait_ge(L[l]["added"], 4 * (NG + 1))
                for t in range(TT):
                    nc.vector.tensor_tensor(y_[:, t, :], y_[:, t, :], gate, ALU.mult).then_inc(mix_used, 1)
                dve.wait_ge(mix_used, MIXED[l])
                for t in range(TT):
                    nc.vector.tensor_tensor(xl[:, t, :], xl[:, t, :], y_[:, t, :], ALU.add).then_inc(mix_used, 1)
                dve.wait_ge(mix_used, MIXED[l] + TT)

            residual(0, [0, 1, 2, 3], mod0[:, 0, :])
            dve.wait_ge(mod_ready, 16)
            norm_mod(2, 4, mod0[:, 2, :], mod0[:, 1, :], (gain_in, 32))
            route(0)
            experts(0)
            close(0, mod0[:, 3, :])
            dve.wait_ge(mod_ready, 16 + 4)
            norm_mod(3, 5, mod1[:, 1, :], mod1[:, 0, :], (gain_late, 16))
            mixed[0] = 4
            dve.wait_ge(mod_ready, 16 + N_ADA)
            residual(4, [0, 1, 2, 3], mod1[:, 2, :])
            norm_mod(4, 6, mod1[:, 4, :], mod1[:, 3, :], (gain_late, 32))
            route(1)
            experts(1)
            close(1, mod1[:, 5, :])
            norm_mod(5, 7, None, None, (gain_late, 48))

        @block.tensor
        def _(pe):
            mm = nc.tensor.matmul
            pe.wait_ge(consts_in, 16)
            pe.wait_ge(one_minus, 1)
            for c in range(4):
                s, fl = slot_of[("ada", c)], fill_of[("ada", c)]
                pe.wait_ge(full0[s], 16 * fl)
                pe.wait_ge(bias_in[c % 2], 16 * (c // 2 + 1))
                if c:
                    pe.wait_ge(mod_ready, 2 * c)
                for k in range(KD):
                    mm(ps[7][:], cc[:, KD + k:KD + k + 1].to_broadcast([P, P]), slot(s)[:, k, :],
                       start=(k == 0), stop=False)
                mm(ps[7][:], ones, bias[:, c % 2, :], start=False, stop=True).then_inc(w_used, 1)
                pe.wait_ge(acc_ready, c + 1)
                mm(ps[6][:], ones, acc0, start=True, stop=True).then_inc(ada_sum, 1)

            def turn_h(src, wait, banks, done, q0):
                for b in range(2):
                    for k in range(4):
                        ins = nc.tensor.transpose(ps[banks[b]][:, k * P:(k + 1) * P], src[:, 4 * b + k:D:KD], ident)
                    ins.then_inc(done, 1)

            for t in range(NT):
                pe.wait_ge(h_ready, t + 1)
                if t >= 3:
                    pe.wait_ge(ht_ready, 2 * (t - 3) + 2)
                turn_h(hst[:, t % 2, :], None, [(2 * t) % 6, (2 * t + 1) % 6], ht_ps, 0)
            pe.wait_ge(ht_ready, 2 * NT)
            pe.wait_ge(smalls_in, 16 * 7)

            def read(bank):
                mm(ps[bank][0:1, 0:1], ones[:, 0:1], ones[:, 0:1], start=True, stop=True).then_inc(w_used, 1)

            def ada_after(n):
                if ADA_AFTER.get(n - 1, N_ADA) < N_ADA:
                    c = ADA_AFTER[n - 1]
                    pe.wait_ge(acc_ready, c + 1)
                    pe.wait_ge(mod_ready, 8 + c - 4)
                    mm(ps[6][:], ones, acc0, start=True, stop=True).then_inc(ada_sum, 1)

            wgk = wgt_s.rearrange("p (k n) -> p k n", k=KD)
            for n, (kind, a) in enumerate(ITEMS):
                bank = ps[n % 6]
                if n >= 6:
                    if EV_A[n - 6]:
                        pe.wait_ge(evac_a, EV_A[n - 6])
                    if EV_D[n - 6]:
                        pe.wait_ge(evac_d, EV_D[n - 6])
                if kind != "g":
                    col = {"k": C_K, "v": C_V, "q": C_Q, "mk": C_MK, "mq": C_MQ, "mv": C_MV, "o": C_O}[kind]
                    s, fl = slot_of[("in", col)], fill_of[("in", col)]
                    w = slot(s)
                    pe.wait_ge(full0[s], 16 * fl)
                if kind == "k":
                    b, par = a // 2, a % 2
                    for k in range(KD):
                        ins = mm(bank[:], w[:, k, 256 * b + par:256 * (b + 1):2], hT[:, k, :],
                                 start=(k == 0), stop=(k == KD - 1))
                elif kind == "q":
                    for par in range(2):
                        for k in range(KD):
                            ins = mm(bank[:, par * SEQ:(par + 1) * SEQ], w[:, k, 256 * a + par:256 * (a + 1):2],
                                     hT[:, k, SEQ:TOK], start=(k == 0), stop=(k == KD - 1))
                elif kind in ("v", "mv", "o"):
                    t = a if kind != "o" else TT + a
                    for k in range(KD):
                        ins = mm(bank[:], hT[:, k, t * P:(t + 1) * P], w[:, k, :], start=(k == 0),
                                 stop=(k == KD - 1))
                elif kind == "mk":
                    for k in range(KD):
                        ins = mm(bank[:], w[:, k, a * HD:(a + 1) * HD], hT[:, k, :], start=(k == 0),
                                 stop=(k == KD - 1))
                elif kind == "mq":
                    for q in range(2):
                        for k in range(KD):
                            ins = mm(bank[:, q * SEQ:(q + 1) * SEQ], w[:, k, (2 * a + q) * HD:(2 * a + q + 1) * HD],
                                     hT[:, k, SEQ:TOK], start=(k == 0), stop=(k == KD - 1))
                else:
                    for t in range(NT):
                        for k in range(KD):
                            ins = mm(bank[:, t * NE:(t + 1) * NE], hT[:, k, t * P:(t + 1) * P], wgk[:, k, :],
                                     start=(k == 0), stop=(k == KD - 1))
                ins.then_inc(proj, 1)
                if (kind, a) in LAST_OF:
                    read(7)
                ada_after(n)

            pe.wait_ge(lf_ready, 1)
            pe.wait_ge(mod_ready, 16)
            pe.wait_ge(evac_a, N_EV_A)
            le, ge, lt, gt_ = cst("le"), cst("ge"), cst("lt"), cst("gt")

            def rr(t, lhs, rhs, start=False, stop=False):
                return mm(ps[6][0:8, t * P:(t + 1) * P], lhs, rhs, start=start, stop=stop, skip_group_check=True)

            for t in range(NT):
                rr(t, li8[:, t, :], ident, start=(t == 0))
            rr(2, nlfF[:, 2, :], le)
            rr(3, nlfF[:, 2, :], ones)
            rr(3, nlfF[:, 3, :], le)
            rr(1, lfF[:, 1, :], gt_)
            rr(0, lfF[:, 1, :], ones)
            rr(0, lfF[:, 0, :], gt_)
            rr(3, nlfB[:, 3, :], ge)
            rr(2, nlfB[:, 3, :], ones)
            rr(2, nlfB[:, 2, :], ge)
            rr(0, lfB[:, 0, :], lt)
            rr(1, lfB[:, 0, :], ones)
            rr(1, lfB[:, 1, :], lt, stop=True)

            def bb(t, lhs, rhs, start=False, stop=False):
                return mm(ps[7][:, t * 8:(t + 1) * 8], lhs, rhs, start=start, stop=stop, skip_group_check=True)

            bb(0, le, lfF[:, 2, :], start=True)
            bb(1, ones, lfF[:, 2, :])
            bb(1, le, lfF[:, 3, :])
            bb(1, ge, lfB[:, 3, :])
            bb(0, ones, lfB[:, 3, :])
            bb(0, ge, lfB[:, 2, :], stop=True).then_inc(r_ps, 1)

            def scores(it):
                base = 3 * (it % 2)
                if it >= 2:
                    pe.wait_ge(prob, 2 * (it - 1))
                if it >= 10:
                    pe.wait_ge(s_free, it - 9)
                if it < 8:
                    h, t = it // 2, it % 2
                    for m in range(2):
                        hm = 2 * h + m
                        r = slice((hm % 2) * 64, (hm % 2) * 64 + 64)
                        ins = mm(ps[base + m][:], qT[r, hm // 2, t * P:(t + 1) * P], kT[r, hm // 2, :],
                                 start=True, stop=True)
                else:
                    h, t = (it - 8) // 2, it % 2
                    if it == 8:
                        pe.wait_ge(r_ready, 1)
                    mm(ps[base][:], mqT[:, h, t * P:(t + 1) * P], mkT[:, h, :], start=True, stop=True)
                    for m in range(2):
                        row = 4 * m + h
                        bank = ps[base + 1 + m]
                        mm(bank[:], ident[0:8, row:row + 1].to_broadcast([8, P]), r8, start=True, stop=False,
                           skip_group_check=True)
                        if m == 0:
                            cols, msk = (slice(2 * P, 4 * P), mask[:, 0:2 * P]) if t == 0 else (
                                slice(3 * P, 4 * P), mask[:, 0:P])
                        else:
                            cols, msk = (slice(2 * P, 3 * P), mask[:, 2 * P:3 * P]) if t == 0 else (
                                slice(2 * P, 4 * P), mask[:, P:3 * P])
                        ins = mm(bank[:, cols], ident, msk, start=False, stop=True, skip_group_check=True)
                ins.then_inc(s_ps, 1)

            def weights_t(it):
                pe.wait_ge(wc_ready, it + 1)
                for q in range(4):
                    ins = nc.tensor.transpose(ps[6][:, q * P:(q + 1) * P], Wc[:, q * P:(q + 1) * P], ident)
                ins.then_inc(wt_ps, 1)

            def values(it):
                pe.wait_ge(wt_ready, it + 1)
                if it >= 1:
                    pe.wait_ge(o_used, it)
                h = it % 8 // 2
                vv = v_ if it < 8 else mv
                for q in range(4):
                    ins = mm(ps[7][:, 0:HD], WT[:, q * P:(q + 1) * P], vv[:, q, h * HD:(h + 1) * HD],
                             start=(q == 0), stop=(q == 3))
                ins.then_inc(o_ps, 1)

            pe.wait_ge(b_ready, 1)
            pe.wait_ge(evac_d, EV_D[-1])
            scores(0)
            scores(1)
            for it in range(16):
                if it + 2 < 16:
                    scores(it + 2)
                weights_t(it)
                values(it)
            pe.wait_ge(mg_ready, 1)
            for t in range(TT):
                turn_h(mg[:, t, :], None, [2 * t, 2 * t + 1], mgt_ps, 0)
            pe.wait_ge(mgt_ready, 4)
            for q in range(4):
                hf, t = q // 2, q % 2
                s, fl = slot_of[("out", hf)], fill_of[("out", hf)]
                pe.wait_ge(full0[s], 16 * fl)
                for k in range(KD):
                    ins = mm(ps[q][:], mgT[:, k, t * P:(t + 1) * P], slot(s)[:, k, :], start=(k == 0),
                             stop=(k == KD - 1))
                ins.then_inc(mix_ps, 1)
                if t == TT - 1:
                    read(7)

            def experts(l):
                S = L[l]
                for t in range(TT):
                    pe.wait_ge(h_ready, 2 * (2 + 2 * l) + t + 1)
                    turn_h(f_[:, t, :], None, [2 * t, 2 * t + 1], ft_ps, 0)
                pe.wait_ge(ft_ready, 4 * l + 4)
                rwk = rw_s.rearrange("p (k n) -> p k n", k=KD)
                for t in range(TT):
                    for k in range(KD):
                        ins = mm(ps[7][:, t * NE:(t + 1) * NE], fT[:, k, t * P:(t + 1) * P], rwk[:, k, :],
                                 start=(k == 0), stop=(k == KD - 1))
                ins.then_inc(lg_ps, 1)
                pe.wait_ge(route_m, TT * (l + 1))
                ing = rt["ing"]

                def rk(c, lhs, rhs, **kw):
                    return mm(ps[7][:, 64 + c * NG:64 + (c + 1) * NG], lhs, rhs, skip_group_check=True, **kw)

                rk(0, cst("lt"), ing[:, 0, :], start=True, stop=False)
                rk(1, ones, ing[:, 0, :], start=False, stop=False)
                rk(1, cst("lt"), ing[:, 1, :], start=False, stop=False)
                rk(2, ones, ing[:, 0, :], start=False, stop=False)
                rk(2, ones, ing[:, 1, :], start=False, stop=True).then_inc(rank_ps, 1)
                pe.wait_ge(count_ready, l + 1)

                def turn(g, tiles):
                    inc = 2 // tiles
                    steps = [(i, t) for i in range(EG) for t in range(tiles)]

                    def landed(kind, i):
                        n = TURN.index((kind, i))
                        pe.wait_ge(full[l][turn_slot(l, n)], turn_fill(l, g, n))
                        return ring[:, turn_slot(l, n), :].rearrange("p (k n) -> p k n", k=KF if kind == "down" else KD)

                    def gate_up(s, kind):
                        i, t = steps[s]
                        w = landed(kind, i)
                        if kind == "gate" and s:
                            pe.wait_ge(S["silu_done"], g * (2 * EG) + s * inc)
                        for k in range(KD):
                            ins = mm(ps[kind != "gate"][:], xTg[:, t, k, :], w[:, k, :], start=(k == 0),
                                     stop=(k == KD - 1))
                        ins.then_inc(S["g_done" if kind == "gate" else "u_done"], inc)

                    def turn_he(s):
                        pe.wait_ge(S["he_ready"], g * (2 * EG) + (s + 1) * inc)
                        for q in range(KF):
                            ins = nc.tensor.transpose(ps[2][:, q * P:(q + 1) * P], he[:, q:FE:KF], ident)
                        ins.then_inc(S["t_done"], inc)

                    def down(s):
                        i, t = steps[s]
                        w = landed("down", i)
                        pe.wait_ge(S["heT_ready"], g * (2 * EG) + (s + 1) * inc)
                        for q in range(KF):
                            for hf in range(2):
                                ins = mm(ps[3 + 2 * t + hf][:], heT[:, q * P:(q + 1) * P],
                                         w[:, q, hf * W:(hf + 1) * W], start=(i == 0 and q == 0),
                                         stop=(i == EG - 1 and q == KF - 1), skip_group_check=True)
                        ins.then_inc(S["d_done"], inc)

                    pe.wait_ge(S["p_ready"], g + 1)
                    pe.wait_ge(S["added"], g * 4 + 4)
                    for tile in range(tiles):
                        for k in range(KD):
                            for t in range(TT):
                                mm(ps[3 + 2 * tile + k // 4][:, (k % 4) * P:(k % 4 + 1) * P], f_[:, t, k:D:KD],
                                   Pg[:, tile, t, :], start=(t == 0), stop=(t == TT - 1))
                        for t in range(TT):
                            mm(ps[2][:, tile * EG:(tile + 1) * EG], Pg[:, tile, t, :], comb4[:, t, :],
                               start=(t == 0), stop=(t == TT - 1))
                        for t in range(TT):
                            ins = nc.tensor.transpose(ps[7][:, tile * SEQ + t * P:tile * SEQ + (t + 1) * P],
                                                      Pg[:, tile, t, :], ident)
                    ins.then_inc(S["gathered"], 1)
                    pe.wait_ge(S["x_ready"], g * 2 + 2)
                    for s in range(len(steps)):
                        gate_up(s, "gate")
                        if s:
                            turn_he(s - 1)
                        gate_up(s, "up")
                        if s:
                            down(s - 1)
                    turn_he(len(steps) - 1)
                    down(len(steps) - 1)
                    pe.wait_ge(S["y_copied"], g * 2 + 2)
                    for t in range(TT):
                        for hf in range(2):
                            for tile in range(tiles):
                                ins = mm(ps[SC[2 * t + hf]][:], PT[:, tile, t * P:(t + 1) * P],
                                         Yg[:, tile, hf * W:(hf + 1) * W], start=(tile == 0), stop=(tile == tiles - 1))
                            ins.then_inc(S["scattered"], 1)

                with pe.Fori(0, NG) as g:
                    n_tok = pe.value_load(cnt_i[0:1, bass.ds(g + l * NG, 1)], min_val=0, max_val=SEQ)
                    with pe.If(n_tok > P):
                        turn(g, 2)
                    with pe.Else():
                        turn(g, 1)

            experts(0)
            pe.wait_ge(acc_back, 16)
            pe.wait_ge(bias1_in, 16)
            for n, c in enumerate(MOD1_ORDER):
                if n >= 2:
                    pe.wait_ge(mod_ready, 16 + n - 1)
                mm(ps[6 + n % 2][:], ones, mod1[:, c // 2, (c % 2) * W:(c % 2 + 1) * W], start=True, stop=False)
                mm(ps[6 + n % 2][:], ones[0:1, :], bias1[:, c, :], start=False, stop=True).then_inc(ada_sum, 1)
            for m in range(KD):
                pe.wait_ge(h_ready, 8)
                if m >= 4:
                    pe.wait_ge(z_ready, m - 3)
                for t in range(TT):
                    ins = mm(ps[m % 4][:], f_[:, t, m * P:(m + 1) * P], dft[:, t, 0:2 * SEQ], start=(t == 0), stop=(t == 1))
                ins.then_inc(z_ps, 1)
            for m in range(KD):
                g, half = m // 2, m % 2
                pe.wait_ge(z_ready, KD)
                if m >= 2:
                    pe.wait_ge(fT2_ready, m - 1)
                for u in range(2):
                    mm(ps[4 + m % 2][:, 0:SEQ], dft[:, u, half * P:(half + 1) * P], Z[:, 2 * g + u, 0:SEQ],
                       start=(u == 0), stop=False)
                for u in range(2):
                    ins = mm(ps[4 + m % 2][:, 0:SEQ], dft[:, u, SEQ + half * P:SEQ + (half + 1) * P], Z[:, 2 * g + u, SEQ:2 * SEQ],
                             start=False, stop=(u == 1))
                ins.then_inc(fT2_ps, 1)
            pe.wait_ge(fT2_ready, KD)
            for q in range(4):
                hf, t = q // 2, q % 2
                s = (BASE0 + hf) % RING
                pe.wait_ge(full1[s], 16)
                for k in range(KD):
                    ins = mm(ps[q][:], FT[:, k, t * P:(t + 1) * P], slot(s)[:, k, :], start=(k == 0),
                             stop=(k == KD - 1))
                ins.then_inc(mix_ps, 1)
            experts(1)


def kernel(**inputs):
    import numpy as np
    import concourse.bacc as bacc
    from concourse.bass_utils import run_bass_kernel_spmd as run

    a = {n: np.ascontiguousarray(v) for n, v in inputs.items()}
    arrays = {
        "x": a["x"].reshape(SEQ, D),
        "ctx": a["ctx"].reshape(SEQ, D),
        "cvec": np.concatenate([a["c"].reshape(P, KD), a["c_ctx"].reshape(P, KD)], 1),
        "ada_w": a["ada_w"],
        "ada_b": a["ada_b"],
        "norm_mix_g": a["norm_mix_g"],
        "norm_ffn_g": a["norm_ffn_g"],
        "w_in": a["even_w_in"][0],
        "w_out": a["even_w_out"][0],
        "conv_w": a["even_conv_w"][0].reshape(3, 2 * HEADS, HD).transpose(2, 1, 0).reshape(P, -1),
        "gate_b": a["even_gate_b"].reshape(1, -1),
        "lam": a["even_lam"].reshape(1, -1),
        "subln_g": a["even_subln_g"].reshape(1, -1),
        "w_fnet": a["odd_w_fnet"][0],
        "router_w": a["router_w"],
        "router_b": a["router_b"].reshape(1, -1),
        "w_gate": a["exp_w_gate"],
        "w_up": a["exp_w_up"],
        "w_down": a["exp_w_down"],
        "final_g": a["final_g"].reshape(1, -1),
        "constants": constants(),
    }
    arrays = {n: np.ascontiguousarray(v) for n, v in arrays.items()}
    nc = bacc.Bacc("TRN2", target_bir_lowering=False, num_devices=1)
    args = [nc.dram_tensor(f"in_{n}", v.shape, mybir.dt.from_np(v.dtype), kind="ExternalInput").ap()
            for n, v in arrays.items()]
    args.append(nc.dram_tensor("ada_sums", (N_ADA, P, W), F32, kind="Internal").ap())
    args.append(nc.dram_tensor("out", (SEQ, D), F32, kind="ExternalOutput").ap())
    program(nc, *args)
    r = run(nc, [{f"in_{n}": v for n, v in arrays.items()}], core_ids=[0])
    return r.results[0]["out"].reshape(1, SEQ, D)
```

```python
from contextlib import ExitStack
import math

import concourse.bass as bass
from concourse import mybir

F32 = mybir.dt.float32
F32R = mybir.dt.float32r
I32 = mybir.dt.int32
ALU = mybir.AluOpType
ACT = mybir.ActivationFunctionType
AX = mybir.AxisListType.X

P = 128
D = 1024
KD = D // P
SEQ = 256
TT = SEQ // P
TOK = 2 * SEQ
NT = TOK // P
HEADS = 4
QK = 64
HD = 128
W = 512
FE = 512
KF = FE // P
NE = 16
NG = 4
EG = NE // NG
RING = 6
EPS = 1e-6
LAM_INIT = 0.8 - 0.6 * math.exp(0.0)
BIG = 1e30
NC = SEQ // 2 + 1

C_Q, C_K, C_V, C_MQ, C_MK, C_MV, C_O, C_G = 0, 512, 1024, 1536, 2048, 2560, 3072, 3584

CONSTS = {}
_at = 0
for _name, _n in (("ident", P), ("dft", TT * 2 * SEQ), ("cos", SEQ), ("sin", SEQ), ("le", P), ("ge", P),
                  ("lt", P), ("gt", P), ("mask", 3 * P), ("iota", P), ("ones", P), ("first4", NG),
                  ("first16", NE)):
    CONSTS[_name] = (_at, _at + _n)
    _at += _n
N_CONSTS = _at


def constants():
    import numpy as np

    t = np.zeros((P, N_CONSTS), np.float32)

    def put(name, a):
        t[:, CONSTS[name][0]:CONSTS[name][1]] = a

    r, c = np.arange(P)[:, None], np.arange(P)[None, :]
    put("ident", r == c)
    n = np.arange(SEQ)
    ang = 2 * np.pi * ((n[:, None] * n[None, :]) % SEQ) / SEQ
    cs = np.concatenate([np.cos(ang), np.sin(ang)], 1) / math.sqrt(SEQ)
    put("dft", cs.reshape(TT, P, 2 * SEQ).transpose(1, 0, 2).reshape(P, -1))
    pairs = QK // 4
    inv = 10000.0 ** (-np.arange(pairs, dtype=np.float32) / pairs)
    pair, tok = np.arange(P)[:, None] % (2 * pairs), np.arange(SEQ)[None, :]
    pos = np.where(pair < pairs, tok // 64, tok % 64).astype(np.float32)
    rot = pos * inv[pair % pairs].astype(np.float32)
    put("cos", np.cos(rot))
    put("sin", np.sin(rot))
    put("le", r <= c)
    put("ge", r >= c)
    put("lt", r < c)
    put("gt", r > c)
    put("mask", np.concatenate([np.where(c > r, -BIG, 0), np.full((P, P), -BIG), np.where(c < r, -BIG, 0)], 1))
    put("iota", np.broadcast_to(c, (P, P)))
    put("ones", 1.0)
    put("first4", np.broadcast_to(NG - np.arange(NG), (P, NG)))
    put("first16", np.broadcast_to(NE - np.arange(NE), (P, NE)))
    return t


N_ADA = 6 * D // W
STREAM = ([("ada", c) for c in range(4)] + [("ada", 4), ("ada", 5), ("in", C_K), ("ada", 6), ("ada", 7),
          ("in", C_V), ("ada", 8), ("ada", 9), ("ada", 10), ("in", C_Q), ("ada", 11), ("ada", 12), ("in", C_MK),
          ("ada", 13), ("ada", 14), ("in", C_MQ), ("ada", 15), ("ada", 16), ("in", C_MV), ("ada", 17), ("ada", 18),
          ("ada", 19), ("in", C_O)]
          + [("ada", c) for c in range(20, 2 * N_ADA)] + [("out", 0), ("out", 1)])
ADA_AFTER = {n: 4 + i for i, n in enumerate((0, 2, 4, 5, 6, 7, 8, 9, 11, 12, 14, 16, 17, 18, 19, 20))}
ADA_LATE = range(4 + len(ADA_AFTER), 2 * N_ADA)

TURN = [("gate", 0), ("up", 0)]
for _i in range(1, EG):
    TURN += [("gate", _i), ("up", _i), ("down", _i - 1)]
TURN += [("down", EG - 1)]
HALVES = [(_k, _i, _h) for _k, _i in TURN for _h in range(2)]
RAWS, SPLITS, LEAD = 6, 4, 3
HW_ = KD * W // 2
assert len(HALVES) % RAWS == 0 and len(HALVES) % SPLITS == 0


ITEMS = ([("k", a) for a in range(4)] + [("v", a) for a in range(4)] + [("q", a) for a in range(2)]
         + [("mk", a) for a in range(4)] + [("mq", a) for a in range(2)] + [("g", 0)]
         + [("mv", a) for a in range(4)] + [("o", a) for a in range(2)])
LAST_OF = [("k", 3), ("v", 3), ("q", 1), ("mk", 3), ("mq", 1), ("mv", 3), ("o", 1)]
EV_A, EV_D, EV_C = [], [], []
_a = _d = 0
for _kind, _i in ITEMS:
    if _kind in ("k", "v", "mv", "o", "mk", "mq"):
        _a += 1
        EV_A.append(_a)
    else:
        EV_A.append(0)
    if _kind in ("mk", "mq"):
        EV_C.append(_a)
    if _kind in ("q", "g") or (_kind == "k" and _i % 2):
        _d += 1
    EV_D.append(_d + 1 if _kind == "k" and _i % 2 == 0 else _d if _kind in ("k", "q", "g") else 0)
N_EV_A, N_EV_D = _a, _d


def program(nc, x, ctx, cvec, adaw, adab, gmix, gffn, w_in, w_out, convw, gateb, lamv, subln, fnet, rw, rb,
            wg, wu, wd, gfin, consts, scratch, out):
    es = ExitStack()
    with es:
        def sb(name, shape, dt=F32):
            return es.enter_context(nc.sbuf_tensor(name, shape, dt))

        def sem(name):
            return es.enter_context(nc.semaphore(name))

        K_ = sb("consts_sb", [P, N_CONSTS])
        xl = sb("xl", [P, TT, D])
        bias = sb("bias", [P, 2, W])
        gain_at = nc.sbuf_base
        gain = sb("gain", [P, D])
        small = sb("small", [P, 512])
        cnt_i = sb("cnt_i", [P, 2 * NG], I32)
        ROOM = 20480
        base = nc.sbuf_base
        region = sb("region", [P, RING * KD * W + ROOM])

        def placed(name, shape, dt, at):
            return nc.alloc_sbuf_tensor_at(name, shape, dt, offset=base + 4 * at)

        base = (base + 31) // 32 * 32
        ring = placed("ring", [P, RING, KD * W], F32, 0)
        arena = placed("arena", [P, ROOM], F32, RING * KD * W)
        raw = placed("raw", [P, RAWS, HW_], F32, 0)
        w_hi = placed("w_hi", [P, SPLITS, HW_], F32R, 3 * KD * W)
        w_lo = placed("w_lo", [P, SPLITS, HW_], F32R, 5 * KD * W)

        def cst(name, *more):
            return K_[:, CONSTS[name][0]:CONSTS[name][1]]

        ident, ones, iota = cst("ident"), cst("ones"), cst("iota")
        dft = cst("dft").rearrange("p (t n) -> p t n", t=TT)
        cosT, sinT = cst("cos"), cst("sin")
        mask = cst("mask")

        def lay(spec, base=0):
            views, at = {}, base
            for name, dims in spec:
                n = math.prod(dims)
                v = arena[:, at:at + n]
                if len(dims) == 2:
                    v = v.rearrange("p (a b) -> p a b", a=dims[0])
                if len(dims) == 3:
                    v = v.rearrange("p (a b c) -> p a b c", a=dims[0], b=dims[1])
                views[name] = v
                at += n
            assert at <= ROOM, at
            return views, at

        MODS = 11776
        mods = arena[:, MODS:MODS + 7 * D].rearrange("p (a n) -> p a n", a=7)
        AT1 = [2, 3, 0, 1, 5, 6]
        mod1, mod0 = [mods[:, a, :] for a in AT1], mods[:, 3:7, :]
        SC = [5, 6, 3, 4]
        mx, at = lay([("hT", (KD, TOK)), ("kT", (4, TOK)), ("qT", (4, SEQ)), ("v", (NT, W)), ("mv", (NT, W)),
                      ("mkT", (HEADS, TOK)), ("mqT", (HEADS, SEQ)), ("acc", (W,))])
        assert at <= MODS + 3 * D
        mx.update(lay([("og", (TT, W)), ("xcst", (480,))], MODS + 7 * D)[0])
        hT, kT, qT, v_, mv, mkT, mqT, og, acc0 = (mx[n] for n in (
            "hT", "kT", "qT", "v", "mv", "mkT", "mqT", "og", "acc"))
        work = gain[:]
        exact = sb("exact", [P, 4 * P + 8], F32R)
        ident_r, mask_r = exact[:, 0:P], exact[:, P:4 * P]
        pick = exact[:, 4 * P:4 * P + 8]
        r_parts = nc.alloc_sbuf_tensor_at("decay_rows", [P, W], F32R, offset=gain_at + 4 * W)
        r_hi, r_lo = r_parts[0:8, :], r_parts[32:40, :]
        early, _ = lay([("h", (2, D)), ("junk", (D,)), ("mod", (4, D)), ("xc", (TT, D))], KD * TOK)
        modc = early["mod"]
        xc, hst = early["xc"], early["h"]
        late, _ = lay([("mg", (TT, D)), ("mgT", (KD, SEQ))])
        mg, mgT = late["mg"], late["mgT"]
        me, at = lay([("f", (TT, D)), ("Yg", (2, D)), ("xhi", (2, KD, P)), ("xlo", (2, KD, P)),
                      ("Pg", (2, TT, P)), ("PT", (2, SEQ)), ("sg", (2, FE)), ("h", (2, FE)), ("hhi", (2, FE)),
                      ("hlo", (2, FE))], KD * W)
        assert at <= MODS + 6 * D
        f_, Yg, Pg, PT, sg, he = (me[n] for n in ("f", "Yg", "Pg", "PT", "sg", "h"))
        A0 = RING * KD * W
        x_hi = placed("x_hi", [P, 2, KD, P], F32R, A0 + KD * W + 4 * D)
        x_lo = placed("x_lo", [P, 2, KD, P], F32R, A0 + KD * W + 6 * D)
        h_hi = placed("h_hi", [P, 2, FE], F32R, A0 + at - 4 * FE)
        h_lo = placed("h_lo", [P, 2, FE], F32R, A0 + at - 2 * FE)
        fT = lay([("fT", (KD, SEQ))], KD * W + 4 * D)[0]["fT"]
        fo, _ = lay([("Z", (KD, SEQ)), ("C", (2, NC))], KD * W + 2 * D)
        Z, C = fo["Z"], fo["C"]
        JUNK = KD * W + 4 * D
        FT = lay([("FT", (KD, SEQ))], 2048)[0]["FT"]

        so = [0]

        def sm(n):
            a = so[0]
            so[0] += n
            assert so[0] <= 512
            return small[:, a:a + n]

        cc = sm(2 * KD)
        convs = sm(2 * HEADS * 3)
        rw_s = sm(KD * NE)
        rb_s = sm(NE)
        gb_s = sm(NE)
        lam_s = sm(8)
        ssq = sm(8)
        rstd = sm(8)
        att = sm(16)
        oss = sm(8)
        ors = sm(8)
        wgt_s = sm(KD * NE)
        bt = sm(TT * 8)
        G16 = mx["xcst"][:, 0:64].rearrange("p (t c) -> p t c", t=NT)
        lfF = mx["xcst"][:, 64:96].rearrange("p (t c) -> p t c", t=NT)
        lfB = mx["xcst"][:, 96:128].rearrange("p (t c) -> p t c", t=NT)
        nlfF = mx["xcst"][:, 128:160].rearrange("p (t c) -> p t c", t=NT)
        nlfB = mx["xcst"][:, 160:192].rearrange("p (t c) -> p t c", t=NT)
        li8 = mx["xcst"][:, 192:224].rearrange("p (t c) -> p t c", t=NT)
        gtmp = mx["xcst"][:, 224:288].rearrange("p (t c) -> p t c", t=NT)
        gtmp2 = mx["xcst"][:, 288:352].rearrange("p (t c) -> p t c", t=NT)
        subs = mx["xcst"][:, 352:480]
        E_ = arena[:, TT * D:2 * TT * D].rearrange("p (b n) -> p b n", b=4)
        lamrow = mx["xcst"][:, 0:256]
        WT = [acc0, work[:, 0:W]]

        rt, _ = lay([("aff", (TT, NE)), ("bi", (TT, NE)), ("t16", (TT, NE)), ("u16", (TT, NE)), ("o1", (TT, NE)),
                     ("o2", (TT, NE)), ("pair", (TT, 6 * NG)), ("gs", (TT, NG)), ("ing", (TT, NG)),
                     ("g1", (TT, NG)), ("s1", (TT, 8))], MODS + 8 * D)
        NKEY = 2 * NG + 1
        key = sm(TT * NKEY).rearrange("p (t c) -> p t c", t=TT)
        comb4 = sm(TT * EG).rearrange("p (t c) -> p t c", t=TT)
        combS = sm(2 * EG)

        ps = [es.enter_context(nc.psum_tensor(f"bank{b}", [P, W], F32)) for b in range(8)]

        consts_in, x_in, c_in, xc_in, smalls_in, gain_in = (sem(n) for n in (
            "consts_in", "x_in", "c_in", "xc_in", "smalls_in", "gain_in"))
        bias_in = [sem(f"bias_in{b}") for b in range(2)]
        full0 = [sem(f"ring_full_a{s}") for s in range(RING)]
        fnet_in = [sem(f"fnet_in{s}") for s in range(2)]
        full = [[sem(f"raw_full{l}{s}") for s in range(RAWS)] for l in range(2)]
        w_used = sem("w_used")
        dve_c, bias_zero, silu_c, silu_ready = (sem(n) for n in (
            "dve_chain", "bias_zero", "silu_c", "silu_ready"))
        acc_ready, ada_sum, mod_ready = (sem(n) for n in ("acc_ready", "ada_sum", "mod_ready"))
        gain_late = sem("gain_late")
        bias1_added = sem("bias1_added")
        acc_back, bias1_in = ([sem(f"{n}{p}") for p in range(3)] for n in ("acc_back", "bias1_in"))
        acc_saved = [sem(f"acc_saved{b}") for b in range(2)]
        sq_ready, ms_ready, root_ready, h_ready, ht_ps, ht_ready, gain_used = (sem(n) for n in (
            "sq_ready", "ms_ready", "root_ready", "h_ready", "hT_in_psum", "hT_ready", "gain_used"))
        proj, evac_a, evac_d, conv_done = (sem(n) for n in ("proj_done", "evac_by_act", "evac_by_dve", "conv_done"))
        exp_g, ln_g, gate_x, lf_ready, r_ps, r_ready, b_ready = (sem(n) for n in (
            "gate_exp", "gate_ln", "gate_x", "lf_ready", "r_in_psum", "r_ready", "b_ready"))
        c_ready = sem("cosine_part_ready")
        comb_ready = sem("combine_weights_ready")
        lam_e, lam_x, exact_ready = sem("lam_exp"), sem("lam_sum"), sem("exact_ready")
        s_ps, nmax, prob, s_free, wc_ready, wt_ps, wt_ready, o_ps, o_used, expm = (sem(n) for n in (
            "scores_in_psum", "neg_max", "probs", "scores_used", "weights_ready", "wT_in_psum", "wT_ready",
            "o_in_psum", "o_used",
            "exp_m"))
        mg_ready, mgt_ps, mgt_ready, mix_ps, mix_used = (sem(n) for n in (
            "merged_ready", "mT_in_psum", "mT_ready", "mix_in_psum", "mix_used"))
        ft_ps, ft_ready, lg_ps, sig_ready, route_m, rank_ps, count_ready, z_ps, z_ready, fT2_ps, fT2_ready = (
            sem(n) for n in ("fT_in_psum", "fT_ready", "logits_in_psum", "affinity_ready", "member_ready", "rank_in_psum",
                             "count_ready", "z_in_psum", "z_ready", "FT_in_psum", "FT_ready"))
        L = []
        for l in range(2):
            L.append({n: sem(f"{n}{l}") for n in ("p_ready", "cols_ahead", "x_hi_ahead", "x_ahead",
                                                  "gathered", "x1_ready", "hi_ready",
                                                  "lo_ready", "half_used", "silu_done", "he_ready", "t_done",
                                                  "h_hi_ready", "h_ready", "y_ready", "scattered", "added")})
        stored = sem("stored")

        block = es.enter_context(nc.Block())

        n_pe, n_ada, used_at = 0, 0, []
        for kind, c in STREAM:
            if kind == "ada":
                n_ada += 1
                if c < 4:
                    n_pe += 1
                used_at.append((n_pe if c < 4 else 0, n_ada))
            else:
                n_pe += 1
                used_at.append((n_pe, 0))
        TURNED = (3 - (len(STREAM) - 2)) % RING
        slot_of = {c: (n + TURNED) % RING for n, c in enumerate(STREAM)}
        fill_of = {c: n // RING + 1 for n, c in enumerate(STREAM)}
        NH = len(HALVES)
        RAW0 = [0, 4]

        def raw_slot(l, n):
            return (RAW0[l] + n) % RAWS

        def raw_fill(g, n):
            return g * (16 * (NH // RAWS)) + 16 * (n // RAWS + 1)

        ada_v = adaw.rearrange("l (p k) n -> l p k n", k=KD)
        w_in_v = w_in.rearrange("(p k) n -> p k n", k=KD)
        w_out_v = w_out.rearrange("(p k) n -> p k n", k=KD)
        fnet_v = fnet.rearrange("(k p) n -> p k n", p=P)

        def slot(s):
            return ring[:, s, :].rearrange("p (k n) -> p k n", k=KD)

        H_FIN = 6 * TT
        MOD1_ORDER = [2, 3, 0, 1] + list(range(4, N_ADA))

        def load_sums(queue, p):
            queue.dma_start(mods[:, AT1[2 * p]:AT1[2 * p] + 2, :].rearrange("p a (b n) -> p (a b) n", b=2),
                            scratch[4 * p:4 * p + 4].rearrange("c p n -> p c n")).then_inc(acc_back[p], 16)
            queue.dma_start(arena[32 * p:32 * p + 1, 0:2 * D],
                            adab[1:2, 2 * p * D:2 * (p + 1) * D]).then_inc(bias1_in[p], 16)

        @block.sync
        def _(sp):
            sp.dma_start(cc, cvec).then_inc(c_in, 16)
            sp.wait_ge(bias_zero, 1)

            def load_bias(c):
                if c >= 2:
                    sp.wait_ge(acc_ready, c - 1)
                    sp.wait_ge(w_used, min(c - 1, 4))
                sp.dma_start(bias[0:1, c % 2, :], adab[0:1, c * W:(c + 1) * W]).then_inc(bias_in[c % 2], 16)

            for n, (kind, c) in enumerate(STREAM):
                s = (n + TURNED) % RING
                if n >= RING:
                    pe_n, ada_n = used_at[n - RING]
                    if pe_n:
                        sp.wait_ge(w_used, pe_n)
                    if ada_n:
                        sp.wait_ge(acc_ready, ada_n)
                if kind == "ada":
                    src = ada_v[c // N_ADA, :, :, (c % N_ADA) * W:(c % N_ADA + 1) * W]
                elif kind == "in":
                    src = w_in_v[:, :, c:c + W]
                else:
                    src = w_out_v[:, :, c * W:(c + 1) * W]
                sp.dma_start(slot(s), src).then_inc(full0[s], 16)
                if kind == "ada" and c < 4:
                    load_bias(c)
                if n and STREAM[n - 1][0] == "ada" and 4 <= STREAM[n - 1][1] < N_ADA:
                    load_bias(STREAM[n - 1][1])
                if n == 0:
                    sp.dma_start(K_[:], consts).then_inc(consts_in, 16)
                if n == 3:
                    sp.dma_start(xl[:], x.rearrange("(t p) d -> p t d", p=P)).then_inc(x_in, 16)
                    sp.dma_start(xc, ctx.rearrange("(t p) d -> p t d", p=P)).then_inc(xc_in, 16)
                    sp.dma_start(gain[:], gmix[0:1, :].to_broadcast([P, D])).then_inc(gain_in, 16)
                    sp.dma_start(wgt_s.rearrange("p (k n) -> p k n", k=KD),
                                 w_in_v[:, :, C_G:C_G + NE]).then_inc(smalls_in, 16)
                    for dst, src in ((convs, convw), (rw_s, rw.rearrange("(p k) n -> p (k n)", k=KD)),
                                     (rb_s, rb.to_broadcast([P, NE])), (gb_s, gateb.to_broadcast([P, NE])),
                                     (subs, subln.to_broadcast([P, HD]))):
                        sp.dma_start(dst, src).then_inc(smalls_in, 16)
                    sp.dma_start(lamrow, lamv.to_broadcast([P, 4 * QK])).then_inc(smalls_in, 16)

            def load(l, g, n):
                kind, i, hf = HALVES[n]
                s = raw_slot(l, n)
                wt, rows = (wd, KF) if kind == "down" else (wg if kind == "gate" else wu, KD)
                src = wt[l, bass.ds(g * EG + i, 1), :, :].rearrange("e (p k) n -> p (e k n)", k=rows)
                sp.dma_start(raw[:, s, :], src[:, hf * HW_:(hf + 1) * HW_]).then_inc(full[l][s], 16)

            def load_experts(l, before):
                for n in range(NH):
                    if n < RAWS:
                        before[n]()
                    else:
                        sp.wait_ge(L[l]["lo_ready"], n - RAWS + 1)
                    load(l, 0, n)
                with sp.Fori(1, NG) as g:
                    for n in range(NH):
                        sp.wait_ge(L[l]["lo_ready"], g * NH + (n - RAWS + 1))
                        load(l, g, n)

            def stream_used(n):
                at = max(m for m in range(len(STREAM)) if (m + TURNED) % RING == n // 2)
                pe_n, ada_n = used_at[at]
                if pe_n:
                    sp.wait_ge(w_used, pe_n)
                if ada_n:
                    sp.wait_ge(acc_ready, ada_n)

            load_experts(0, [lambda n=n: stream_used(n) for n in range(RAWS)])
            for b in range(2):
                sp.wait_ge(acc_saved[b], 16 * (N_ADA // 2))
            sp.wait_ge(L[0]["half_used"], NG * NH)
            load_sums(sp, 0)
            for hf in range(2):
                sp.dma_start(slot(hf), fnet_v[:, :, hf * W:(hf + 1) * W]).then_inc(fnet_in[hf], 16)
            load_experts(1, [lambda n=n: sp.wait_ge(mix_ps, 8) if n >= 2 else None for n in range(RAWS)])
            sp.wait_ge(h_ready, H_FIN)
            sp.dma_start(out.rearrange("(t p) d -> p t d", p=P), f_).then_inc(stored, 16)
            sp.wait_ge(stored, 16)

        @block.gpsimd
        def _(pool):
            for c in range(N_ADA, 2 * N_ADA):
                pool.wait_ge(acc_ready, c + 1)
                pool.dma_start(scratch[c - N_ADA], bias[:, c % 2, :]).then_inc(acc_saved[c % 2], 16)
            def load_gain(gains, row, n):
                pool.wait_ge(gain_used, n)
                pool.dma_start(gain[:], gains[row:row + 1, :].to_broadcast([P, D])).then_inc(gain_late, 16)

            load_gain(gmix, 1, 2)
            for b in range(2):
                pool.wait_ge(acc_saved[b], 16 * (N_ADA // 2))
            pool.wait_ge(L[0]["added"], 4 * (NG + 1))
            for p in range(1, 3):
                load_sums(pool, p)
            load_gain(gffn, 1, 3)
            load_gain(gfin, 0, 4)

        @block.scalar
        def _(act):
            act.wait_ge(c_in, 16)
            nc.scalar.activation(att[:, 0:2 * KD], cc, ACT.Sigmoid).then_inc(silu_c, 1)

            def mod_copy(c):
                act.wait_ge(ada_sum, c + 1)
                nc.scalar.copy(modc[:, c // 2, (c % 2) * W:(c % 2 + 1) * W], ps[2 * c][:]).then_inc(mod_ready, 1)
                act.wait_ge(w_used, c + 1)
                nc.scalar.copy(modc[:, 2 + c // 2, (c % 2) * W:(c % 2 + 1) * W], ps[2 * c + 1][:]
                               ).then_inc(mod_ready, 1)

            for c in range(3):
                mod_copy(c)
            act.wait_ge(xc_in, 16)
            act.wait_ge(x_in, 16)
            for n in range(2):
                for t in range(TT):
                    q = TT * n + t
                    if q:
                        act.wait_ge(sq_ready, q)
                    nc.scalar.activation(early["junk"], (xc, xl)[n][:, t, :], ACT.Square, accum_out=ssq[:, q:q + 1]
                                         ).then_inc(sq_ready, 1)
            act.wait_ge(ms_ready, 2)
            nc.scalar.activation(att[:, 4:8], att[:, 0:4], ACT.Sqrt).then_inc(root_ready, 2)
            mod_copy(3)
            for t in range(NT):
                for b in range(2):
                    act.wait_ge(ht_ps, 2 * t + b + 1)
                    nc.scalar.copy(hT[:, 4 * b:4 * b + 4, t * P:(t + 1) * P],
                                   ps[(2 * t + b) % 6][:].rearrange("p (k n) -> p k n", k=4)).then_inc(ht_ready, 1)

            def mod0_copy(c):
                act.wait_ge(ada_sum, c + 1)
                nc.scalar.copy(mod0[:, (c - 4) // 2, (c % 2) * W:(c % 2 + 1) * W], ps[6][:]).then_inc(mod_ready, 1)

            def ada_after(n):
                if ADA_AFTER.get(n - 1, N_ADA) < N_ADA:
                    mod0_copy(ADA_AFTER[n - 1])

            def a_evac(n, dst, src, fn=ACT.Copy, first=True):
                if first:
                    act.wait_ge(proj, n + 1)
                return nc.scalar.activation(dst, src, fn)

            for n, item in enumerate(ITEMS):
                kind, a = item
                bank = ps[n % 6]
                if kind == "k":
                    b, par = a // 2, a % 2
                    for g in range(4):
                        hm = 4 * b + g
                        ins = a_evac(n, kT[(hm % 2) * 64 + par * 32:(hm % 2) * 64 + par * 32 + 32, hm // 2, 0:SEQ],
                                     bank[32 * g:32 * g + 32, 0:SEQ], first=g == 0)
                    ins.then_inc(evac_a, 1)
                elif kind == "v":
                    a_evac(n, v_[:, a, :], bank[:]).then_inc(evac_a, 1)
                elif kind == "mv":
                    a_evac(n, mv[:, a, :], bank[:]).then_inc(evac_a, 1)
                elif kind == "o":
                    a_evac(n, og[:, a, :], bank[:], ACT.Sigmoid).then_inc(evac_a, 1)
                elif kind == "mk":
                    act.wait_ge(conv_done, a + 1)
                    nc.scalar.activation(mkT[:, a, :], work[:, (a % 2) * TOK:(a % 2 + 1) * TOK],
                                         ACT.Silu).then_inc(evac_a, 1)
                elif kind == "mq":
                    act.wait_ge(conv_done, HEADS + a + 1)
                    nc.scalar.activation(mqT[:, 2 * a:2 * a + 2, :],
                                         work[:, (a % 2) * TOK:(a % 2 + 1) * TOK].rearrange("p (a n) -> p a n", a=2),
                                         ACT.Silu).then_inc(evac_a, 1)
                elif kind == "g":
                    act.wait_ge(lam_x, 1)
                    nc.scalar.activation(lam_s[:, 2:4], lam_s[:, 0:2], ACT.Exp).then_inc(lam_e, 1)
                    act.wait_ge(gate_x, 1)
                    nc.scalar.activation(gtmp, gtmp2, ACT.Exp, scale=-1.0).then_inc(exp_g, 1)
                    act.wait_ge(gate_x, 2)
                    nc.scalar.activation(gtmp2, gtmp, ACT.Ln).then_inc(ln_g, 1)
                ada_after(n)

            def probs(it):
                base = 3 * (it % 2)
                if it >= 2:
                    act.wait_ge(wt_ps, it - 1)
                if it < 8:
                    act.wait_ge(nmax, it + 1)
                    for m in range(2):
                        nc.scalar.activation(E_[:, 2 * (it % 2) + m, :], ps[base + m][:], ACT.Exp,
                                             bias=att[:, 2 * (it % 2) + m:2 * (it % 2) + m + 1], scale=QK ** -0.5,
                                             accum_out=att[:, 4 + 2 * (it % 2) + m:5 + 2 * (it % 2) + m]
                                             ).then_inc(prob, 1)
                else:
                    act.wait_ge(nmax, it + 1)
                    for m in range(2):
                        nc.scalar.activation(E_[:, 2 * (it % 2) + m, :], ps[base + 1 + m][:], ACT.Exp,
                                             bias=att[:, 2 * (it % 2) + m:2 * (it % 2) + m + 1]).then_inc(prob, 1)
                    act.wait_ge(b_ready, it - 8 + 2)
                    nc.scalar.activation(att[:, 12 + 2 * (it % 2):14 + 2 * (it % 2)],
                                         att[:, 8 + 2 * (it % 2):10 + 2 * (it % 2)], ACT.Exp).then_inc(expm, 1)

            def wt_copy(it):
                act.wait_ge(wt_ps, it + 1)
                if it >= 2:
                    act.wait_ge(o_ps, it - 1)
                nc.scalar.copy(WT[it % 2], ps[6][:]).then_inc(wt_ready, 1)

            def o_copy(it):
                if it < 8:
                    act.wait_ge(o_ps, it + 1)
                    h, t = it // 2, it % 2
                    nc.scalar.copy(mg[:, t, h * HD:(h + 1) * HD], ps[7][:, 0:HD])
                    nc.scalar.activation(mx["xcst"][:, 224:352], ps[7][:, 0:HD], ACT.Square,
                                         accum_out=oss[:, it:it + 1]).then_inc(o_used, 1)

            nc.scalar.copy(ident_r, ident)
            nc.scalar.copy(mask_r, mask).then_inc(exact_ready, 1)
            probs(0)
            for it in range(16):
                if it + 1 < 16:
                    probs(it + 1)
                if it >= 2:
                    o_copy(it - 2)
                wt_copy(it)
            act.wait_ge(ms_ready, 3)
            nc.scalar.activation(ors, oss, ACT.Sqrt).then_inc(root_ready, 1)
            act.wait_ge(mg_ready, 1)
            act.dma_start(gain[:], gffn[0:1, :].to_broadcast([P, D])).then_inc(gain_in, 16)
            for n in range(4):
                act.wait_ge(mgt_ps, n + 1)
                t, b = n // 2, n % 2
                nc.scalar.copy(mgT[:, 4 * b:4 * b + 4, t * P:(t + 1) * P],
                               ps[n][:].rearrange("p (k n) -> p k n", k=4)).then_inc(mgt_ready, 1)

            def norm2(k, x_wait):
                for t in range(TT):
                    x_wait(t)
                    nc.scalar.activation(arena[:, JUNK + t * D:JUNK + (t + 1) * D], xl[:, t, :], ACT.Square,
                                         accum_out=ssq[:, t:t + 1]).then_inc(sq_ready, 1)
                act.wait_ge(ms_ready, k + 2)
                nc.scalar.activation(rstd[:, 0:TT], rstd[:, 2:2 + TT], ACT.Sqrt).then_inc(root_ready, 1)

            def high(l, n):
                return nc.scalar.copy(w_hi[:, n % SPLITS, :], raw[:, raw_slot(l, n), :])

            def first_splits(l, halves):
                for n in halves:
                    act.wait_ge(full[l][raw_slot(l, n)], raw_fill(0, n))
                    high(l, n).then_inc(L[l]["hi_ready"], 1)

            def experts(l):
                for t in range(TT):
                    for b in range(2):
                        act.wait_ge(ft_ps, 4 * l + 2 * t + b + 1)
                        nc.scalar.copy(fT[:, 4 * b:4 * b + 4, t * P:(t + 1) * P],
                                       ps[2 * t + b][:].rearrange("p (k n) -> p k n", k=4)).then_inc(ft_ready, 1)
                act.wait_ge(lg_ps, l + 1)
                nc.scalar.activation(rt["aff"], ps[7][:, 0:TT * NE].rearrange("p (t n) -> p t n", t=TT),
                                     ACT.Sigmoid).then_inc(sig_ready, 1)
                S = L[l]

                def split(g, n):
                    act.wait_ge(full[l][raw_slot(l, n)], raw_fill(g, n))
                    act.wait_ge(S["half_used"], g * NH + (n - SPLITS + 1))
                    high(l, n).then_inc(S["hi_ready"], 1)

                def x_high(g):
                    act.wait_ge(S["cols_ahead"], g + 1)
                    for hf in range(2):
                        ins = nc.scalar.copy(x_hi[:, 0, 4 * hf:4 * hf + 4, :],
                                             ps[hf][:].rearrange("p (k n) -> p k n", k=4))
                    ins.then_inc(S["x_hi_ahead"], 1)

                def turn(g, tiles):
                    inc = 2 // tiles

                    def silu(i):
                        act.wait_ge(S["half_used"], g * NH + (HALVES.index(("gate", i, 1)) + 1))
                        if i:
                            act.wait_ge(S["he_ready"], g * EG + i)
                        for t in range(tiles):
                            ins = nc.scalar.activation(sg[:, t, :], ps[(0, 7)[t]][:], ACT.Silu)
                        ins.then_inc(S["silu_done"], 1)

                    def h_copy(i, t):
                        act.wait_ge(S["t_done"], g * (2 * EG) + (2 * i + (t + 1) * inc))
                        nc.scalar.copy(h_hi[:, t, :], ps[2][:]).then_inc(S["h_hi_ready"], inc)

                    for n, (kind, i, hf) in enumerate(HALVES):
                        if n + LEAD < NH:
                            split(g, n + LEAD)
                        else:
                            with act.If(g < NG - 1):
                                split(g + 1, n + LEAD - NH)
                        if (kind, hf) == ("gate", 1):
                            silu(i)
                            if i:
                                h_copy(i - 1, 0)
                        if (kind, hf) == ("up", 0) and i and tiles > 1:
                            h_copy(i - 1, 1)
                        if (kind, i, hf) == ("down", EG - 2, 1):
                            for t in range(tiles):
                                h_copy(EG - 1, t)
                            with act.If(g < NG - 1):
                                x_high(g + 1)

                x_high(0)
                act.wait_ge(count_ready, l + 1)
                with act.Fori(0, NG) as g:
                    n_tok = act.value_load(cnt_i[0:1, bass.ds(g + l * NG, 1)], min_val=0, max_val=SEQ)
                    with act.If(n_tok > P):
                        turn(g, 2)
                    with act.Else():
                        turn(g, 1)

            norm2(2, lambda t: act.wait_ge(mix_used, 3 + t))
            first_splits(0, range(LEAD))
            experts(0)
            norm2(3, lambda t: act.wait_ge(L[0]["added"], 4 * NG + 3 + t))
            def mod1_copy(n):
                c = MOD1_ORDER[n]
                act.wait_ge(ada_sum, N_ADA + n + 1)
                nc.scalar.copy(mod1[c // 2][:, (c % 2) * W:(c % 2 + 1) * W], ps[6 + n % 2][:]).then_inc(mod_ready, 1)

            for n in range(4):
                mod1_copy(n)
            first_splits(1, range(2))
            for m in range(KD):
                act.wait_ge(z_ps, m + 1)
                nc.scalar.copy(Z[:, m, :], ps[m % 4][:, 0:SEQ]).then_inc(z_ready, 1)
            for m in range(KD):
                act.wait_ge(fT2_ps, m + 1)
                if m >= 2:
                    act.wait_ge(fT2_ready, m - 1)
                nc.scalar.copy(FT[:, m, 0:NC:NC - 1], ps[4 + m % 2][:, 0:NC:NC - 1])
                nc.scalar.copy(C[:, m % 2, :], ps[4 + m % 2][:, 0:NC]).then_inc(c_ready, 1)
            for n in range(4, N_ADA):
                mod1_copy(n)
            norm2(4, lambda t: act.wait_ge(mix_used, 7 + t))
            first_splits(1, range(2, LEAD))
            experts(1)
            norm2(5, lambda t: act.wait_ge(L[1]["added"], 4 * NG + 3 + t))

        @block.vector
        def _(dve):
            chain = [0]

            def link(ins):
                chain[0] += 1
                ins.then_inc(dve_c, 1)
                dve.wait_ge(dve_c, chain[0])
                return ins

            nc.vector.memset(bias[:], 0.0).then_inc(bias_zero, 1)
            dve.wait_ge(silu_c, 1)
            nc.vector.tensor_tensor(cc, cc, att[:, 0:2 * KD], ALU.mult).then_inc(silu_ready, 1)
            dve.wait_ge(silu_ready, 1)

            def ada_part(c, w, acc, wait_full):
                wait_full()
                for k in range(KD):
                    if k == 0 and c >= N_ADA:
                        ins = nc.vector.tensor_scalar(acc, w[:, k, :], cc[:, k:k + 1], None, ALU.mult)
                    else:
                        ins = nc.vector.scalar_tensor_tensor(acc, w[:, k, :], cc[:, k:k + 1],
                                                             bias[:, c % 2, :] if k == 0 else acc, ALU.mult, ALU.add)
                    if k < KD - 1:
                        link(ins)
                return ins

            def ada0(c):
                s, f = slot_of[("ada", c)], fill_of[("ada", c)]
                if 0 < c < N_ADA:
                    dve.wait_ge(ada_sum, c)
                if c >= N_ADA:
                    dve.wait_ge(acc_ready, N_ADA)
                    if c >= N_ADA + 2:
                        dve.wait_ge(acc_saved[c % 2], 16 * ((c - N_ADA) // 2))

                def wait_full():
                    dve.wait_ge(full0[s], 16 * f)
                    if c < N_ADA:
                        dve.wait_ge(bias_in[c % 2], 16 * (c // 2 + 1))

                if c < N_ADA:
                    ada_part(c, slot(s), acc0, wait_full).then_inc(acc_ready, 1)
                else:
                    ada_part(c, slot(s), bias[:, c % 2, :], wait_full).then_inc(acc_ready, 1)

            for c in range(4):
                ada0(c)
            dve.wait_ge(sq_ready, 4)
            nc.vector.tensor_scalar(att[:, 0:4], ssq[:, 0:4], 1.0 / D, EPS, ALU.mult, ALU.add).then_inc(ms_ready, 2)
            dve.wait_ge(root_ready, 2)
            link(nc.vector.reciprocal(att[:, 8:12], att[:, 4:8]))
            dve.wait_ge(mod_ready, 8)
            dve.wait_ge(gain_in, 16)
            for m in (3, 1):
                ins = nc.vector.scalar_tensor_tensor(modc[:, m, :], modc[:, m, :], 1.0, gain[:], ALU.add, ALU.mult)
            ins.then_inc(gain_used, 1)
            dve.wait_ge(gain_used, 1)

            def mean_root(n, i, between=None):
                dve.wait_ge(sq_ready, 2 * n + 2)
                nc.vector.tensor_scalar(rstd[:, 2:4], ssq[:, 0:2], 1.0 / D, EPS, ALU.mult, ALU.add
                                        ).then_inc(ms_ready, 1)
                if between:
                    between()
                dve.wait_ge(root_ready, i)
                link(nc.vector.reciprocal(rstd[:, 4:6], rstd[:, 0:2]))

            for n in range(2):
                for t in range(TT):
                    q = 2 * n + t
                    if q >= 2:
                        dve.wait_ge(ht_ps, 2 * (q - 1))
                    link(nc.vector.scalar_tensor_tensor(hst[:, q % 2, :], (xc, xl)[n][:, t, :], att[:, 8 + q:9 + q],
                                                        modc[:, 3 if n == 0 else 1, :], ALU.mult, ALU.mult))
                    nc.vector.tensor_tensor(hst[:, q % 2, :], hst[:, q % 2, :], modc[:, 2 if n == 0 else 0, :],
                                            ALU.add).then_inc(h_ready, 1)

            dve.wait_ge(smalls_in, 16 * 7)
            for m in range(2):
                link(nc.vector.tensor_tensor(lamrow[:, m * 128:m * 128 + QK], lamrow[:, m * 128:m * 128 + QK],
                                             lamrow[:, m * 128 + QK:m * 128 + 2 * QK], ALU.mult))
                ins = nc.vector.reduce_sum(lam_s[:, m:m + 1], lamrow[:, m * 128:m * 128 + QK], axis=AX)
            ins.then_inc(lam_x, 1)
            link(nc.vector.tensor_scalar(subs, subs, 1.0 - LAM_INIT, None, ALU.mult))

            def ada_after(n):
                if n in ADA_AFTER:
                    ada0(ADA_AFTER[n])

            rot = work[:, 0:1024].rearrange("p (a n) -> p a n", a=4)

            ropes = [0]

            def rope(even, odd, dst, b):
                if ropes[0]:
                    dve.wait_ge(evac_d, ropes[0])
                ropes[0] += 1
                nc.vector.tensor_tensor(rot[:, 0, :], even, cosT, ALU.mult)
                nc.vector.tensor_tensor(rot[:, 1, :], odd, sinT, ALU.mult)
                nc.vector.tensor_tensor(rot[:, 2, :], even, sinT, ALU.mult)
                link(nc.vector.tensor_tensor(rot[:, 3, :], odd, cosT, ALU.mult))
                for par, op in ((0, ALU.subtract), (1, ALU.add)):
                    for g in range(4):
                        hm = 4 * b + g
                        o = (hm % 2) * 64 + par * 32
                        ins = nc.vector.tensor_tensor(dst(o, hm // 2), rot[32 * g:32 * g + 32, 2 * par, :],
                                                      rot[32 * g:32 * g + 32, 2 * par + 1, :], op)
                return ins

            def conv(src, dst, taps):
                for s_ in range(2):
                    sl, dl, tp = src[:, s_ * SEQ:(s_ + 1) * SEQ], dst[:, s_ * SEQ:(s_ + 1) * SEQ], taps(s_)
                    link(nc.vector.tensor_scalar(dl, sl, tp[:, 1:2], None, ALU.mult))
                    link(nc.vector.scalar_tensor_tensor(dl[:, 1:SEQ], sl[:, 0:SEQ - 1], tp[:, 0:1], dl[:, 1:SEQ],
                                                        ALU.mult, ALU.add))
                    ins = nc.vector.scalar_tensor_tensor(dl[:, 0:SEQ - 1], sl[:, 1:SEQ], tp[:, 2:3],
                                                         dl[:, 0:SEQ - 1], ALU.mult, ALU.add)
                    if s_ == 0:
                        link(ins)
                ins.then_inc(conv_done, 1)

            tap = convs.rearrange("p (h j) -> p h j", j=3)
            for n, (kind, a) in enumerate(ITEMS):
                bank = ps[n % 6]
                if kind == "k" and a % 2 == 1:
                    dve.wait_ge(proj, n + 1)
                    dve.wait_ge(evac_a, EV_A[n])
                    b = a // 2
                    ins = rope(ps[(n - 1) % 6][:, SEQ:TOK], bank[:, SEQ:TOK],
                               lambda o, t: kT[o:o + 32, t, SEQ:TOK], b)
                    ins.then_inc(evac_d, 1)
                if kind == "q":
                    dve.wait_ge(proj, n + 1)
                    ins = rope(bank[:, 0:SEQ], bank[:, SEQ:TOK], lambda o, t: qT[o:o + 32, t, :], a)
                    ins.then_inc(evac_d, 1)
                if kind == "mk" or kind == "mq":
                    ci = a if kind == "mk" else HEADS + a
                    dve.wait_ge(proj, n + 1)
                    if ci == 0:
                        dve.wait_ge(evac_d, ropes[0])
                    if ci >= 2:
                        dve.wait_ge(evac_a, EV_C[ci - 2])
                    conv(bank, work[:, (a % 2) * TOK:(a % 2 + 1) * TOK],
                         (lambda s_: tap[:, HEADS + a, :]) if kind == "mk" else (lambda s_: tap[:, 2 * a + s_, :]))
                if kind == "g":
                    dve.wait_ge(proj, n + 1)
                    nc.vector.tensor_tensor(G16, bank[:, 0:NT * NE].rearrange("p (t c) -> p t c", t=NT),
                                            gb_s.rearrange("p (a c) -> p a c", a=1).to_broadcast([P, NT, NE]),
                                            ALU.add).then_inc(evac_d, 1)
                    dve.wait_ge(evac_d, EV_D[n])
                    for z in (lfF, lfB, nlfF, nlfB):
                        nc.vector.memset(z, 0.0)
                    nc.vector.scalar_tensor_tensor(gtmp2, G16, -1.0, G16, ALU.mult, ALU.max).then_inc(gate_x, 1)
                    dve.wait_ge(exp_g, 1)
                    nc.vector.tensor_scalar(gtmp, gtmp, 1.0, None, ALU.add).then_inc(gate_x, 1)
                    dve.wait_ge(ln_g, 1)
                    link(nc.vector.scalar_tensor_tensor(gtmp, G16, 0.0, gtmp2, ALU.min, ALU.subtract))
                    link(nc.vector.tensor_copy(lfF[:, :, 0:4], gtmp[:, :, 4:8]))
                    link(nc.vector.tensor_copy(lfB[:, :, 4:8], gtmp[:, :, 12:16]))
                    nc.vector.tensor_scalar(nlfF[:, :, 0:4], gtmp[:, :, 4:8], -1.0, None, ALU.mult)
                    nc.vector.tensor_scalar(nlfB[:, :, 4:8], gtmp[:, :, 12:16], -1.0, None, ALU.mult)
                    nc.vector.tensor_copy(li8[:, :, 0:4], G16[:, :, 0:4])
                    nc.vector.tensor_copy(li8[:, :, 4:8], G16[:, :, 8:12]).then_inc(lf_ready, 1)
                    dve.wait_ge(lam_e, 1)
                    link(nc.vector.tensor_tensor(lam_s[:, 4:5], lam_s[:, 3:4], lam_s[:, 2:3], ALU.subtract))
                    link(nc.vector.tensor_scalar(lam_s[:, 5:6], lam_s[:, 4:5], LAM_INIT, None, ALU.subtract))
                ada_after(n)
            dve.wait_ge(r_ps, 1)
            nc.vector.tensor_tensor(pick, ident[:, 0:8], ident[:, 32:40], ALU.add)
            link(nc.vector.memset(r_parts[0:40, :].bitcast(F32), 0.0))
            link(nc.vector.tensor_copy(r_hi, ps[6][0:8, :]))
            nc.vector.tensor_tensor(r_lo, ps[6][0:8, :], r_hi.bitcast(F32), ALU.subtract).then_inc(r_ready, 1)
            nc.vector.tensor_copy(bt, ps[7][:, 0:TT * 8]).then_inc(b_ready, 1)
            dve.wait_ge(b_ready, 1)

            def maxes(it):
                dve.wait_ge(s_ps, it + 1)
                base, o = 3 * (it % 2), 2 * (it % 2)
                if it < 8:
                    for m in range(2):
                        ins = nc.vector.tensor_reduce(att[:, o + m:o + m + 1], ps[base + m][:], AX, ALU.max,
                                                      negate=True)
                    link(ins)
                    nc.vector.tensor_scalar(att[:, o:o + 2], att[:, o:o + 2], QK ** -0.5, None, ALU.mult
                                            ).then_inc(nmax, 1)
                else:
                    h, t = (it - 8) // 2, it % 2
                    for m in range(2):
                        ins = nc.vector.tensor_reduce(att[:, o + m:o + m + 1], ps[base + 1 + m][:], AX, ALU.max,
                                                      negate=True)
                    ins.then_inc(nmax, 1)
                    dve.wait_ge(nmax, it + 1)
                    nc.vector.tensor_tensor(att[:, 8 + o:10 + o], att[:, o:o + 2],
                                            bt.rearrange("p (t m h) -> p t m h", t=TT, m=2)[:, t, :, h],
                                            ALU.subtract).then_inc(b_ready, 1)

            def products(it):
                o = 2 * (it % 2)
                if it >= 8:
                    dve.wait_ge(prob, 2 * it + 2)
                    for m in range(2):
                        ins = nc.vector.tensor_tensor_reduce(
                            out=E_[:, o + m, :], in0=E_[:, o + m, :], in1=ps[3 * (it % 2)][:], scale=HD ** -0.5,
                            scalar=0.0, op0=ALU.mult, op1=ALU.add, accum_out=att[:, 4 + o + m:5 + o + m])
                    ins.then_inc(s_free, 1)

            def combine(it):
                o = 2 * (it % 2)
                dve.wait_ge(prob, 2 * it + 2)
                if it < 8:
                    link(nc.vector.reciprocal(att[:, 4 + o:6 + o], att[:, 4 + o:6 + o]))
                    link(nc.vector.tensor_tensor(att[:, 5 + o:6 + o], att[:, 5 + o:6 + o], lam_s[:, 5:6], ALU.mult))
                else:
                    dve.wait_ge(s_free, it - 8 + 1)
                    dve.wait_ge(expm, it - 8 + 1)
                    link(nc.vector.scalar_tensor_tensor(att[:, 4 + o:6 + o], att[:, 4 + o:6 + o], -1.0,
                                                        att[:, 4 + o:6 + o], ALU.mult, ALU.max))
                    link(nc.vector.tensor_tensor(att[:, 4 + o:6 + o], att[:, 4 + o:6 + o],
                                                 att[:, 12 + o:14 + o], ALU.max))
                    link(nc.vector.reciprocal(att[:, 4 + o:6 + o], att[:, 4 + o:6 + o]))
                link(nc.vector.tensor_scalar(E_[:, o, :], E_[:, o, :], att[:, 4 + o:5 + o], None, ALU.mult))
                nc.vector.scalar_tensor_tensor(E_[:, o, :], E_[:, o + 1, :], att[:, 5 + o:6 + o], E_[:, o, :],
                                               ALU.mult, ALU.add).then_inc(wc_ready, 1)

            def o_gate(it):
                if it >= 8:
                    h, t = (it - 8) // 2, it % 2
                    dve.wait_ge(o_ps, it + 1)
                    nc.vector.tensor_tensor(mg[:, t, W + h * HD:W + (h + 1) * HD], ps[7][:, 0:HD],
                                            og[:, t, h * HD:(h + 1) * HD], ALU.mult).then_inc(o_used, 1)

            maxes(0)
            for it in range(16):
                products(it)
                if it + 1 < 16:
                    maxes(it + 1)
                if it >= 2:
                    o_gate(it - 2)
                combine(it)
            o_gate(14)
            o_gate(15)
            dve.wait_ge(o_used, 16)
            nc.vector.tensor_scalar(oss, oss, 1.0 / HD, EPS, ALU.mult, ALU.add).then_inc(ms_ready, 1)
            dve.wait_ge(root_ready, 3)
            link(nc.vector.reciprocal(oss, ors))
            for it in range(8):
                h, t = it // 2, it % 2
                m = mg[:, t, h * HD:(h + 1) * HD]
                ins = nc.vector.scalar_tensor_tensor(m, m, oss[:, it:it + 1], subs, ALU.mult, ALU.mult)
            ins.then_inc(mg_ready, 1)
            for c in ADA_LATE:
                ada0(c)

            def residual(n, banks, gate):
                for q, b in enumerate(banks):
                    hf, t = q // 2, q % 2
                    dve.wait_ge(mix_ps, n + q + 1)
                    sl = slice(hf * W, (hf + 1) * W)
                    tmp = sgt[:, q % 2, :]
                    link(nc.vector.tensor_tensor(tmp, ps[b][:], gate[:, sl], ALU.mult))
                    nc.vector.tensor_tensor(xl[:, t, sl], xl[:, t, sl], tmp, ALU.add).then_inc(mix_used, 1)
                dve.wait_ge(mix_used, n + len(banks))

            sgt = arena[:, 6144:6144 + 1024].rearrange("p (a n) -> p a n", a=2)

            def norm_mod(n, i, scale, shift, wait_gain, mods_ready=0):
                def scaled_gain():
                    if mods_ready:
                        dve.wait_ge(mod_ready, mods_ready)
                    dve.wait_ge(*wait_gain)
                    if scale is not None:
                        nc.vector.scalar_tensor_tensor(scale, scale, 1.0, gain[:], ALU.add, ALU.mult
                                                       ).then_inc(gain_used, 1)

                mean_root(n, i, scaled_gain)
                if scale is not None:
                    dve.wait_ge(gain_used, n)
                g = gain[:] if scale is None else scale
                for t in range(TT):
                    ins = nc.vector.scalar_tensor_tensor(f_[:, t, :], xl[:, t, :], rstd[:, 4 + t:5 + t], g,
                                                         ALU.mult, ALU.mult)
                    if mods_ready:
                        dve.wait_ge(mod_ready, mods_ready + 2)
                    if shift is not None:
                        link(ins)
                        ins = nc.vector.tensor_tensor(f_[:, t, :], f_[:, t, :], shift, ALU.add)
                    ins.then_inc(h_ready, 1)

            def low(l, n):
                s = n % SPLITS
                return nc.vector.tensor_tensor(w_lo[:, s, :], raw[:, raw_slot(l, n), :], w_hi[:, s, :].bitcast(F32),
                                               ALU.subtract)

            def first_splits(l, halves):
                for n in halves:
                    dve.wait_ge(L[l]["hi_ready"], n + 1)
                    low(l, n).then_inc(L[l]["lo_ready"], 1)

            def select(l, g):
                for tile in range(2):
                    for t in range(TT):
                        ins = nc.vector.tensor_scalar(Pg[:, tile, t, :], iota,
                                                      key[:, t, bass.ds(g + tile * NG, 1)], None, ALU.is_equal)
                ins.then_inc(L[l]["p_ready"], 1)

            def route(l):
                dve.wait_ge(sig_ready, l + 1)
                aff, bi, t16, u16, o1, o2 = (rt[n] for n in ("aff", "bi", "t16", "u16", "o1", "o2"))
                pair, gs, ing, g1, s1 = (rt[n] for n in ("pair", "gs", "ing", "g1", "s1"))

                def bc(a, n, m):
                    return a.rearrange("p (a c) -> p a c", a=1).to_broadcast([P, n, m])

                def every(col, n):
                    return s1[:, :, col:col + 1].to_broadcast([P, TT, n])

                def first_max(src, tmp, dst, col, table, n):
                    link(nc.vector.tensor_reduce(s1[:, :, col:col + 1], src, AX, ALU.max))
                    link(nc.vector.tensor_tensor(tmp, src, every(col, n), ALU.is_equal))
                    link(nc.vector.tensor_tensor(tmp, tmp, bc(cst(table), TT, n), ALU.mult))
                    link(nc.vector.tensor_reduce(s1[:, :, col + 1:col + 2], tmp, AX, ALU.max))
                    return nc.vector.tensor_tensor(dst, bc(cst(table), TT, n), every(col + 1, n), ALU.is_equal)

                link(nc.vector.tensor_tensor(bi, aff, bc(rb_s, TT, NE), ALU.add))
                b4 = bi.rearrange("p t (g e) -> p (t g) e", g=NG)
                pr = pair.rearrange("p t (g q) -> p (t g) q", g=NG)
                q = 0
                for a in range(EG):
                    for b in range(a + 1, EG):
                        ins = nc.vector.tensor_tensor(pr[:, :, q], b4[:, :, a], b4[:, :, b], ALU.add)
                        q += 1
                link(ins)
                link(nc.vector.tensor_reduce(gs.rearrange("p t g -> p (t g)"), pr, AX, ALU.max))
                first_max(gs, g1, ing, 0, "first4", NG).then_inc(route_m, 1)
                dve.wait_ge(route_m, l + 1)
                inb = ing.rearrange("p t (g a) -> p (t g) a", a=1).to_broadcast([P, TT * NG, EG])
                t4, u4 = (a.rearrange("p t (g e) -> p (t g) e", g=NG) for a in (t16, u16))
                nc.vector.tensor_tensor(t4, b4, inb, ALU.mult)
                link(nc.vector.tensor_scalar(u4, inb, 1.0, BIG, ALU.subtract, ALU.mult))
                link(nc.vector.tensor_tensor(t16, t16, u16, ALU.add))
                link(first_max(t16, u16, o1, 2, "first16", NE))
                link(nc.vector.scalar_tensor_tensor(t16, o1, -BIG, t16, ALU.mult, ALU.add))
                dve.wait_ge(rank_ps, l + 1)
                link(nc.vector.scalar_tensor_tensor(g1, ps[7][:, 64:64 + TT * NG].rearrange("p (t g) -> p t g", t=TT),
                                                    1.0, ing, ALU.add, ALU.mult))
                nc.vector.memset(key[:, :, 2 * NG:NKEY], -1.0)
                nc.vector.tensor_scalar(key[:, :, 0:NG], g1, 1.0, None, ALU.subtract)
                link(nc.vector.tensor_scalar(key[:, :, NG:2 * NG], g1, 1.0 + P, None, ALU.subtract))
                nc.vector.tensor_copy(cnt_i[:, l * NG:(l + 1) * NG], ps[7][:, 64 + TT * NG:64 + (TT + 1) * NG]
                                      ).then_inc(count_ready, 1)
                dve.wait_ge(count_ready, l + 1)
                select(l, 0)
                link(first_max(t16, u16, o2, 4, "first16", NE))
                link(nc.vector.tensor_tensor(o1, o1, o2, ALU.add))
                link(nc.vector.tensor_tensor(o1, o1, aff, ALU.mult))
                link(nc.vector.reduce_sum(s1[:, :, 6:7], o1, axis=AX))
                link(nc.vector.reciprocal(s1[:, :, 7:8], s1[:, :, 6:7]))
                link(nc.vector.tensor_tensor(o1, o1, every(7, NE), ALU.mult))
                for t in range(TT):
                    ins = nc.vector.reduce_sum(comb4[:, t, :], o1[:, t, :].rearrange("p (g e) -> p e g", g=NG),
                                               axis=AX)
                ins.then_inc(comb_ready, 1)

            def experts(l, gate):
                S = L[l]
                dve.wait_ge(count_ready, l + 1)

                def split(g, n):
                    dve.wait_ge(S["hi_ready"], g * NH + (n + 1))
                    low(l, n).then_inc(S["lo_ready"], 1)

                def x_low(g):
                    dve.wait_ge(S["cols_ahead"], g + 1)
                    nc.vector.tensor_copy(combS[:, 0:EG], ps[7][:, 0:EG])
                    dve.wait_ge(S["x_hi_ahead"], g + 1)
                    for hf in range(2):
                        ins = nc.vector.tensor_tensor(x_lo[:, 0, 4 * hf:4 * hf + 4, :],
                                                      ps[hf][:].rearrange("p (k n) -> p k n", k=4),
                                                      x_hi[:, 0, 4 * hf:4 * hf + 4, :].bitcast(F32), ALU.subtract)
                    ins.then_inc(S["x_ahead"], 1)

                def turn(g, tiles):
                    inc = 2 // tiles

                    def hidden(i):
                        dve.wait_ge(S["silu_done"], g * EG + (i + 1))
                        dve.wait_ge(S["half_used"], g * NH + (HALVES.index(("up", i, 1)) + 1))
                        for t in range(tiles):
                            ins = nc.vector.scalar_tensor_tensor(he[:, t, :], sg[:, t, :],
                                                                 combS[:, t * EG + i:t * EG + i + 1],
                                                                 ps[(1, 0)[t]][:], ALU.mult, ALU.mult)
                        ins.then_inc(S["he_ready"], 1)

                    def h_low(i, t):
                        dve.wait_ge(S["h_hi_ready"], g * (2 * EG) + (2 * i + (t + 1) * inc))
                        nc.vector.tensor_tensor(h_lo[:, t, :], ps[2][:], h_hi[:, t, :].bitcast(F32), ALU.subtract
                                                ).then_inc(S["h_ready"], inc)

                    def output():
                        dve.wait_ge(S["half_used"], g * NH + NH)
                        for hf in range(2):
                            sl = slice(hf * W, (hf + 1) * W)
                            for t in range(tiles):
                                ins = nc.vector.tensor_tensor(Yg[:, t, sl], ps[3 + 2 * t + hf][:], gate[:, sl],
                                                              ALU.mult)
                            ins.then_inc(S["y_ready"], 1)

                    dve.wait_ge(S["x_ahead"], g + 1)
                    dve.wait_ge(S["gathered"], g + 1)
                    ins = nc.vector.tensor_copy(PT[:, 0:tiles, :],
                                                ps[2][:, 0:tiles * SEQ].rearrange("p (t n) -> p t n", t=tiles))
                    if tiles == 1:
                        ins.then_inc(S["x1_ready"], 4)
                    else:
                        nc.vector.tensor_copy(combS[:, EG:2 * EG], ps[7][:, EG:2 * EG])
                        for hf in range(2):
                            nc.vector.tensor_copy(x_hi[:, 1, 4 * hf:4 * hf + 4, :],
                                                  ps[5 + hf][:].rearrange("p (k n) -> p k n", k=4)
                                                  ).then_inc(S["x1_ready"], 1)
                        for hf in range(2):
                            dve.wait_ge(S["x1_ready"], g * 4 + (hf + 1))
                            nc.vector.tensor_tensor(x_lo[:, 1, 4 * hf:4 * hf + 4, :],
                                                    ps[5 + hf][:].rearrange("p (k n) -> p k n", k=4),
                                                    x_hi[:, 1, 4 * hf:4 * hf + 4, :].bitcast(F32), ALU.subtract
                                                    ).then_inc(S["x1_ready"], 1)
                        dve.wait_ge(S["x1_ready"], g * 4 + 4)
                    for n, (kind, i, hf) in enumerate(HALVES):
                        if n == NH - 1:
                            output()
                        if n + LEAD < NH:
                            split(g, n + LEAD)
                        else:
                            with dve.If(g < NG - 1):
                                split(g + 1, n + LEAD - NH)
                        if n == 0:
                            select(l, g + 1)
                        if (kind, hf) == ("gate", 1) and i:
                            h_low(i - 1, 0)
                        if (kind, hf) == ("up", 0) and i and tiles > 1:
                            h_low(i - 1, 1)
                        if (kind, hf) == ("up", 1):
                            hidden(i)
                        if (kind, i, hf) == ("down", EG - 2, 1):
                            for t in range(tiles):
                                h_low(EG - 1, t)
                            with dve.If(g < NG - 1):
                                x_low(g + 1)
                    for hf in range(2):
                        for t in range(TT):
                            q = 2 * hf + t
                            sl = slice(hf * W, (hf + 1) * W)
                            dve.wait_ge(S["scattered"], g * 4 + (q + 1))
                            dve.wait_ge(S["added"], g * 4 + (q + 1))
                            nc.vector.tensor_tensor(xl[:, t, sl], xl[:, t, sl], ps[SC[q]][:], ALU.add
                                                    ).then_inc(S["added"], 1)

                nc.vector.memset(lam_s[:, 7:8], 0.0).then_inc(S["added"], 4)
                dve.wait_ge(S["added"], 4)
                x_low(0)
                with dve.Fori(0, NG) as g:
                    n_tok = dve.value_load(cnt_i[0:1, bass.ds(g + l * NG, 1)], min_val=0, max_val=SEQ)
                    with dve.If(n_tok > P):
                        turn(g, 2)
                    with dve.Else():
                        turn(g, 1)

            def add_bias1(p):
                dve.wait_ge(acc_back[p], 16)
                dve.wait_ge(bias1_in[p], 16)
                rows = mods[32 * p:32 * p + 1, AT1[2 * p]:AT1[2 * p] + 2, :].rearrange("p a n -> p (a n)")
                nc.vector.tensor_tensor(rows, rows, arena[32 * p:32 * p + 1, 0:2 * D], ALU.add
                                        ).then_inc(bias1_added, 1)

            residual(0, [0, 1, 2, 3], mod0[:, 0, :])
            dve.wait_ge(mod_ready, 16)
            norm_mod(2, 4, mod0[:, 2, :], mod0[:, 1, :], (gain_in, 32))
            first_splits(0, range(LEAD))
            route(0)
            experts(0, mod0[:, 3, :])
            add_bias1(0)
            norm_mod(3, 5, mod1[1], mod1[0], (gain_late, 16), 16 + 2)
            add_bias1(1)
            add_bias1(2)
            for m in range(KD):
                dve.wait_ge(c_ready, m + 1)
                dve.wait_ge(fT2_ps, m + 1)
                s_part = ps[4 + m % 2][:, NC:SEQ]
                nc.vector.tensor_tensor(FT[:, m, 1:NC - 1], C[:, m % 2, 1:NC - 1], s_part, ALU.subtract)
                nc.vector.tensor_tensor(FT[:, m, SEQ - 1:NC - 1:-1], C[:, m % 2, 1:NC - 1], s_part, ALU.add
                                        ).then_inc(fT2_ready, 1)
            first_splits(1, range(2))
            dve.wait_ge(mod_ready, 16 + N_ADA)
            residual(4, [0, 1, 2, 3], mod1[2])
            norm_mod(4, 6, mod1[4], mod1[3], (gain_late, 32))
            first_splits(1, range(2, LEAD))
            route(1)
            experts(1, mod1[5])
            norm_mod(5, 7, None, None, (gain_late, 48))

        @block.tensor
        def _(pe):
            mm = nc.tensor.matmul
            pe.wait_ge(silu_ready, 1)
            for c in range(4):
                s, fl = slot_of[("ada", c)], fill_of[("ada", c)]
                pe.wait_ge(full0[s], 16 * fl)
                pe.wait_ge(bias_in[c % 2], 16 * (c // 2 + 1))
                for k in range(KD):
                    mm(ps[2 * c + 1][:], cc[:, KD + k:KD + k + 1].to_broadcast([P, P]), slot(s)[:, k, :],
                       start=(k == 0), stop=False)
                if c == 0:
                    pe.wait_ge(consts_in, 16)
                mm(ps[2 * c + 1][:], ones, bias[:, c % 2, :], start=False, stop=True).then_inc(w_used, 1)
                pe.wait_ge(acc_ready, c + 1)
                mm(ps[2 * c][:], ones, acc0, start=True, stop=True).then_inc(ada_sum, 1)

            def turn_h(src, banks, done):
                for b in range(2):
                    for k in range(4):
                        ins = nc.tensor.transpose(ps[banks[b]][:, k * P:(k + 1) * P], src[:, 4 * b + k:D:KD], ident)
                    ins.then_inc(done, 1)

            for t in range(NT):
                pe.wait_ge(h_ready, t + 1)
                if t >= 3:
                    pe.wait_ge(ht_ready, 2 * (t - 3) + 2)
                turn_h(hst[:, t % 2, :], [(2 * t) % 6, (2 * t + 1) % 6], ht_ps)
            pe.wait_ge(ht_ready, 2 * NT)
            pe.wait_ge(smalls_in, 16 * 7)

            def read(bank):
                mm(ps[bank][0:1, 0:1], ones[:, 0:1], ones[:, 0:1], start=True, stop=True).then_inc(w_used, 1)

            def ada_after(n):
                if ADA_AFTER.get(n - 1, N_ADA) < N_ADA:
                    c = ADA_AFTER[n - 1]
                    pe.wait_ge(acc_ready, c + 1)
                    pe.wait_ge(mod_ready, 8 + c - 4)
                    mm(ps[6][:], ones, acc0, start=True, stop=True).then_inc(ada_sum, 1)

            wgk = wgt_s.rearrange("p (k n) -> p k n", k=KD)
            for n, (kind, a) in enumerate(ITEMS):
                bank = ps[n % 6]
                if n >= 6:
                    if EV_A[n - 6]:
                        pe.wait_ge(evac_a, EV_A[n - 6])
                    if EV_D[n - 6]:
                        pe.wait_ge(evac_d, EV_D[n - 6])
                if kind != "g":
                    col = {"k": C_K, "v": C_V, "q": C_Q, "mk": C_MK, "mq": C_MQ, "mv": C_MV, "o": C_O}[kind]
                    s, fl = slot_of[("in", col)], fill_of[("in", col)]
                    w = slot(s)
                    pe.wait_ge(full0[s], 16 * fl)
                if kind == "k":
                    b, par = a // 2, a % 2
                    for k in range(KD):
                        ins = mm(bank[:], w[:, k, 256 * b + par:256 * (b + 1):2], hT[:, k, :],
                                 start=(k == 0), stop=(k == KD - 1))
                elif kind == "q":
                    for par in range(2):
                        for k in range(KD):
                            ins = mm(bank[:, par * SEQ:(par + 1) * SEQ], w[:, k, 256 * a + par:256 * (a + 1):2],
                                     hT[:, k, SEQ:TOK], start=(k == 0), stop=(k == KD - 1))
                elif kind in ("v", "mv", "o"):
                    t = a if kind != "o" else TT + a
                    for k in range(KD):
                        ins = mm(bank[:], hT[:, k, t * P:(t + 1) * P], w[:, k, :], start=(k == 0),
                                 stop=(k == KD - 1))
                elif kind == "mk":
                    for k in range(KD):
                        ins = mm(bank[:], w[:, k, a * HD:(a + 1) * HD], hT[:, k, :], start=(k == 0),
                                 stop=(k == KD - 1))
                elif kind == "mq":
                    for q in range(2):
                        for k in range(KD):
                            ins = mm(bank[:, q * SEQ:(q + 1) * SEQ], w[:, k, (2 * a + q) * HD:(2 * a + q + 1) * HD],
                                     hT[:, k, SEQ:TOK], start=(k == 0), stop=(k == KD - 1))
                else:
                    for t in range(NT):
                        for k in range(KD):
                            ins = mm(bank[:, t * NE:(t + 1) * NE], hT[:, k, t * P:(t + 1) * P], wgk[:, k, :],
                                     start=(k == 0), stop=(k == KD - 1))
                ins.then_inc(proj, 1)
                if (kind, a) in LAST_OF:
                    read(7)
                ada_after(n)

            pe.wait_ge(lf_ready, 1)
            pe.wait_ge(mod_ready, 16)
            pe.wait_ge(evac_a, N_EV_A)
            le, ge, lt, gt_ = cst("le"), cst("ge"), cst("lt"), cst("gt")

            def rr(t, lhs, rhs, start=False, stop=False):
                return mm(ps[6][0:8, t * P:(t + 1) * P], lhs, rhs, start=start, stop=stop, skip_group_check=True)

            for t in range(NT):
                rr(t, li8[:, t, :], ident, start=(t == 0))
            rr(2, nlfF[:, 2, :], le)
            rr(3, nlfF[:, 2, :], ones)
            rr(3, nlfF[:, 3, :], le)
            rr(1, lfF[:, 1, :], gt_)
            rr(0, lfF[:, 1, :], ones)
            rr(0, lfF[:, 0, :], gt_)
            rr(3, nlfB[:, 3, :], ge)
            rr(2, nlfB[:, 3, :], ones)
            rr(2, nlfB[:, 2, :], ge)
            rr(0, lfB[:, 0, :], lt)
            rr(1, lfB[:, 0, :], ones)
            rr(1, lfB[:, 1, :], lt, stop=True)

            def bb(t, lhs, rhs, start=False, stop=False):
                return mm(ps[7][:, t * 8:(t + 1) * 8], lhs, rhs, start=start, stop=stop, skip_group_check=True)

            bb(0, le, lfF[:, 2, :], start=True)
            bb(1, ones, lfF[:, 2, :])
            bb(1, le, lfF[:, 3, :])
            bb(1, ge, lfB[:, 3, :])
            bb(0, ones, lfB[:, 3, :])
            bb(0, ge, lfB[:, 2, :], stop=True).then_inc(r_ps, 1)

            def scores(it):
                base = 3 * (it % 2)
                if it >= 2:
                    pe.wait_ge(prob, 2 * (it - 1))
                if it >= 10:
                    pe.wait_ge(s_free, it - 9)
                if it < 8:
                    h, t = it // 2, it % 2
                    for m in range(2):
                        hm = 2 * h + m
                        r = slice((hm % 2) * 64, (hm % 2) * 64 + 64)
                        ins = mm(ps[base + m][:], qT[r, hm // 2, t * P:(t + 1) * P], kT[r, hm // 2, :],
                                 start=True, stop=True)
                else:
                    h, t = (it - 8) // 2, it % 2
                    if it == 8:
                        pe.wait_ge(r_ready, 1)
                        pe.wait_ge(exact_ready, 1)
                    mm(ps[base][:], mqT[:, h, t * P:(t + 1) * P], mkT[:, h, :], start=True, stop=True)
                    for m in range(2):
                        row = 4 * m + h
                        bank = ps[base + 1 + m]
                        mm(bank[:], pick[0:40, row:row + 1].to_broadcast([40, P]), r_parts[0:40, :], start=True,
                           stop=False, skip_group_check=True)
                        if m == 0:
                            cols, msk = (slice(2 * P, 4 * P), mask_r[:, 0:2 * P]) if t == 0 else (
                                slice(3 * P, 4 * P), mask_r[:, 0:P])
                        else:
                            cols, msk = (slice(2 * P, 3 * P), mask_r[:, 2 * P:3 * P]) if t == 0 else (
                                slice(2 * P, 4 * P), mask_r[:, P:3 * P])
                        ins = mm(bank[:, cols], ident_r, msk, start=False, stop=True, skip_group_check=True)
                ins.then_inc(s_ps, 1)

            def weights_t(it):
                pe.wait_ge(wc_ready, it + 1)
                if it:
                    pe.wait_ge(wt_ready, it)
                for q in range(4):
                    ins = nc.tensor.transpose(ps[6][:, q * P:(q + 1) * P], E_[:, 2 * (it % 2), q * P:(q + 1) * P],
                                              ident)
                ins.then_inc(wt_ps, 1)

            def values(it):
                pe.wait_ge(wt_ready, it + 1)
                if it >= 1:
                    pe.wait_ge(o_used, it)
                h = it % 8 // 2
                vv = v_ if it < 8 else mv
                for q in range(4):
                    ins = mm(ps[7][:, 0:HD], WT[it % 2][:, q * P:(q + 1) * P], vv[:, q, h * HD:(h + 1) * HD],
                             start=(q == 0), stop=(q == 3))
                ins.then_inc(o_ps, 1)

            pe.wait_ge(b_ready, 1)
            pe.wait_ge(evac_d, N_EV_D)
            scores(0)
            scores(1)
            for it in range(16):
                if it + 2 < 16:
                    scores(it + 2)
                weights_t(it)
                if it:
                    values(it - 1)
            values(15)
            pe.wait_ge(mg_ready, 1)
            for t in range(TT):
                turn_h(mg[:, t, :], [2 * t, 2 * t + 1], mgt_ps)
            pe.wait_ge(mgt_ready, 4)
            for q in range(4):
                hf, t = q // 2, q % 2
                s, fl = slot_of[("out", hf)], fill_of[("out", hf)]
                pe.wait_ge(full0[s], 16 * fl)
                for k in range(KD):
                    ins = mm(ps[q][:], mgT[:, k, t * P:(t + 1) * P], slot(s)[:, k, :], start=(k == 0),
                             stop=(k == KD - 1))
                ins.then_inc(mix_ps, 1)
                if t == TT - 1:
                    read(7)

            def experts(l):
                S = L[l]
                for t in range(TT):
                    pe.wait_ge(h_ready, 2 * (2 + 2 * l) + t + 1)
                    turn_h(f_[:, t, :], [2 * t, 2 * t + 1], ft_ps)
                pe.wait_ge(ft_ready, 4 * l + 4)
                rwk = rw_s.rearrange("p (k n) -> p k n", k=KD)
                for t in range(TT):
                    for k in range(KD):
                        ins = mm(ps[7][:, t * NE:(t + 1) * NE], fT[:, k, t * P:(t + 1) * P], rwk[:, k, :],
                                 start=(k == 0), stop=(k == KD - 1))
                ins.then_inc(lg_ps, 1)
                pe.wait_ge(route_m, l + 1)
                ing = rt["ing"]

                def rk(c, lhs, rhs, **kw):
                    return mm(ps[7][:, 64 + c * NG:64 + (c + 1) * NG], lhs, rhs, skip_group_check=True, **kw)

                rk(0, cst("lt"), ing[:, 0, :], start=True, stop=False)
                rk(1, ones, ing[:, 0, :], start=False, stop=False)
                rk(1, cst("lt"), ing[:, 1, :], start=False, stop=False)
                rk(2, ones, ing[:, 0, :], start=False, stop=False)
                rk(2, ones, ing[:, 1, :], start=False, stop=True).then_inc(rank_ps, 1)
                pe.wait_ge(count_ready, l + 1)

                def columns(tile, banks, first=False):
                    for k in range(KD):
                        for t in range(TT):
                            mm(ps[banks[k // 4]][:, (k % 4) * P:(k % 4 + 1) * P], f_[:, t, k:D:KD], Pg[:, tile, t, :],
                               start=(t == 0), stop=(t == TT - 1))
                    if first:
                        pe.wait_ge(comb_ready, l + 1)
                    for t in range(TT):
                        ins = mm(ps[7][:, tile * EG:(tile + 1) * EG], Pg[:, tile, t, :], comb4[:, t, :],
                                 start=(t == 0), stop=(t == TT - 1))
                    return ins

                def turn(g, tiles):
                    inc = 2 // tiles

                    def three(bank, xh, xo, wh, wo, **kw):
                        mm(bank, xh, wo, start=kw["start"], stop=False, skip_group_check=True)
                        mm(bank, xh, wh, start=False, stop=False, skip_group_check=True)
                        return mm(bank, xo, wh, start=False, stop=kw["stop"], skip_group_check=True)

                    def half(n):
                        kind, i, hf = HALVES[n]
                        s = n % SPLITS
                        pe.wait_ge(S["lo_ready"], g * NH + (n + 1))
                        if kind == "down":
                            if (i, hf, tiles) == (0, 0, 1):
                                pe.wait_ge(S["added"], g * 4 + 4)
                            if hf == 0:
                                pe.wait_ge(S["h_ready"], g * (2 * EG) + 2 * (i + 1))
                            wh, wo = (w[:, s, :].rearrange("p (k n) -> p k n", k=KF // 2) for w in (w_hi, w_lo))
                            for t in range(tiles):
                                for q in range(KF // 2):
                                    k = hf * (KF // 2) + q
                                    for c in range(2):
                                        ins = three(ps[3 + 2 * t + c][:], h_hi[:, t, k * P:(k + 1) * P],
                                                    h_lo[:, t, k * P:(k + 1) * P], wh[:, q, c * W:(c + 1) * W],
                                                    wo[:, q, c * W:(c + 1) * W], start=(i == 0 and k == 0),
                                                    stop=(i == EG - 1 and k == KF - 1))
                        else:
                            banks = (0, 7) if kind == "gate" else (1, 0)
                            wh, wo = (w[:, s, :].rearrange("p (k n) -> p k n", k=KD // 2) for w in (w_hi, w_lo))
                            if (kind, hf) == ("gate", 0) and i:
                                pe.wait_ge(S["he_ready" if tiles > 1 else "silu_done"], g * EG + i)
                            for t in range(tiles):
                                if (kind, i, hf, t) == ("gate", 0, 0, 1):
                                    pe.wait_ge(S["x1_ready"], g * 4 + 4)
                                if (kind, hf, t) == ("up", 0, 1):
                                    pe.wait_ge(S["silu_done"], g * EG + (i + 1))
                                for q in range(KD // 2):
                                    k = hf * (KD // 2) + q
                                    ins = three(ps[banks[t]][:], x_hi[:, t, k, :], x_lo[:, t, k, :], wh[:, q, :],
                                                wo[:, q, :], start=(k == 0), stop=(k == KD - 1))
                        ins.then_inc(S["half_used"], 1)

                    def turn_he(i, t):
                        if i == 0 and tiles == 1:
                            pe.wait_ge(S["x1_ready"], g * 4 + 4)
                        if t == 0:
                            pe.wait_ge(S["he_ready"], g * EG + (i + 1))
                        else:
                            pe.wait_ge(S["h_ready"], g * (2 * EG) + (2 * i + 1))
                        for q in range(KF):
                            ins = nc.tensor.transpose(ps[2][:, q * P:(q + 1) * P], he[:, t, q:FE:KF], ident)
                        ins.then_inc(S["t_done"], inc)

                    for tile in range(tiles):
                        for t in range(TT):
                            ins = nc.tensor.transpose(ps[2][:, tile * SEQ + t * P:tile * SEQ + (t + 1) * P],
                                                      Pg[:, tile, t, :], ident)
                    pe.wait_ge(S["x_ahead"], g + 1)
                    if tiles > 1:
                        pe.wait_ge(S["added"], g * 4 + 4)
                        ins = columns(1, [5, 6])
                    ins.then_inc(S["gathered"], 1)
                    for n, (kind, i, hf) in enumerate(HALVES):
                        half(n)
                        if (kind, hf) == ("gate", 1) and i:
                            turn_he(i - 1, 0)
                        if (kind, hf) == ("up", 0) and i and tiles > 1:
                            turn_he(i - 1, 1)
                        if (kind, i, hf) == ("down", EG - 2, 1):
                            for t in range(tiles):
                                turn_he(EG - 1, t)
                            with pe.If(g < NG - 1):
                                pe.wait_ge(S["p_ready"], g + 2)
                                columns(0, [0, 1]).then_inc(S["cols_ahead"], 1)
                    for hf in range(2):
                        pe.wait_ge(S["y_ready"], g * 2 + (hf + 1 if tiles == 1 else 2))
                        for t in range(TT):
                            for tile in range(tiles):
                                ins = mm(ps[SC[2 * hf + t]][:], PT[:, tile, t * P:(t + 1) * P],
                                         Yg[:, tile, hf * W:(hf + 1) * W], start=(tile == 0), stop=(tile == tiles - 1))
                            ins.then_inc(S["scattered"], 1)

                pe.wait_ge(S["p_ready"], 1)
                columns(0, [0, 1], True).then_inc(S["cols_ahead"], 1)
                with pe.Fori(0, NG) as g:
                    n_tok = pe.value_load(cnt_i[0:1, bass.ds(g + l * NG, 1)], min_val=0, max_val=SEQ)
                    with pe.If(n_tok > P):
                        turn(g, 2)
                    with pe.Else():
                        turn(g, 1)

            experts(0)
            def sum_mod1(n):
                c = MOD1_ORDER[n]
                pe.wait_ge(bias1_added, c // 4 + 1)
                pe.wait_ge(acc_back[c // 4], 16)
                if n >= 2:
                    pe.wait_ge(mod_ready, 16 + n - 1)
                mm(ps[6 + n % 2][:], ones, mod1[c // 2][:, (c % 2) * W:(c % 2 + 1) * W], start=True, stop=True
                   ).then_inc(ada_sum, 1)

            for n in range(4):
                sum_mod1(n)
            for m in range(KD):
                pe.wait_ge(h_ready, 8)
                if m >= 4:
                    pe.wait_ge(z_ready, m - 3)
                for cols, tab in ((slice(0, NC), slice(0, NC)), (slice(NC, SEQ), slice(SEQ + 1, SEQ + NC - 1))):
                    for t in range(TT):
                        ins = mm(ps[m % 4][:, cols], f_[:, t, m * P:(m + 1) * P], dft[:, t, tab], start=(t == 0),
                                 stop=(t == 1))
                ins.then_inc(z_ps, 1)
            for m in range(KD):
                g, half = m // 2, m % 2
                pe.wait_ge(z_ready, 2 * g + 2)
                if m >= 2:
                    pe.wait_ge(fT2_ready, m - 1)
                for cols, tab in ((slice(0, NC), half * P), (slice(NC, SEQ), SEQ + half * P)):
                    for u in range(2):
                        ins = mm(ps[4 + m % 2][:, cols], dft[:, u, tab:tab + P], Z[:, 2 * g + u, cols],
                                 start=(u == 0), stop=(u == 1))
                ins.then_inc(fT2_ps, 1)
            for n in range(4, N_ADA):
                sum_mod1(n)
            for q in range(4):
                hf, t = q // 2, q % 2
                pe.wait_ge(fnet_in[hf], 16)
                for k in range(KD):
                    if q == 0:
                        pe.wait_ge(fT2_ready, k + 1)
                    ins = mm(ps[q][:], FT[:, k, t * P:(t + 1) * P], slot(hf)[:, k, :], start=(k == 0),
                             stop=(k == KD - 1))
                ins.then_inc(mix_ps, 1)
            experts(1)


def kernel(**inputs):
    import numpy as np
    import concourse.bacc as bacc
    from concourse.bass_utils import run_bass_kernel_spmd as run

    a = {n: np.ascontiguousarray(v) for n, v in inputs.items()}
    arrays = {
        "x": a["x"].reshape(SEQ, D),
        "ctx": a["ctx"].reshape(SEQ, D),
        "cvec": np.concatenate([a["c"].reshape(P, KD), a["c_ctx"].reshape(P, KD)], 1),
        "ada_w": a["ada_w"],
        "ada_b": a["ada_b"],
        "norm_mix_g": a["norm_mix_g"],
        "norm_ffn_g": a["norm_ffn_g"],
        "w_in": a["even_w_in"][0],
        "w_out": a["even_w_out"][0],
        "conv_w": a["even_conv_w"][0].reshape(3, 2 * HEADS, HD).transpose(2, 1, 0).reshape(P, -1),
        "gate_b": a["even_gate_b"].reshape(1, -1),
        "lam": a["even_lam"].reshape(1, -1),
        "subln_g": a["even_subln_g"].reshape(1, -1),
        "w_fnet": a["odd_w_fnet"][0],
        "router_w": a["router_w"],
        "router_b": a["router_b"].reshape(1, -1),
        "w_gate": a["exp_w_gate"],
        "w_up": a["exp_w_up"],
        "w_down": a["exp_w_down"],
        "final_g": a["final_g"].reshape(1, -1),
        "constants": constants(),
    }
    arrays = {n: np.ascontiguousarray(v) for n, v in arrays.items()}
    nc = bacc.Bacc("TRN2", target_bir_lowering=False, num_devices=1)
    args = [nc.dram_tensor(f"in_{n}", v.shape, mybir.dt.from_np(v.dtype), kind="ExternalInput").ap()
            for n, v in arrays.items()]
    args.append(nc.dram_tensor("ada_sums", (N_ADA, P, W), F32, kind="Internal").ap())
    args.append(nc.dram_tensor("out", (SEQ, D), F32, kind="ExternalOutput").ap())
    program(nc, *args)
    r = run(nc, [{f"in_{n}": v for n, v in arrays.items()}], core_ids=[0])
    return r.results[0]["out"].reshape(1, SEQ, D)
```
